# Optimizing a Trainium2 kernel written in Bass

```python
import math
import jax
import jax.numpy as jnp
from jax import lax
import numpy as np

D_MODEL = 1024
BATCH = 1
SEQ = 1024
DEPTH = 1

CONV_WIDTH = 4
NORM_EPS = 1e-6
RWKV_HEADS = 4
D_A = D_MODEL // 4
RWKV_HEAD_DIM = D_A // RWKV_HEADS
RWKV_DECAY_LORA = 32
RWKV_AAA_LORA = 32
RWKV_GATE_LORA = 64
RWKV_GN_EPS = 64e-5
A_COLS = 3 * D_A + RWKV_DECAY_LORA + RWKV_AAA_LORA + RWKV_GATE_LORA
GDN_HEADS = 4
D_B = D_MODEL // 2
GDN_HEAD_DIM = D_B // GDN_HEADS
GDN_CHUNK = 64
B_COLS = 4 * D_B + 2 * GDN_HEADS
D_C = D_MODEL - D_A - D_B
LRU_BLOCKS = 4
LRU_BLOCK_DIM = D_C // LRU_BLOCKS
LRU_C = 8.0
C_COLS = 2 * D_C
D_MIX = D_A + D_B + D_C
N_IN = A_COLS + B_COLS + C_COLS
MOE_GROUPS = 4
MOE_EXPERTS_PER_GROUP = 8
MOE_EXPERTS = MOE_GROUPS * MOE_EXPERTS_PER_GROUP
MOE_TOP_K = 2
D_EXPERT = D_MODEL // 4
MOE_BLOCK = 128

kernel_name = 'hybrid_rwkv7_gdn_rglru_hmoe'

def rms_norm(x, gain):
    xf = x.astype(jnp.float32)
    y = xf * lax.rsqrt(jnp.mean(xf * xf, axis=-1, keepdims=True) + NORM_EPS)
    return (y * gain.astype(jnp.float32)).astype(x.dtype)

def l2_normalize(x):
    return x * lax.rsqrt(jnp.sum(x * x, axis=-1, keepdims=True) + 1e-6)

def causal_depthwise_conv(x, w):
    return lax.conv_general_dilated(
        x, w[:, None, :].astype(x.dtype), window_strides=(1,),
        padding=[(CONV_WIDTH - 1, 0)], dimension_numbers=('NWC', 'WIO', 'NWC'),
        feature_group_count=x.shape[-1])

def rwkv7_scan(r, w, k, v, kk, b):
    bsz, T, H, N = r.shape

    def step(state, inp):
        r_t, w_t, k_t, v_t, kk_t, b_t = inp
        sa = jnp.einsum('bhvk,bhk->bhv', state, kk_t)
        state = (state * w_t[:, :, None, :] - sa[..., None] * b_t[:, :, None, :]
                 + v_t[..., None] * k_t[:, :, None, :])
        return state, jnp.einsum('bhvk,bhk->bhv', state, r_t)

    xs = tuple(jnp.swapaxes(t, 0, 1) for t in (r, w, k, v, kk, b))
    state0 = jnp.zeros((bsz, H, N, N), r.dtype)
    _, o = lax.scan(step, state0, xs)
    return jnp.swapaxes(o, 0, 1)

def rwkv7_group(p, mu, w0, w2, a0, a2, g2, k_k, k_a, r_k, lnx_w, lnx_b):
    bsz, T, _ = p.shape
    H, N = RWKV_HEADS, RWKV_HEAD_DIM
    p_prev = jnp.pad(p, ((0, 0), (1, 0), (0, 0)))[:, :-1]
    xs = p + (p_prev - p) * mu
    r, k, v, w_lo, a_lo, g_lo = jnp.split(
        xs, [D_A, 2 * D_A, 3 * D_A, 3 * D_A + RWKV_DECAY_LORA,
             3 * D_A + RWKV_DECAY_LORA + RWKV_AAA_LORA], axis=-1)
    w_log = -jax.nn.softplus(-(w0 + jnp.tanh(w_lo) @ w2)) - 0.5
    decay = jnp.exp(-jnp.exp(w_log))
    a = jax.nn.sigmoid(a0 + a_lo @ a2)
    g = jax.nn.sigmoid(g_lo) @ g2
    kk = l2_normalize((k * k_k).reshape(bsz, T, H, N))
    k = k * (1.0 + (a - 1.0) * k_a)
    r_h, k_h, v_h, a_h, w_h = (t.reshape(bsz, T, H, N) for t in (r, k, v, a, decay))
    o = rwkv7_scan(r_h, w_h, k_h, v_h, kk, kk * a_h)
    mean = jnp.mean(o, axis=-1, keepdims=True)
    var = jnp.mean(jnp.square(o - mean), axis=-1, keepdims=True)
    o = ((o - mean) * lax.rsqrt(var + RWKV_GN_EPS)).reshape(bsz, T, D_A) * lnx_w + lnx_b
    bonus = jnp.sum(r_h * k_h * r_k, axis=-1, keepdims=True) * v_h
    return (o + bonus.reshape(bsz, T, D_A)) * g

def gated_delta_rule_chunked(q, k, v, g, beta):
    bsz, T, H, DK = q.shape
    DV = v.shape[-1]
    C = GDN_CHUNK
    n = T // C

    def to_chunks(t):
        return jnp.moveaxis(t.reshape((bsz, n, C, H) + t.shape[3:]), 3, 1)

    q = to_chunks(q * DK ** -0.5)
    k = to_chunks(k)
    v = to_chunks(v)
    beta = to_chunks(beta)
    g = jnp.cumsum(to_chunks(g), axis=-1)
    causal = jnp.tril(jnp.ones((C, C), dtype=bool))
    strict = jnp.tril(jnp.ones((C, C), dtype=bool), -1)
    decay = jnp.exp(jnp.where(causal, g[..., :, None] - g[..., None, :], -jnp.inf))
    kb = k * beta[..., None]
    lower = jnp.where(strict, jnp.einsum('bhncd,bhnsd->bhncs', kb, k) * decay, 0.0)
    eye = jnp.eye(C, dtype=lower.dtype)
    rhs = jnp.concatenate([v * beta[..., None], kb * jnp.exp(g)[..., None]], axis=-1)
    sol = lax.linalg.triangular_solve(eye + lower, rhs, left_side=True, lower=True,
                                      unit_diagonal=True)
    u, w = sol[..., :DV], sol[..., DV:]
    intra = jnp.where(causal, jnp.einsum('bhncd,bhnsd->bhncs', q, k) * decay, 0.0)

    def step(state, inp):
        q_c, k_c, u_c, w_c, g_c, a_c = inp
        v_new = u_c - jnp.einsum('bhcd,bhdv->bhcv', w_c, state)
        o_c = (jnp.einsum('bhcd,bhdv->bhcv', q_c * jnp.exp(g_c)[..., None], state)
               + jnp.einsum('bhcs,bhsv->bhcv', a_c, v_new))
        g_last = g_c[..., -1:]
        state = (state * jnp.exp(g_last)[..., None]
                 + jnp.einsum('bhcd,bhcv->bhdv', k_c * jnp.exp(g_last - g_c)[..., None], v_new))
        return state, o_c

    xs = tuple(jnp.moveaxis(t, 2, 0) for t in (q, k, u, w, g, intra))
    state0 = jnp.zeros((bsz, H, DK, DV), q.dtype)
    _, o = lax.scan(step, state0, xs)
    return o.transpose(1, 0, 3, 2, 4).reshape(bsz, T, H, DV)

def gdn_group(p, conv_w, a_log, dt_bias, norm_w):
    bsz, T, _ = p.shape
    H, Dh = GDN_HEADS, GDN_HEAD_DIM
    qkv, z, beta_lo, a_lo = jnp.split(p, [3 * D_B, 4 * D_B, 4 * D_B + H], axis=-1)
    qkv = jax.nn.silu(causal_depthwise_conv(qkv, conv_w))
    q, k, v = (t.reshape(bsz, T, H, Dh) for t in jnp.split(qkv, 3, axis=-1))
    q = l2_normalize(q)
    k = l2_normalize(k)
    beta = jax.nn.sigmoid(beta_lo)
    g = -jnp.exp(a_log) * jax.nn.softplus(a_lo + dt_bias)
    o = gated_delta_rule_chunked(q, k, v, g, beta)
    o = o * lax.rsqrt(jnp.mean(o * o, axis=-1, keepdims=True) + NORM_EPS) * norm_w
    o = o * jax.nn.silu(z.reshape(bsz, T, H, Dh))
    return o.reshape(bsz, T, D_B)

def _linear_combine(c1, c2):
    a1, b1 = c1
    a2, b2 = c2
    return a1 * a2, a2 * b1 + b2

def rglru_group(p, conv_w, conv_b, w_a, b_a, w_x, b_x, lam):
    bsz, T, _ = p.shape
    xb, gate = jnp.split(p, [D_C], axis=-1)
    xb = causal_depthwise_conv(xb, conv_w) + conv_b
    blocks = xb.reshape(bsz, T, LRU_BLOCKS, LRU_BLOCK_DIM)
    r = jax.nn.sigmoid(jnp.einsum('btnc,ncd->btnd', blocks, w_a.astype(blocks.dtype)).reshape(bsz, T, D_C) + b_a)
    i = jax.nn.sigmoid(jnp.einsum('btnc,ncd->btnd', blocks, w_x.astype(blocks.dtype)).reshape(bsz, T, D_C) + b_x)
    log_a = -LRU_C * r * jax.nn.softplus(-lam)
    a = jnp.exp(log_a)
    mult = jnp.sqrt(-jnp.expm1(2.0 * log_a))
    mult = jnp.where(jnp.arange(T)[None, :, None] == 0, 1.0, mult)
    _, h = lax.associative_scan(_linear_combine, (a, xb * i * mult), axis=1)
    return h * jax.nn.gelu(gate, approximate=True)

def hybrid_mixer(h, w_in, w_out, rwkv_mu, rwkv_w0, rwkv_w2, rwkv_a0, rwkv_a2, rwkv_g2,
                 rwkv_k_k, rwkv_k_a, rwkv_r_k, rwkv_lnx_w, rwkv_lnx_b,
                 gdn_conv_w, gdn_a_log, gdn_dt_bias, gdn_norm_w,
                 lru_conv_w, lru_conv_b, lru_w_a, lru_b_a, lru_w_x, lru_b_x, lru_lambda):
    proj = jnp.matmul(h, w_in).astype(jnp.float32)
    p_a, p_b, p_c = jnp.split(proj, [A_COLS, A_COLS + B_COLS], axis=-1)
    o_a = rwkv7_group(p_a, rwkv_mu, rwkv_w0, rwkv_w2, rwkv_a0, rwkv_a2, rwkv_g2,
                      rwkv_k_k, rwkv_k_a, rwkv_r_k, rwkv_lnx_w, rwkv_lnx_b)
    o_b = gdn_group(p_b, gdn_conv_w, gdn_a_log, gdn_dt_bias, gdn_norm_w)
    o_c = rglru_group(p_c, lru_conv_w, lru_conv_b, lru_w_a, lru_b_a, lru_w_x, lru_b_x, lru_lambda)
    mix = jnp.concatenate([o_a, o_b, o_c], axis=-1).astype(h.dtype)
    return jnp.matmul(mix, w_out)

def hierarchical_moe(h, w_group, b_group, w_expert, b_expert, w_gate, w_up, w_down):
    bsz, T, D = h.shape
    n_tok = bsz * T
    xt = h.reshape(n_tok, D)
    grp_logits = jnp.matmul(xt, w_group).astype(jnp.float32) + b_group.astype(jnp.float32)
    grp_idx = jnp.argmax(grp_logits, axis=-1)
    grp_w = jnp.take_along_axis(jax.nn.softmax(grp_logits, axis=-1), grp_idx[:, None], axis=-1)[:, 0]
    exp_logits = (jnp.matmul(xt, w_expert).astype(jnp.float32) + b_expert.astype(jnp.float32)
                  ).reshape(n_tok, MOE_GROUPS, MOE_EXPERTS_PER_GROUP)
    exp_logits = jnp.take_along_axis(exp_logits, grp_idx[:, None, None], axis=1)[:, 0]
    top_val, top_loc = lax.top_k(exp_logits, MOE_TOP_K)
    gate = jax.nn.softmax(top_val, axis=-1) * grp_w[:, None]
    eid = (grp_idx[:, None] * MOE_EXPERTS_PER_GROUP + top_loc).reshape(-1).astype(jnp.int32)
    n_assign = n_tok * MOE_TOP_K
    tok = jnp.arange(n_assign, dtype=jnp.int32) // MOE_TOP_K
    order = jnp.argsort(eid)
    eid_s, tok_s, gate_s = eid[order], tok[order], gate.reshape(-1)[order]
    counts = jnp.bincount(eid, length=MOE_EXPERTS)
    padded = (counts + MOE_BLOCK - 1) // MOE_BLOCK * MOE_BLOCK
    pad_end = jnp.cumsum(padded)
    pad_start = pad_end - padded
    start = jnp.cumsum(counts) - counts
    dest = pad_start[eid_s] + jnp.arange(n_assign, dtype=jnp.int32) - start[eid_s]
    n_blocks = (n_assign + MOE_EXPERTS * (MOE_BLOCK - 1) + MOE_BLOCK - 1) // MOE_BLOCK
    buf_len = n_blocks * MOE_BLOCK
    buf_tok = jnp.full((buf_len,), n_tok, dtype=jnp.int32).at[dest].set(tok_s)
    blk_expert = jnp.minimum(
        jnp.searchsorted(pad_end, jnp.arange(n_blocks) * MOE_BLOCK, side='right'), MOE_EXPERTS - 1)
    x_pad = jnp.concatenate([xt, jnp.zeros((1, D), xt.dtype)], axis=0)
    xb = x_pad[buf_tok].reshape(n_blocks, MOE_BLOCK, D)

    def expert_block(args):
        x_blk, e = args
        hid = jax.nn.silu(jnp.matmul(x_blk, w_gate[e])) * jnp.matmul(x_blk, w_up[e])
        return jnp.matmul(hid, w_down[e])

    yb = lax.map(expert_block, (xb, blk_expert)).reshape(buf_len, D)
    contrib = (yb[dest].astype(jnp.float32) * gate_s[:, None]).astype(h.dtype)
    y = jnp.zeros((n_tok, D), h.dtype).at[tok_s].add(contrib)
    return y.reshape(bsz, T, D)

def setup_inputs(seed: int = 0) -> dict:
    key = jax.random.key(seed)
    keys = iter(jax.random.split(key, 35))
    f32 = jnp.float32

    def nrm(shape, scale):
        return jax.random.normal(next(keys), shape, f32) * scale

    def uni(shape, lo, hi):
        return jax.random.uniform(next(keys), shape, f32, lo, hi)

    L = DEPTH
    x = nrm((BATCH, SEQ, D_MODEL), 1.0)
    norm_mix = 1.0 + nrm((L, D_MODEL), 0.02)
    norm_ffn = 1.0 + nrm((L, D_MODEL), 0.02)
    norm_final = 1.0 + nrm((D_MODEL,), 0.02)
    w_in = nrm((L, D_MODEL, N_IN), D_MODEL ** -0.5)
    w_out = nrm((L, D_MIX, D_MODEL), D_MIX ** -0.5)
    rwkv_mu = uni((L, A_COLS), 0.0, 1.0)
    rwkv_w0 = uni((L, D_A), -6.0, -1.0)
    rwkv_w2 = nrm((L, RWKV_DECAY_LORA, D_A), 0.5 * RWKV_DECAY_LORA ** -0.5)
    rwkv_a0 = nrm((L, D_A), 0.1)
    rwkv_a2 = nrm((L, RWKV_AAA_LORA, D_A), RWKV_AAA_LORA ** -0.5)
    rwkv_g2 = nrm((L, RWKV_GATE_LORA, D_A), RWKV_GATE_LORA ** -0.5)
    rwkv_k_k = 0.85 + nrm((L, D_A), 0.02)
    rwkv_k_a = 1.0 + nrm((L, D_A), 0.02)
    rwkv_r_k = nrm((L, RWKV_HEADS, RWKV_HEAD_DIM), 0.1)
    rwkv_lnx_w = 1.0 + nrm((L, D_A), 0.02)
    rwkv_lnx_b = nrm((L, D_A), 0.02)
    gdn_conv_w = nrm((L, CONV_WIDTH, 3 * D_B), CONV_WIDTH ** -0.5)
    gdn_a_log = jnp.log(uni((L, GDN_HEADS), 1.0, 16.0))
    dt = jnp.exp(uni((L, GDN_HEADS), math.log(1e-3), math.log(1e-1)))
    gdn_dt_bias = dt + jnp.log(-jnp.expm1(-dt))
    gdn_norm_w = 1.0 + nrm((L, GDN_HEAD_DIM), 0.02)
    lru_conv_w = nrm((L, CONV_WIDTH, D_C), CONV_WIDTH ** -0.5)
    lru_conv_b = nrm((L, D_C), 0.02)
    lru_w_a = nrm((L, LRU_BLOCKS, LRU_BLOCK_DIM, LRU_BLOCK_DIM), LRU_BLOCK_DIM ** -0.5)
    lru_b_a = nrm((L, D_C), 0.02)
    lru_w_x = nrm((L, LRU_BLOCKS, LRU_BLOCK_DIM, LRU_BLOCK_DIM), LRU_BLOCK_DIM ** -0.5)
    lru_b_x = nrm((L, D_C), 0.02)
    s = uni((L, D_C), 0.9, 0.999) ** (1.0 / LRU_C)
    lru_lambda = jnp.log(s) - jnp.log1p(-s)
    moe_w_group = nrm((L, D_MODEL, MOE_GROUPS), D_MODEL ** -0.5)
    moe_b_group = nrm((L, MOE_GROUPS), 0.01)
    moe_w_expert = nrm((L, D_MODEL, MOE_EXPERTS), D_MODEL ** -0.5)
    moe_b_expert = nrm((L, MOE_EXPERTS), 0.01)
    moe_w_gate = nrm((L, MOE_EXPERTS, D_MODEL, D_EXPERT), D_MODEL ** -0.5)
    moe_w_up = nrm((L, MOE_EXPERTS, D_MODEL, D_EXPERT), D_MODEL ** -0.5)
    moe_w_down = nrm((L, MOE_EXPERTS, D_EXPERT, D_MODEL), D_EXPERT ** -0.5)
    return {
        'x': x, 'norm_mix': norm_mix, 'norm_ffn': norm_ffn, 'norm_final': norm_final,
        'w_in': w_in, 'w_out': w_out,
        'rwkv_mu': rwkv_mu, 'rwkv_w0': rwkv_w0, 'rwkv_w2': rwkv_w2, 'rwkv_a0': rwkv_a0,
        'rwkv_a2': rwkv_a2, 'rwkv_g2': rwkv_g2, 'rwkv_k_k': rwkv_k_k, 'rwkv_k_a': rwkv_k_a,
        'rwkv_r_k': rwkv_r_k, 'rwkv_lnx_w': rwkv_lnx_w, 'rwkv_lnx_b': rwkv_lnx_b,
        'gdn_conv_w': gdn_conv_w, 'gdn_a_log': gdn_a_log, 'gdn_dt_bias': gdn_dt_bias,
        'gdn_norm_w': gdn_norm_w,
        'lru_conv_w': lru_conv_w, 'lru_conv_b': lru_conv_b, 'lru_w_a': lru_w_a, 'lru_b_a': lru_b_a,
        'lru_w_x': lru_w_x, 'lru_b_x': lru_b_x, 'lru_lambda': lru_lambda,
        'moe_w_group': moe_w_group, 'moe_b_group': moe_b_group, 'moe_w_expert': moe_w_expert,
        'moe_b_expert': moe_b_expert, 'moe_w_gate': moe_w_gate, 'moe_w_up': moe_w_up,
        'moe_w_down': moe_w_down,
    }

def reference(x, norm_mix, norm_ffn, norm_final, w_in, w_out,
              rwkv_mu, rwkv_w0, rwkv_w2, rwkv_a0, rwkv_a2, rwkv_g2, rwkv_k_k, rwkv_k_a,
              rwkv_r_k, rwkv_lnx_w, rwkv_lnx_b,
              gdn_conv_w, gdn_a_log, gdn_dt_bias, gdn_norm_w,
              lru_conv_w, lru_conv_b, lru_w_a, lru_b_a, lru_w_x, lru_b_x, lru_lambda,
              moe_w_group, moe_b_group, moe_w_expert, moe_b_expert, moe_w_gate, moe_w_up,
              moe_w_down):
    for l in range(DEPTH):
        h = rms_norm(x, norm_mix[l])
        x = x + hybrid_mixer(h, w_in[l], w_out[l],
                             rwkv_mu[l], rwkv_w0[l], rwkv_w2[l], rwkv_a0[l], rwkv_a2[l],
                             rwkv_g2[l], rwkv_k_k[l], rwkv_k_a[l], rwkv_r_k[l],
                             rwkv_lnx_w[l], rwkv_lnx_b[l],
                             gdn_conv_w[l], gdn_a_log[l], gdn_dt_bias[l], gdn_norm_w[l],
                             lru_conv_w[l], lru_conv_b[l], lru_w_a[l], lru_b_a[l],
                             lru_w_x[l], lru_b_x[l], lru_lambda[l])
        h = rms_norm(x, norm_ffn[l])
        x = x + hierarchical_moe(h, moe_w_group[l], moe_b_group[l], moe_w_expert[l],
                                 moe_b_expert[l], moe_w_gate[l], moe_w_up[l], moe_w_down[l])
    return rms_norm(x, norm_final)


_drawn_inputs = setup_inputs


def setup_inputs(seed=0):
    import zlib

    import numpy as np

    out = dict(_drawn_inputs(seed))
    spreads = {}
    factors = {'norm_final': 9.005,
     'rwkv_w2': 3.214,
     'rwkv_k_k': 9.745,
     'rwkv_k_a': 2.698,
     'rwkv_lnx_w': 11.435,
     'rwkv_lnx_b': 12.254,
     'gdn_norm_w': 7.599,
     'lru_b_a': 36.161,
     'lru_b_x': 27.354,
     'moe_b_group': 8.646,
     'moe_b_expert': 4.682,
     'norm_ffn': 2.971}
    for name, (base, spread) in spreads.items():
        noise = np.random.default_rng([zlib.crc32(name.encode()), seed]).standard_normal(out[name].shape)
        drawn = base * np.exp(spread * noise) if base else spread * noise
        out[name] = jnp.asarray(drawn.astype(out[name].dtype))
    for name, factor in factors.items():
        out[name] = (out[name] * factor).astype(out[name].dtype)
    return out
```

```python
from contextlib import ExitStack

import numpy as np

import concourse.bass as bass
from concourse import mybir

F32 = mybir.dt.float32
I32 = mybir.dt.int32
U32 = mybir.dt.uint32
ALU = mybir.AluOpType
ACT = mybir.ActivationFunctionType
AX = mybir.AxisListType.X

P = 128
T = 1024
D = 1024
NT = T // P
KT = D // P
HALF = 512
EPS = 1e-6

DA, DB, DC = D // 4, D // 2, D // 4
A_COLS = 3 * DA + 32 + 32 + 64
B_COLS = 4 * DB + 8
COL_B = A_COLS
COL_BETA = COL_B + 4 * DB
COL_C = A_COLS + B_COLS
GN_EPS = 64e-5
EM05 = float(np.exp(-0.5))

GH = 4
NG = T // P
CR = 64
NCR = T // CR

E = 32
DE = D // 4
NOV = 15
NBLK = E + NOV

PAR = {}
_n = 0
for _name, _rows in (("norm_mix", 8), ("norm_ffn", 8), ("mu_lo", 1), ("rwkv", 20), ("gdn_conv", 48),
                     ("lru_conv", 8), ("lru_conv_b", 2), ("lru_b_a", 2), ("lru_b_x", 2),
                     ("lru_lambda", 2), ("gdn_norm", 1)):
    PAR[_name] = _n
    _n += _rows
NPAR = _n

CON = {}
_n = 0
for _name, _cols in (("ident", P), ("ones", P), ("ones64", P), ("upper", P), ("below", P), ("low", P),
                     ("low_strict", P), ("up64_strict", P), ("up64", P), ("lev_low", 7 * P),
                     ("lev_up", 6 * P), ("iota128", P), ("iota_blk", NBLK), ("iota_tok", NT),
                     ("iota_e", E), ("iota_e128", E), ("half", 2), ("j128", 7), ("iota_p", 1), ("idx4", 4),
                     ("keep", 2), ("nhalf", 2)):
    CON[_name] = (_n, _cols)
    _n += _cols
NCON = _n


def constants():
    c = np.zeros((P, NCON), np.float32)
    i, j = np.arange(P)[:, None], np.arange(P)[None, :]

    def put(name, value):
        a, n = CON[name]
        c[:, a:a + n] = value

    put("ident", i == j)
    put("ones", 1)
    put("ones64", i // 64 == j // 64)
    put("upper", i <= j)
    put("below", i < j)
    put("low", i >= j)
    put("low_strict", i > j)
    put("up64_strict", (i < j) & (i // 64 == j // 64))
    put("up64", (i <= j) & (i // 64 == j // 64))
    lev = [(i // (2 * s) == j // (2 * s)) & (i % (2 * s) >= s) & (j % (2 * s) < s) for s in (1, 2, 4, 8, 16, 32, 64)]
    put("lev_low", np.concatenate(lev, 1))
    put("lev_up", np.concatenate([m.T for m in lev[:6]], 1))
    put("iota128", j)
    put("iota_blk", np.arange(NBLK)[None, :])
    put("iota_tok", i + P * np.arange(NT)[None, :])
    put("iota_e", np.arange(E)[None, :])
    put("iota_e128", P * np.arange(E)[None, :])
    put("half", i // 64 == np.arange(2)[None, :])
    put("j128", P * np.arange(1, 8)[None, :])
    put("iota_p", i)
    put("idx4", 4 - np.arange(4)[None, :])
    put("keep", np.arange(2)[None, :])
    put("nhalf", -1.0 * (i // 64 == np.arange(2)[None, :]))
    return c


class Step:

    def __init__(self, eng, sem, base=0):
        self.eng, self.sem, self.base, self.n = eng, sem, base, 0

    def inc(self, ins):
        ins.then_inc(self.sem, 1)
        self.n += 1

    def wait(self):
        self.eng.wait_ge(self.sem, self.base + self.n)

    def __call__(self, ins):
        self.inc(ins)
        self.wait()


class Build:
    def __init__(self, nc, ins, out):
        self.nc, self.i, self.out = nc, ins, out
        self.ctx = ExitStack()

    def sb(self, ctx, name, shape, dt=F32):
        return ctx.enter_context(self.nc.sbuf_tensor(name, shape, dt))

    def sem(self, ctx, name):
        return self.nc.alloc_semaphore(name)

    def run_stage(self, stage):
        before = self.nc.snapshot_sems()
        stage()
        self.nc.clear_and_free_semaphores(self.nc.allocated_since(before))
        self.nc.all_engine_barrier()

    def con(self, name):
        a, n = CON[name]
        return self.cons[:, a:a + n]

    def parc(self, name, k=0, n=1):
        return self.par[:, PAR[name] + k:PAR[name] + k + n]

    def pass_gate(self, eng):
        eng.sem_inc(self.gates[eng.engine], 1)

    def norm_stage(self):
        nc = self.nc
        with ExitStack() as c:
            x = self.sb(c, "x_in", [P, NT, D])
            sq = self.sb(c, "x_sq", [P, D])
            prow = self.sb(c, "par_rows_sb", [P, P])
            ss = self.sb(c, "x_ss", [P, NT])
            rs = self.sb(c, "x_rs", [P, NT])
            s_par, s_con, s_x, s_ss, s_v, s_rs, s_xn, s_tr, s_par_t, s_par_ok = (
                self.sem(c, n) for n in ("par_landed", "cons_landed", "x_landed", "x_squared", "norm_dve", "norm_root", "x_scaled", "x_turned", "par_turned", "par_ready"))
            s_ev = [self.sem(c, "turned_out_dve"), self.sem(c, "turned_out_act")]
            block = c.enter_context(nc.Block())
            xv = self.i["x"].rearrange("(i p) d -> p i d", p=P)

            @block.sync
            def _(sp):
                sp.dma_start(x[:, 0, :], xv[:, 0, :]).then_inc(s_x, 16)
                sp.dma_start(prow[0:NPAR, :], self.i["par_rows"]).then_inc(s_par, 16)
                sp.dma_start(self.cons[:], self.i["cons"]).then_inc(s_con, 16)
                for i in range(1, NT):
                    sp.wait_ge(s_x, 16 * i)
                    sp.dma_start(x[:, i, :], xv[:, i, :]).then_inc(s_x, 16)

            @block.scalar
            def _(act):
                for i in range(NT):
                    act.wait_ge(s_x, 16 * (i + 1))
                    if i:
                        act.wait_ge(s_ss, i)
                    act.activation(sq[:], x[:, i, :], ACT.Square, accum_out=ss[:, i:i + 1]).then_inc(s_ss, 1)
                act.wait_ge(s_v, 2)
                act.activation(rs[:], rs[:], ACT.Sqrt).then_inc(s_rs, 1)
                act.wait_ge(s_par_ok, 1)
                for t in range(1, 2 * KT, 2):
                    self.norm_out(act, t, s_tr, s_ev)

            @block.vector
            def _(dve):
                dve.wait_ge(s_ss, NT)
                dve.tensor_scalar(rs[:], ss[:], 1.0 / D, EPS, ALU.mult, ALU.add).then_inc(s_v, 1)
                dve.wait_ge(s_v, 1)
                dve.reciprocal(rs[:], rs[:]).then_inc(s_v, 1)
                dve.wait_ge(s_rs, 1)
                for i in range(NT):
                    dve.tensor_scalar(x[:, i, :], x[:, i, :], rs[:, i:i + 1], None, ALU.mult).then_inc(s_xn, 1)
                dve.wait_ge(s_par_t, 1)
                dve.tensor_copy(self.par[:, 0:NPAR], self.bank[7][:, 0:NPAR]).then_inc(s_par_ok, 1)
                dve.wait_ge(s_par_ok, 1)
                for t in range(0, 2 * KT, 2):
                    self.norm_out(dve, t, s_tr, s_ev)

            @block.tensor
            def _(pe):
                pe.wait_ge(s_par, 16)
                pe.wait_ge(s_con, 16)
                pe.transpose(self.bank[7][:, 0:NPAR], prow[0:NPAR, :], self.con("ident")[0:NPAR, 0:NPAR]).then_inc(s_par_t, 1)
                for t in range(2 * KT):
                    kt, half = t // 2, t % 2
                    pe.wait_ge(s_xn, 4 * half + 4)
                    if t >= 6:
                        pe.wait_ge(s_ev[t % 2], (t - 6) // 2 + 1)
                    for q in range(4):
                        ins = pe.transpose(self.bank[t % 6][:, q * P:(q + 1) * P],
                                           x[:, 4 * half + q, kt * P:(kt + 1) * P], self.con("ident"))
                    ins.then_inc(s_tr, 1)

    def norm_out(self, eng, t, s_tr, s_ev):
        kt, half = t // 2, t % 2
        eng.wait_ge(s_tr, t + 1)
        dst = self.hT[:, kt, half * HALF:(half + 1) * HALF]
        gain = self.parc("norm_mix", kt)
        if t % 2 == 0:
            eng.tensor_scalar(dst, self.bank[t % 6][:], gain, None, ALU.mult).then_inc(s_ev[0], 1)
        else:
            eng.activation(dst, self.bank[t % 6][:], ACT.Copy, scale=gain).then_inc(s_ev[1], 1)

    def lru_stage(self):
        nc = self.nc
        with ExitStack() as c:
            w = self.sb(c, "lru_w", [P, KT, 2 * DC])
            wg = self.sb(c, "lru_gate_w", [P, 2, 2, P])
            raw = self.sb(c, "lru_raw", [P, 2, 3 + T])
            xb = self.sb(c, "lru_xb", [P, 2, T])
            gg = self.sb(c, "lru_gelu", [P, 2, T])
            r = self.sb(c, "lru_r", [P, 2, T])
            ig = self.sb(c, "lru_i", [P, 2, T])
            a = self.sb(c, "lru_a", [P, 2, T])
            th = self.sb(c, "lru_tanh", [P, 2, T])
            lt = self.sb(c, "lru_ln", [P, 2, T])
            v = self.sb(c, "lru_small", [P, 12, 2])
            S = {n: self.sem(c, "lru_" + n) for n in (
                "w", "wz", "wg", "proj", "raw", "gelu", "conv", "gates", "sig", "spe", "spd", "act", "step", "init", "out")}
            block = c.enter_context(nc.Block())

            @block.sync
            def _(sp):
                for kt in range(KT):
                    sp.dma_start(w[:, kt, :], self.i["w_in"][kt * P:(kt + 1) * P, COL_C:COL_C + 2 * DC]).then_inc(S["w"], 16)
                sp.wait_ge(S["wz"], 1)
                for g, name in enumerate(("lru_w_a", "lru_w_x")):
                    for b in range(4):
                        o = 64 * (b % 2)
                        sp.dma_start(wg[o:o + 64, g, b // 2, o:o + 64], self.i[name][b]).then_inc(S["wg"], 16)

            @block.gpsimd
            def _(pool):
                pool.memset(wg[:], 0.0).then_inc(S["wz"], 1)
                pool.memset(raw[:, :, 0:3], 0.0).then_inc(S["init"], 1)

            @block.tensor
            def _(pe):
                pe.wait_ge(S["w"], 16 * KT)
                for m in range(4):
                    for kt in range(KT):
                        for half in range(2):
                            ins = pe.matmul(self.bank[2 * m + half][:], w[:, kt, m * P:(m + 1) * P],
                                            self.hT[:, kt, half * HALF:(half + 1) * HALF], start=kt == 0, stop=kt == KT - 1)
                    ins.then_inc(S["proj"], 1)
                pe.wait_ge(S["wg"], 16 * 8)
                pe.wait_ge(S["raw"], 4)
                pe.wait_ge(S["conv"], 8)
                for g in range(2):
                    if g:
                        pe.wait_ge(S["gelu"], 4)
                    for j in range(2):
                        for half in range(2):
                            pe.matmul(self.bank[4 * g + 2 * j + half][:], wg[:, g, j, :],
                                      xb[:, j, half * HALF:(half + 1) * HALF], start=True, stop=True).then_inc(S["gates"], 1)

            @block.scalar
            def _(act):
                act.wait_ge(S["spd"], 2)
                act.activation(v[:, 2, :], v[:, 1, :], ACT.Exp, scale=-1.0).then_inc(S["spe"], 1)
                act.wait_ge(S["spd"], 3)
                act.activation(v[:, 4, :], v[:, 3, :], ACT.Ln).then_inc(S["spe"], 1)
                for m in range(2):
                    act.wait_ge(S["proj"], m + 1)
                    for half in range(2):
                        act.activation(raw[:, m, 3 + half * HALF:3 + (half + 1) * HALF], self.bank[2 * m + half][:],
                                       ACT.Copy).then_inc(S["raw"], 1)
                for m in range(2):
                    act.wait_ge(S["proj"], m + 3)
                    for half in range(2):
                        act.activation(gg[:, m, half * HALF:(half + 1) * HALF], self.bank[4 + 2 * m + half][:],
                                       ACT.Gelu_apprx_tanh).then_inc(S["gelu"], 1)
                for g, dst, bias in ((0, r, "lru_b_a"), (1, ig, "lru_b_x")):
                    for j in range(2):
                        for half in range(2):
                            act.wait_ge(S["gates"], 4 * g + 2 * j + half + 1)
                            act.activation(dst[:, j, half * HALF:(half + 1) * HALF], self.bank[4 * g + 2 * j + half][:],
                                           ACT.Sigmoid, bias=self.parc(bias, j)).then_inc(S["sig"], 1)
                act.wait_ge(S["spd"], 13)
                act.wait_ge(S["sig"], 8)
                for j in range(2):
                    act.activation(a[:, j, :], r[:, j, :], ACT.Exp, scale=v[:, 11, j:j + 1]).then_inc(S["act"], 1)
                    act.activation(th[:, j, :], r[:, j, :], ACT.Tanh, scale=v[:, 11, j:j + 1]).then_inc(S["act"], 1)
                act.wait_ge(S["act"], 4)
                act.activation(lt[:], th[:], ACT.Ln, scale=-1.0, bias=1.0).then_inc(S["act"], 1)
                act.activation(r[:], th[:], ACT.Sqrt, scale=-2.0).then_inc(S["act"], 1)
                act.wait_ge(S["act"], 6)
                act.activation(lt[:], lt[:], ACT.Exp, scale=-0.5).then_inc(S["act"], 1)

            @block.vector
            def _(dve):
                step = Step(dve, S["step"])
                lam = self.parc("lru_lambda", 0, 2)
                dve.tensor_scalar(v[:, 0, :], lam, -1.0, None, ALU.mult).then_inc(S["spd"], 1)
                dve.wait_ge(S["spd"], 1)
                dve.tensor_tensor(v[:, 1, :], v[:, 0, :], lam, ALU.max).then_inc(S["spd"], 1)
                dve.wait_ge(S["spe"], 1)
                dve.tensor_scalar(v[:, 3, :], v[:, 2, :], 1.0, None, ALU.add).then_inc(S["spd"], 1)
                dve.wait_ge(S["spe"], 2)
                sp = Step(dve, S["spd"])
                sp.n = 3
                sp.wait()
                sp(dve.tensor_scalar(v[:, 5, :], v[:, 3, :], -1.0, None, ALU.add))
                sp(dve.tensor_scalar(v[:, 6, :], v[:, 5, :], 1e-30, None, ALU.max))
                sp(dve.reciprocal(v[:, 7, :], v[:, 6, :]))
                sp(dve.tensor_tensor(v[:, 8, :], v[:, 4, :], v[:, 2, :], ALU.mult))
                sp(dve.tensor_tensor(v[:, 8, :], v[:, 8, :], v[:, 7, :], ALU.mult))
                sp(dve.tensor_scalar(v[:, 9, :], v[:, 5, :], 0.0, None, ALU.is_equal))
                sp(dve.tensor_tensor(v[:, 9, :], v[:, 9, :], v[:, 2, :], ALU.mult))
                sp(dve.tensor_tensor(v[:, 8, :], v[:, 8, :], v[:, 9, :], ALU.add))
                sp(dve.tensor_scalar(v[:, 10, :], v[:, 0, :], 0.0, None, ALU.max))
                dve.tensor_tensor(v[:, 10, :], v[:, 10, :], v[:, 8, :], ALU.add).then_inc(S["step"], 1)
                step.n = 1
                step.wait()
                sp.inc(dve.tensor_scalar(v[:, 11, :], v[:, 10, :], -8.0, None, ALU.mult))
                dve.wait_ge(S["raw"], 4)
                dve.wait_ge(S["init"], 1)
                for j in range(2):
                    taps = [self.parc("lru_conv", 4 * j + t) for t in range(4)]
                    dve.tensor_scalar(xb[:, j, :], raw[:, j, 3:3 + T], taps[3], self.parc("lru_conv_b", j),
                                      ALU.mult, ALU.add).then_inc(S["conv"], 1)
                    for t in (2, 1, 0):
                        dve.wait_ge(S["conv"], 4 * j + 3 - t)
                        dve.scalar_tensor_tensor(xb[:, j, :], raw[:, j, t:t + T], taps[t], xb[:, j, :],
                                                 ALU.mult, ALU.add).then_inc(S["conv"], 1)
                dve.wait_ge(S["sig"], 8)
                dve.wait_ge(S["conv"], 8)
                step(dve.tensor_tensor(xb[:], xb[:], ig[:], ALU.mult))
                dve.wait_ge(S["act"], 7)
                step(dve.tensor_tensor(lt[:], lt[:], r[:], ALU.mult))
                step(dve.memset(lt[:, :, 0:1], 1.0))
                step(dve.tensor_tensor(xb[:], xb[:], lt[:], ALU.mult))
                for j in range(2):
                    step.inc(dve.tensor_tensor_scan(th[:, j, :], a[:, j, :], xb[:, j, :], 0.0, ALU.mult, ALU.add))
                step.wait()
                dve.wait_ge(S["gelu"], 4)
                dve.tensor_tensor(self.mixT[:, 6:8, :], th[:], gg[:], ALU.mult).then_inc(S["out"], 1)

    def invert_pe(self, pe, W, S, lhs, upd, tur, ye, levels, final_turn):
        for lv in range(levels + (1 if final_turn else 0)):
            for g in range(2):
                W(pe, "i_upd", 2 * lv + g + 1)
                for q in range(4):
                    ins = pe.transpose(self.bank[g][:, q * P:(q + 1) * P], upd[:, 4 * g + q, :], self.con("ident"))
                ins.then_inc(S["i_turn"], 1)
            if lv == levels:
                break
            for g in range(2):
                W(pe, "i_tur", 2 * lv + g + 1)
                for q in range(4):
                    ins = pe.matmul(self.bank[2 + g][:, q * P:(q + 1) * P], lhs[:, 4 * g + q, :], tur[:, 4 * g + q, :],
                                    start=True, stop=True)
                ins.then_inc(S["i_y"], 1)
            for g in range(2):
                W(pe, "i_ye", 2 * lv + g + 1)
                for q in range(4):
                    ins = pe.matmul(self.bank[4 + g][:, q * P:(q + 1) * P], ye[:, 4 * g + q, :], upd[:, 4 * g + q, :],
                                    start=True, stop=True)
                ins.then_inc(S["i_w"], 1)

    def invert_act(self, act, W, S, tur, ye, levels, final_turn):
        flat = lambda t, g: t[:, 4 * g:4 * g + 4, :].rearrange("p a b -> p (a b)")
        for lv in range(levels + (1 if final_turn else 0)):
            for g in range(2):
                W(act, "i_turn", 2 * lv + g + 1)
                act.activation(flat(tur, g), self.bank[g][:], ACT.Copy).then_inc(S["i_tur"], 1)
            if lv == levels:
                break
            for g in range(2):
                W(act, "i_y", 2 * lv + g + 1)
                act.activation(flat(ye, g), self.bank[2 + g][:], ACT.Copy).then_inc(S["i_ye"], 1)

    def invert_dve(self, dve, W, S, upd, masks, levels):
        for lv in range(levels):
            m = self.cons[:, CON[masks][0] + (lv + 1) * P:CON[masks][0] + (lv + 2) * P].bitcast(U32)
            for g in range(2):
                W(dve, "i_w", 2 * lv + g + 1)
                self.pass_gate(dve)
                dve.copy_predicated(upd[:, 4 * g:4 * g + 4, :], m.unsqueeze(1).to_broadcast([P, 4, P]),
                                    self.bank[4 + g][:].rearrange("p (a b) -> p a b", a=4)).then_inc(S["i_upd"], 1)

    def gdn_stage(self):
        nc = self.nc
        K = dict(w=48, proj=3, raw=6, sil=3, sq=2, ss=4, ln=4, rs=2, qn=2, gcr=2, gr=8, ge=2, gm=4, trv=2, trk=2,
                 kv=6, kk=2, qk=2, nn=8, am=2, at=2, ate=2, i_init=1, i_turn=14, i_tur=14, i_y=12, i_ye=12, i_w=12,
                 i_upd=14, u=2, ue=2, wt=2, wte=2, ws=8, vn=8, sk=8, st=9, qs=2, av=2, t1=2, o=2, osq=3, ol=2, og=2,
                 ot=2, mx=2, hs=3, pad=1, conv=12)
        with ExitStack() as c:
            zw = self.sb(c, "gdn_work", [P, 18624])
            wqkv = self.sb(c, "gdn_w", [P, 3, KT, P])
            zs = self.sb(c, "gdn_z", [P, GH, NG, P])
            scal = self.sb(c, "gdn_scal", [P, GH, 8, NG])
            hs = self.sb(c, "gdn_head_scal", [P, 8, NG])
            taps = self.sb(c, "gdn_taps", [P, 12])
            wb = self.sb(c, "gdn_w_beta", [P, KT, 8])
            ab = self.sb(c, "gdn_ab_sb", [P, 8])
            ba = self.sb(c, "gdn_ba", [P, NT, 8])
            sm = self.sb(c, "gdn_small", [P, 6, GH, NG])
            ev = self.sb(c, "gdn_ea", [P, GH])
            ssum = self.sb(c, "gdn_ssum", [P, 3, NG])
            off = [0]

            def carve(n, shape=None):
                a = zw[:, off[0]:off[0] + n]
                off[0] += n
                return a

            v3 = lambda a, k: a.rearrange("p (a b) -> p a b", a=k)
            r1 = carve(3 * (3 + T))
            raw = v3(r1, 3)
            e, ei, es = (v3(r1[:, k * T:(k + 1) * T], NG) for k in range(3))
            osb, osq, og = e, ei, es
            r2 = carve(3 * T)
            cv = v3(r2, 3)
            nn, am, at = (v3(r2[:, k * T:(k + 1) * T], NG) for k in range(3))
            r3 = carve(2 * T)
            sq = v3(r3, 2)
            upd, tur = (v3(r3[:, k * T:(k + 1) * T], NG) for k in range(2))
            qn, kn = (v3(carve(T), NG) for _ in range(2))
            kd, kbg, vb = (v3(carve(T), NG) for _ in range(3))
            r6 = carve(T)
            glb = ye = v3(r6, NG)
            u, wt = v3(carve(T), NG), v3(carve(T), NG)
            vn = v3(carve(T), NG)
            st = v3(carve(9 * P), 9)
            wz = v3(zw[:, 0:KT * DB], KT)
            flat = lambda t, a, b: t[:, a:b, :].rearrange("p a b -> p (a b)")
            S = {n: self.sem(c, "gdn_" + n) for n in K}
            Z = {n: self.sem(c, "gdnz_" + n) for n in ("w", "z", "zs", "ba", "d", "a", "pe", "hdone")}
            block = c.enter_context(nc.Block())
            win = self.i["w_in"].rearrange("(kt p) c -> p kt c", p=P)

            def waits(h):
                return lambda eng, name, n: eng.wait_ge(S[name], h * K[name] + n)

            @block.sync
            def _(sp):
                for kt in range(KT):
                    sp.dma_start(wz[:, kt, :], win[:, kt, COL_B + 3 * DB:COL_B + 4 * DB]).then_inc(Z["w"], 16)
                sp.dma_start(wb[:], win[:, :, COL_BETA:COL_BETA + 8]).then_inc(Z["w"], 16)
                sp.dma_start(ab[:], self.i["gdn_ab"].partition_broadcast(P)).then_inc(Z["w"], 16)
                with sp.Fori(0, GH) as h:
                    for m in range(3):
                        sp.dma_start(wqkv[:, m, :, :], win[:, :, bass.ds(h * P + (COL_B + m * DB), P)]).then_inc(S["w"], 16)
                    waits(h)(sp, "proj", 3)
                    self.pass_gate(sp)

            @block.gpsimd
            def _(pool):
                low = self.con("low").unsqueeze(1).to_broadcast([P, 4, P])
                lows = self.con("low_strict").unsqueeze(1).to_broadcast([P, 4, P])
                with pool.Fori(0, GH) as h:
                    W = waits(h)
                    for g in range(2):
                        W(pool, "ge", g + 1)
                        pool.tensor_tensor(es[:, 4 * g:4 * g + 4, :], e[:, 4 * g:4 * g + 4, :], lows, ALU.mult).then_inc(S["gm"], 1)
                        pool.tensor_tensor(ei[:, 4 * g:4 * g + 4, :], e[:, 4 * g:4 * g + 4, :], low, ALU.mult).then_inc(S["gm"], 1)

            @block.tensor
            def _(pe):
                pe.wait_ge(Z["w"], 160)
                for i in range(NT):
                    for kt in range(KT):
                        ins = pe.matmul(self.bank[i % 7][:], self.hT[:, kt, i * P:(i + 1) * P], wz[:, kt, :],
                                        start=kt == 0, stop=kt == KT - 1)
                        if i == 7 and kt == 0:
                            pass
                    ins.then_inc(Z["z"], 1)
                    for kt in range(KT):
                        ins = pe.matmul(self.bank[7][:, 8 * i:8 * i + 8], self.hT[:, kt, i * P:(i + 1) * P], wb[:, kt, :],
                                        start=kt == 0, stop=kt == KT - 1)
                    if i == 6:
                        pe.wait_ge(Z["zs"], 1)
                ins.then_inc(Z["ba"], 1)
                pe.wait_ge(Z["d"], 8)
                pe.wait_ge(Z["zs"], 8)
                gl = scal[:, :, 7, :]
                pe.matmul(self.bank[6][:, 0:32], self.con("upper"), gl, start=True, stop=True)
                pe.matmul(self.bank[6][:, 32:64], self.con("ones"), gl, start=True, stop=True).then_inc(Z["pe"], 1)
                pe.wait_ge(Z["d"], 14)
                with pe.Fori(0, GH) as h:
                    self.gdn_pe(pe, waits(h), S, locals() | dict(raw=raw, sq=sq, qn=qn, kn=kn, cv=cv, glb=glb, am=am, nn=nn, upd=upd,
                                tur=tur, ye=ye, vb=vb, kd=kd, kbg=kbg, wt=wt, st=st, vn=vn, at=at, og=og, wqkv=wqkv))

            @block.scalar
            def _(act):
                for i in range(NT):
                    act.wait_ge(Z["z"], i + 1)
                    act.activation(zs[:, :, i, :], self.bank[i % 7][:].rearrange("p (h v) -> p h v", h=GH), ACT.Silu).then_inc(Z["zs"], 1)
                act.wait_ge(Z["d"], 1)
                act.activation(scal[:, :, 4, :], ba[:, :, 0:4].rearrange("p i h -> p h i"), ACT.Sigmoid).then_inc(Z["a"], 1)
                act.wait_ge(Z["d"], 4)
                act.activation(sm[:, 2, :, :], sm[:, 1, :, :], ACT.Exp, scale=-1.0).then_inc(Z["a"], 1)
                act.activation(ev[:], ab[:, 0:4], ACT.Exp).then_inc(Z["a"], 1)
                act.wait_ge(Z["a"], 3)
                act.activation(sm[:, 3, :, :], sm[:, 2, :, :], ACT.Ln, bias=1.0).then_inc(Z["a"], 1)
                act.wait_ge(Z["d"], 11)
                act.activation(scal[:, :, 1, :], scal[:, :, 0, :], ACT.Exp).then_inc(Z["a"], 1)
                act.activation(scal[:, :, 6, :], sm[:, 4, :, :], ACT.Exp).then_inc(Z["a"], 1)
                act.activation(scal[:, :, 2, :], sm[:, 5, :, :], ACT.Exp).then_inc(Z["a"], 1)
                with act.Fori(0, GH) as h:
                    W = waits(h)
                    for b in range(6):
                        m, half = b // 2, b % 2
                        W(act, "proj", m + 1)
                        act.activation(raw[:, m, 3 + half * HALF:3 + (half + 1) * HALF], self.bank[b][:], ACT.Copy).then_inc(S["raw"], 1)
                    for m in (2, 0, 1):
                        W(act, "conv", 4 * (m + 1))
                        act.activation(cv[:, m, :], cv[:, m, :], ACT.Silu).then_inc(S["sil"], 1)
                    for m in range(2):
                        W(act, "sil", m + 2)
                        act.activation(sq[:, m, :], cv[:, m, :], ACT.Square).then_inc(S["sq"], 1)
                    for b in range(4):
                        W(act, "ss", b + 1)
                        act.activation(sq[:, b // 2, b % 2 * HALF:(b % 2 + 1) * HALF], self.bank[b][:], ACT.Ln, bias=EPS).then_inc(S["ln"], 1)
                    for m in range(2):
                        W(act, "ln", 2 * m + 2)
                        act.activation(sq[:, m, :], sq[:, m, :], ACT.Exp, scale=-0.5).then_inc(S["rs"], 1)
                    for g in range(2):
                        W(act, "gr", 4 * g + 4)
                        act.activation(flat(e, 4 * g, 4 * g + 4), flat(e, 4 * g, 4 * g + 4), ACT.Exp, scale=-1.0).then_inc(S["ge"], 1)
                    for g in range(2):
                        W(act, "at", g + 1)
                        act.activation(flat(at, 4 * g, 4 * g + 4), self.bank[6 + g][:], ACT.Copy).then_inc(S["ate"], 1)
                    self.invert_act(act, W, S, tur, ye, 6, True)
                    for g in range(2):
                        W(act, "u", g + 1)
                        act.activation(flat(u, 4 * g, 4 * g + 4), self.bank[2 + g][:], ACT.Copy).then_inc(S["ue"], 1)
                    W(act, "osq", 3)
                    act.activation(ssum[:, 1, :], ssum[:, 1, :], ACT.Ln).then_inc(S["ol"], 1)
                    W(act, "ol", 1)
                    act.activation(ssum[:, 2, :], ssum[:, 1, :], ACT.Exp, scale=-0.5).then_inc(S["ol"], 1)
                    for g in range(2):
                        W(act, "ot", g + 1)
                        act.activation(self.mixT[:, bass.ds(h + 2, 1), g * HALF:(g + 1) * HALF],
                                       self.bank[4 + g][:].unsqueeze(1), ACT.Copy, scale=self.parc("gdn_norm")).then_inc(S["mx"], 1)

            @block.vector
            def _(dve):
                zd = Step(dve, Z["d"])
                dve.wait_ge(Z["ba"], 1)
                zd(dve.tensor_copy(ba[:].rearrange("p i h -> p (i h)"), self.bank[7][:, 0:64]))
                dt = ab[:, 4:8].unsqueeze(2).to_broadcast([P, GH, NG])
                zd(dve.tensor_tensor(sm[:, 0, :, :], ba[:, :, 4:8].rearrange("p i h -> p h i"), dt, ALU.add))
                zd(dve.tensor_scalar(sm[:, 1, :, :], sm[:, 0, :, :], -1.0, None, ALU.mult))
                zd(dve.tensor_tensor(sm[:, 1, :, :], sm[:, 0, :, :], sm[:, 1, :, :], ALU.max))
                dve.wait_ge(Z["a"], 4)
                zd(dve.tensor_scalar(sm[:, 0, :, :], sm[:, 0, :, :], 0.0, None, ALU.max))
                zd(dve.tensor_tensor(sm[:, 0, :, :], sm[:, 0, :, :], sm[:, 3, :, :], ALU.add))
                zd(dve.tensor_tensor(sm[:, 0, :, :], sm[:, 0, :, :], ev[:].unsqueeze(2).to_broadcast([P, GH, NG]), ALU.mult))
                zd(dve.tensor_scalar(scal[:, :, 7, :], sm[:, 0, :, :], -1.0, None, ALU.mult))
                dve.wait_ge(Z["pe"], 1)
                v4 = lambda a: a.rearrange("p (h i) -> p h i", h=GH)
                zd(dve.tensor_copy(scal[:, :, 0, :], v4(self.bank[6][:, 0:32])))
                zd(dve.tensor_copy(sm[:, 4, :, :], v4(self.bank[6][:, 32:64])))
                zd(dve.tensor_tensor(sm[:, 5, :, :], sm[:, 4, :, :], scal[:, :, 0, :], ALU.subtract))
                dve.wait_ge(Z["a"], 7)
                zd(dve.tensor_tensor(scal[:, :, 3, :], scal[:, :, 4, :], scal[:, :, 1, :], ALU.mult))
                zd(dve.tensor_scalar(scal[:, :, 5, :], scal[:, :, 4, :], -1.0, None, ALU.mult))
                zd(dve.memset(st[:, 0, :], 0.0))
                with dve.Fori(0, GH) as h:
                    self.gdn_dve(dve, h, waits(h), S, dict(raw=raw, sq=sq, qn=qn, kn=kn, cv=cv, glb=glb, am=am, nn=nn, upd=upd,
                                 vb=vb, kd=kd, kbg=kbg, wt=wt, st=st, vn=vn, u=u, e=e, ei=ei, es=es, osb=osb, osq=osq, og=og,
                                 zs=zs, scal=scal, hs=hs, taps=taps, ssum=ssum))

    def gdn_pe(self, pe, W, S, t):
        bank = self.bank
        ident = self.con("ident")
        col = lambda q: slice(q * P, (q + 1) * P)
        W(pe, "w", 48)
        for m in range(3):
            for kt in range(KT):
                for half in range(2):
                    ins = pe.matmul(bank[2 * m + half][:], t["wqkv"][:, m, kt, :], self.hT[:, kt, half * HALF:(half + 1) * HALF],
                                    start=kt == 0, stop=kt == KT - 1)
            ins.then_inc(S["proj"], 1)
        W(pe, "raw", 6)
        W(pe, "hs", 3)
        for g in range(2):
            for q in range(4):
                ins = pe.matmul(bank[4 + g][:, col(q)], t["glb"][:, 4 * g + q, :], self.con("upper"), start=True, stop=True)
            ins.then_inc(S["gcr"], 1)
        W(pe, "sil", 1)
        for g in range(2):
            for q in range(4):
                ins = pe.transpose(bank[6 + g][:, col(q)], t["cv"][:, 2, (4 * g + q) * P:(4 * g + q + 1) * P], ident)
            ins.then_inc(S["trv"], 1)
        for b in range(4):
            W(pe, "sq", b // 2 + 1)
            pe.matmul(bank[b][:], self.con("ones"), t["sq"][:, b // 2, b % 2 * HALF:(b % 2 + 1) * HALF],
                      start=True, stop=True).then_inc(S["ss"], 1)
        W(pe, "qn", 2)
        for g in range(2):
            for q in range(4):
                ins = pe.transpose(bank[g][:, col(q)], t["kn"][:, 4 * g + q, :], ident)
            ins.then_inc(S["trk"], 1)
        for g in range(2):
            for q in range(4):
                k = t["kn"][:, 4 * g + q, :]
                ins = pe.matmul(bank[2 + g][:, col(q)], k, k, start=True, stop=True)
            ins.then_inc(S["kk"], 1)
        W(pe, "gr", 8)
        for g in range(2):
            for q in range(4):
                ins = pe.matmul(bank[4 + g][:, col(q)], t["qn"][:, 4 * g + q, :], t["kn"][:, 4 * g + q, :], start=True, stop=True)
            ins.then_inc(S["qk"], 1)
        W(pe, "kv", 2)
        for g in range(2):
            W(pe, "am", g + 1)
            for q in range(4):
                ins = pe.transpose(bank[6 + g][:, col(q)], t["am"][:, 4 * g + q, :], ident)
            ins.then_inc(S["at"], 1)
        W(pe, "kv", 6)
        self.invert_pe(pe, W, S, t["nn"], t["upd"], t["tur"], t["ye"], 6, True)
        for g in range(2):
            W(pe, "i_tur", 12 + g + 1)
            for q in range(4):
                ins = pe.matmul(bank[2 + g][:, col(q)], t["tur"][:, 4 * g + q, :], t["vb"][:, 4 * g + q, :], start=True, stop=True)
            ins.then_inc(S["u"], 1)
        for g in range(2):
            for q in range(4):
                ins = pe.matmul(bank[4 + g][:, col(q)], t["kbg"][:, 4 * g + q, :], t["tur"][:, 4 * g + q, :], start=True, stop=True)
            ins.then_inc(S["wt"], 1)
        W(pe, "ate", 2)
        for i in range(NG):
            W(pe, "wte", i // 4 + 1)
            W(pe, "st", i + 1)
            pe.matmul(bank[6][:, 0:P], t["wt"][:, i, :], t["st"][:, i, :], start=True, stop=True).then_inc(S["ws"], 1)
            W(pe, "vn", i + 1)
            pe.matmul(bank[7][:, 0:P], t["kd"][:, i, :], t["vn"][:, i, :], start=True, stop=True).then_inc(S["sk"], 1)
        for g in range(2):
            for q in range(4):
                ins = pe.matmul(bank[g][:, col(q)], t["qn"][:, 4 * g + q, :], t["st"][:, 4 * g + q, :], start=True, stop=True)
            ins.then_inc(S["qs"], 1)
            for q in range(4):
                ins = pe.matmul(bank[2 + g][:, col(q)], t["at"][:, 4 * g + q, :], t["vn"][:, 4 * g + q, :], start=True, stop=True)
            ins.then_inc(S["av"], 1)
        for g in range(2):
            W(pe, "og", 2)
            for q in range(4):
                ins = pe.transpose(bank[4 + g][:, col(q)], t["og"][:, 4 * g + q, :], ident)
            ins.then_inc(S["ot"], 1)
        W(pe, "mx", 2)

    def gdn_dve(self, dve, h, W, S, t):
        bank = self.bank
        four = lambda b: bank[b][:].rearrange("p (a b) -> p a b", a=4)
        grp = lambda a, g: a[:, 4 * g:4 * g + 4, :]
        hs, cv, raw = t["hs"], t["cv"], t["raw"]
        wide = lambda kind, g: hs[:, kind, 4 * g:4 * g + 4].unsqueeze(2).to_broadcast([P, 4, P])
        dve.tensor_copy(hs[:].rearrange("p a b -> p (a b)"), t["scal"][:, bass.ds(h, 1), :, :].rearrange("p o a b -> p (o a b)")).then_inc(S["hs"], 1)
        dve.tensor_copy(t["taps"][:], self.par[:, bass.ds(h * 12 + PAR["gdn_conv"], 12)]).then_inc(S["hs"], 1)
        W(dve, "hs", 2)
        dve.tensor_copy(t["glb"], hs[:, 7, :].unsqueeze(2).to_broadcast([P, NG, P])).then_inc(S["hs"], 1)
        dve.memset(raw[:, :, 0:3], 0.0).then_inc(S["pad"], 1)
        W(dve, "pad", 1)
        for m in range(3):
            W(dve, "raw", 2 * m + 2)
            dve.tensor_scalar(cv[:, m, :], raw[:, m, 3:3 + T], t["taps"][:, 4 * m + 3:4 * m + 4], None, ALU.mult).then_inc(S["conv"], 1)
            for k in (2, 1, 0):
                W(dve, "conv", 4 * m + 3 - k)
                dve.scalar_tensor_tensor(cv[:, m, :], raw[:, m, k:k + T], t["taps"][:, 4 * m + k:4 * m + k + 1], cv[:, m, :],
                                         ALU.mult, ALU.add).then_inc(S["conv"], 1)
        W(dve, "conv", 12)
        for i in range(NG):
            W(dve, "gcr", i // 4 + 1)
            dve.tensor_scalar(t["e"][:, i, :], bank[4 + i // 4][:, i % 4 * P:(i % 4 + 1) * P], hs[:, 0, i:i + 1], 0.0,
                              ALU.subtract, ALU.max).then_inc(S["gr"], 1)
        for g in range(2):
            W(dve, "trv", g + 1)
            dve.tensor_tensor(grp(t["vb"], g), four(6 + g), wide(4, g), ALU.mult).then_inc(S["kv"], 1)
        flat8 = lambda a: a.rearrange("p a b -> p (a b)")
        for m, dst, scale in ((0, t["qn"], float(P) ** -0.5), (1, t["kn"], 1.0)):
            W(dve, "rs", m + 1)
            dve.scalar_tensor_tensor(flat8(dst), cv[:, m, :], scale, t["sq"][:, m, :], ALU.mult, ALU.mult).then_inc(S["qn"], 1)
        W(dve, "qn", 2)
        for g in range(2):
            W(dve, "trk", g + 1)
            dve.tensor_tensor(grp(t["kd"], g), four(g), wide(2, g), ALU.mult).then_inc(S["kv"], 1)
            dve.tensor_tensor(grp(t["kbg"], g), four(g), wide(3, g), ALU.mult).then_inc(S["kv"], 1)
        dve.tensor_copy(t["upd"], self.con("ident").unsqueeze(1).to_broadcast([P, NG, P])).then_inc(S["i_init"], 1)
        for i in range(NG):
            W(dve, "kk", i // 4 + 1)
            W(dve, "gm", 2 * (i // 4) + 1)
            dve.scalar_tensor_tensor(t["nn"][:, i, :], bank[2 + i // 4][:, i % 4 * P:(i % 4 + 1) * P], hs[:, 5, i:i + 1],
                                     t["es"][:, i, :], ALU.mult, ALU.mult).then_inc(S["nn"], 1)
        for g in range(2):
            W(dve, "qk", g + 1)
            W(dve, "gm", 2 * g + 2)
            dve.tensor_tensor(grp(t["am"], g), four(4 + g), grp(t["ei"], g), ALU.mult).then_inc(S["am"], 1)
        W(dve, "i_init", 1)
        m0 = self.con("lev_low")[:, 0:P].bitcast(U32).unsqueeze(1).to_broadcast([P, 4, P])
        for g in range(2):
            W(dve, "nn", 4 * g + 4)
            self.pass_gate(dve)
            dve.copy_predicated(grp(t["upd"], g), m0, grp(t["nn"], g)).then_inc(S["i_upd"], 1)
        W(dve, "i_upd", 2)
        self.invert_dve(dve, W, S, t["upd"], "lev_low", 6)
        for g in range(2):
            W(dve, "wt", g + 1)
            dve.tensor_copy(t["wt"][:, 4 * g:4 * g + 4, :].rearrange("p a b -> p (a b)"), bank[4 + g][:]).then_inc(S["wte"], 1)
        dve.memset(t["st"][:, 0, :], 0.0).then_inc(S["st"], 1)
        W(dve, "ue", 2)
        for i in range(NG):
            W(dve, "ws", i + 1)
            dve.tensor_tensor(t["vn"][:, i, :], t["u"][:, i, :], bank[6][:, 0:P], ALU.subtract).then_inc(S["vn"], 1)
            W(dve, "st", i + 1)
            W(dve, "sk", i + 1)
            dve.scalar_tensor_tensor(t["st"][:, i + 1, :], t["st"][:, i, :], hs[:, 6, i:i + 1], bank[7][:, 0:P],
                                     ALU.mult, ALU.add).then_inc(S["st"], 1)
        for g in range(2):
            W(dve, "qs", g + 1)
            dve.tensor_tensor(grp(t["osb"], g), four(g), wide(1, g), ALU.mult).then_inc(S["t1"], 1)
            W(dve, "t1", g + 1)
            W(dve, "av", g + 1)
            dve.tensor_tensor(grp(t["osb"], g), grp(t["osb"], g), four(2 + g), ALU.add).then_inc(S["o"], 1)
        W(dve, "o", 2)
        dve.tensor_tensor(t["osq"], t["osb"], t["osb"], ALU.mult).then_inc(S["osq"], 1)
        W(dve, "osq", 1)
        dve.tensor_reduce(t["ssum"][:, 0, :], t["osq"], AX, ALU.add).then_inc(S["osq"], 1)
        W(dve, "osq", 2)
        dve.tensor_scalar(t["ssum"][:, 1, :], t["ssum"][:, 0, :], 1.0 / P, EPS, ALU.mult, ALU.add).then_inc(S["osq"], 1)
        W(dve, "ol", 2)
        dve.tensor_tensor(t["og"], t["osb"], t["ssum"][:, 2, :].unsqueeze(2).to_broadcast([P, NG, P]), ALU.mult).then_inc(S["og"], 1)
        W(dve, "og", 1)
        zh = t["zs"][:, bass.ds(h, 1), :, :].rearrange("p o i v -> p (o i) v")
        dve.tensor_tensor(t["og"], t["og"], zh, ALU.mult).then_inc(S["og"], 1)
        W(dve, "mx", 2)

    def rwkv_stage(self):
        nc = self.nc
        K = dict(proj=3, raw=3, lo=3, sg=3, pp=1, car=2, xs=4, sq=1, ss=1, ln=1, rs=1, cs=1, ex=2, px=4, kp=5, rk=1, bs=1,
                 bon=1, bd=14, tr=6, tok=4, tokv=2, sc=8, am=8, i_init=1, i_turn=10, i_tur=10, i_y=10, i_ye=10, i_w=10, i_upd=12,
                 m0=1, c1=8, rh=8, c2=8, u=8, c3=8, st=8, ot=2, o=2, m1=1, oc=1, osq=1, m2=1, vl=1, vr=1, y=2, mx=1)
        with ExitStack() as c:
            f = lambda n, shape: self.sb(c, "rwkv_" + n, [P] + shape)
            H = HALF
            NCH = H // CR
            w, lw, lot = f("w", [3, KT, P]), f("lora_w", [3, P]), f("lo", [T])
            raw, xs, pp, car = f("raw", [3, 1 + H]), f("xs", [3, H]), f("par", [10]), f("carry", [3])
            sg, a, gs, rs, cs, ex, te = (f(n, [H]) for n in ("sg", "a", "g", "rs", "cs", "ex", "te"))
            pt, pin, pm, pe_ = (f(n, [H]) for n in ("pt", "pin", "pm", "pend"))
            kk, k2, b, bon, rm = (f(n, [H]) for n in ("kk", "k2", "b", "bonus", "reset"))
            kr = f("kap_r", [NCH, 2, P])
            ki, ni, vb, kh, nh = (f(n, [NCH, P]) for n in ("ki", "ni", "vbd", "kh", "nh"))
            vt, kht, nht = (f(n, [NCH, P]) for n in ("vt", "kht", "nht"))
            ak, an = f("ak", [NCH, 2, P]), f("an", [NCH, 2, P])
            upd, tur, ye, us = f("upd", [NCH, P]), kh, nh, vb
            wlo = upd
            lraw = kr[:].rearrange("p a b c -> p (a b c)")[:, 0:1 + T]
            rhs = f("rhs", [2, P])
            st = f("state", [NCH + 1, P])
            o, oc, osq = sg, ex, te
            S = {n: self.sem(c, "rwkv_" + n) for n in K}
            Z = {n: self.sem(c, "rwkvz_" + n) for n in ("w", "wl", "lz", "init", "lp", "lr", "ld", "lt")}
            block = c.enter_context(nc.Block())
            win = self.i["w_in"].rearrange("(kt p) c -> p kt c", p=P)
            bank = self.bank
            col = lambda q: slice(q * P, (q + 1) * P)

            def loops(eng, body):
                with eng.Fori(0, 2) as p:
                    with eng.Fori(0, 2) as hf:
                        body(p, hf, lambda e, name, n: e.wait_ge(S[name], (p * 2 + hf) * K[name] + n))

            @block.sync
            def _(sp):
                sp.dma_start(wlo[:], win[:, :, 3 * DA:3 * DA + P]).then_inc(Z["wl"], 16)
                sp.wait_ge(Z["lz"], 1)
                with sp.Fori(0, 2) as p:
                    for m in range(3):
                        sp.dma_start(w[:, m, :, :], win[:, :, bass.ds(p * P + m * DA, P)]).then_inc(Z["w"], 16)
                    for m, (name, r0, r1) in enumerate((("rwkv_w2", 0, 32), ("rwkv_a2", 32, 64), ("rwkv_g2", 64, 128))):
                        sp.dma_start(lw[r0:r1, m, :], self.i[name][:, bass.ds(p * P, P)]).then_inc(Z["w"], 16)
                    sp.wait_ge(S["lo"], p * 6 + 6)
                    self.pass_gate(sp)

            @block.gpsimd
            def _(pool):
                pool.memset(lw[:], 0.0).then_inc(Z["lz"], 1)
                pool.memset(lraw[:, 0:1], 0.0).then_inc(Z["init"], 1)
                pool.memset(rm[:], 1.0).then_inc(Z["init"], 1)
                pool.wait_ge(Z["init"], 2)
                pool.memset(rm[:].rearrange("p (c t) -> p c t", t=CR)[:, :, 0:1], 0.0).then_inc(Z["init"], 1)
                pool.memset(car[:], 0.0).then_inc(Z["init"], 1)
                pool.memset(st[:, NCH, :], 0.0).then_inc(Z["init"], 1)

            @block.tensor
            def _(pe):
                pe.wait_ge(Z["wl"], 16)
                for kt in range(KT):
                    for half in range(2):
                        ins = pe.matmul(bank[6 + half][:], wlo[:, kt, :], self.hT[:, kt, half * H:(half + 1) * H],
                                        start=kt == 0, stop=kt == KT - 1)
                ins.then_inc(Z["lp"], 1)
                pe.wait_ge(Z["lt"], 2)

                def body(p, hf, W):
                    pe.wait_ge(Z["w"], p * 96 + 96)
                    tok = bass.ds(hf * H, H)
                    for m in range(3):
                        for kt in range(KT):
                            ins = pe.matmul(bank[m][:], w[:, m, kt, :], self.hT[:, kt, tok], start=kt == 0, stop=kt == KT - 1)
                        ins.then_inc(S["proj"], 1)
                    for m in range(3):
                        pe.matmul(bank[3 + m][:], lw[:, m, :], lot[:, tok], start=True, stop=True).then_inc(S["lo"], 1)
                    W(pe, "sq", 1)
                    pe.matmul(bank[6][:], self.con("ones64"), rs[:], start=True, stop=True).then_inc(S["ss"], 1)
                    W(pe, "rk", 1)
                    pe.matmul(bank[7][:], self.con("ones64"), b[:], start=True, stop=True).then_inc(S["bs"], 1)
                    W(pe, "bd", 14)
                    W(pe, "raw", 3)
                    W(pe, "sg", 3)
                    for n, src in enumerate((vb, kh, nh)):
                        for g in range(2):
                            for q in range(4):
                                ins = pe.transpose(bank[2 * n + g][:, col(q)], src[:, 4 * g + q, :], self.con("ident"))
                            ins.then_inc(S["tr"], 1)
                    W(pe, "bon", 1)
                    W(pe, "ln", 1)
                    for n, src in enumerate((ki, ni)):
                        for g in range(4):
                            bk = (6, 7, 0, 1, 2, 3, 4, 5)[4 * n + g]
                            if bk < 6:
                                W(pe, "tokv", bk + 1) if bk < 2 else W(pe, "tok", bk - 1)
                            for q in range(2):
                                i = 2 * g + q
                                ins = pe.matmul(bank[bk][:, q * 256:(q + 1) * 256], src[:, i, :],
                                                kr[:, i, :, :].rearrange("p a b -> p (a b)"), start=True, stop=True)
                            ins.then_inc(S["sc"], 1)
                    W(pe, "am", 8)
                    self.invert_pe(pe, W, S, an[:, :, 0, :], upd, tur, ye, 5, False)
                    W(pe, "i_upd", 12)
                    W(pe, "m0", 1)
                    for i in range(NCH):
                        if i:
                            W(pe, "st", i)
                        pe.matmul(bank[6][:, 0:P], ak[:, i, 0, :], vt[:, i, :], start=True, stop=False)
                        pe.matmul(bank[6][:, 0:P], kr[:, i, 0, :], st[:, i, :], start=False, stop=True).then_inc(S["c1"], 1)
                        W(pe, "rh", i + 1)
                        pe.matmul(bank[7][:, 0:P], upd[:, i, :], rhs[:, i % 2, :], start=True, stop=True).then_inc(S["c2"], 1)
                        pe.matmul(bank[0][:, 0:P], kht[:, i, :], vt[:, i, :], start=True, stop=False)
                        W(pe, "u", i + 1)
                        pe.matmul(bank[0][:, 0:P], nht[:, i, :], us[:, i, :], start=False, stop=True).then_inc(S["c3"], 1)
                    for g in range(2):
                        for q in range(4):
                            i = 4 * g + q
                            pe.matmul(bank[1 + g][:, col(q)], st[:, i, :], kr[:, i, 1, :], start=True, stop=False)
                            pe.matmul(bank[1 + g][:, col(q)], vt[:, i, :], ak[:, i, 1, :], start=False, stop=False)
                            ins = pe.matmul(bank[1 + g][:, col(q)], us[:, i, :], an[:, i, 1, :], start=False, stop=True)
                        ins.then_inc(S["ot"], 1)
                    W(pe, "o", 2)
                    pe.matmul(bank[3][:], self.con("ones64"), o[:], start=True, stop=True).then_inc(S["m1"], 1)
                    W(pe, "osq", 1)
                    pe.matmul(bank[4][:], self.con("ones64"), osq[:], start=True, stop=True).then_inc(S["m2"], 1)
                    W(pe, "mx", 1)

                loops(pe, body)

            @block.scalar
            def _(act):
                act.wait_ge(Z["lp"], 1)
                for half in range(2):
                    act.activation(lraw[:, 1 + half * H:1 + (half + 1) * H], bank[6 + half][:], ACT.Copy).then_inc(Z["lr"], 1)
                act.wait_ge(Z["ld"], 2)
                act.activation(lot[0:32, :], lot[0:32, :], ACT.Tanh).then_inc(Z["lt"], 1)
                act.activation(lot[64:128, :], lot[64:128, :], ACT.Sigmoid).then_inc(Z["lt"], 1)

                def body(p, hf, W):
                    for m in range(3):
                        W(act, "proj", m + 1)
                        act.activation(raw[:, m, 1:1 + H], bank[m][:], ACT.Copy).then_inc(S["raw"], 1)
                    W(act, "pp", 1)
                    for m, dst in enumerate((sg, a)):
                        W(act, "lo", m + 1)
                        act.activation(dst[:], bank[3 + m][:], ACT.Sigmoid, bias=pp[:, 3 + m:4 + m]).then_inc(S["sg"], 1)
                    W(act, "lo", 3)
                    act.activation(gs[:], bank[5][:], ACT.Copy).then_inc(S["sg"], 1)
                    W(act, "xs", 4)
                    act.activation(rs[:], xs[:, 1, :], ACT.Square, scale=pp[:, 5:6]).then_inc(S["sq"], 1)
                    W(act, "ss", 1)
                    act.activation(rs[:], bank[6][:], ACT.Ln, bias=EPS).then_inc(S["ln"], 1)
                    W(act, "ln", 1)
                    act.activation(rs[:], rs[:], ACT.Exp, scale=-0.5).then_inc(S["rs"], 1)
                    W(act, "ex", 2)
                    act.activation(pt[:], cs[:], ACT.Exp, scale=-EM05).then_inc(S["px"], 1)
                    act.activation(pin[:], cs[:], ACT.Exp, scale=EM05).then_inc(S["px"], 1)
                    act.activation(pm[:], ex[:], ACT.Exp, scale=-EM05).then_inc(S["px"], 1)
                    act.activation(pe_[:], te[:], ACT.Exp, scale=-EM05).then_inc(S["px"], 1)
                    for n, dst in ((1, kht), (2, nht)):
                        for g in range(2):
                            W(act, "tr", 2 * n + g + 1)
                            act.activation(dst[:, 4 * g:4 * g + 4, :].rearrange("p a b -> p (a b)"), bank[2 * n + g][:],
                                           ACT.Copy).then_inc(S["tok"], 1)
                    self.invert_act(act, W, S, tur, ye, 5, False)
                    for i in range(NCH):
                        W(act, "c1", i + 1)
                        act.activation(rhs[:, i % 2, :], bank[6][:, 0:P], ACT.Copy).then_inc(S["rh"], 1)
                        W(act, "c2", i + 1)
                        act.activation(us[:, i, :], bank[7][:, 0:P], ACT.Copy).then_inc(S["u"], 1)
                    W(act, "m2", 1)
                    act.activation(cs[:], bank[4][:], ACT.Ln, scale=1.0 / CR, bias=GN_EPS).then_inc(S["vl"], 1)
                    W(act, "vl", 1)
                    act.activation(cs[:], cs[:], ACT.Exp, scale=-0.5).then_inc(S["vr"], 1)

                loops(act, body)

            @block.vector
            def _(dve):
                dve.wait_ge(Z["init"], 5)
                dve.wait_ge(Z["lr"], 2)
                dve.tensor_tensor(lot[:], lraw[:, 0:T], lraw[:, 1:1 + T], ALU.subtract).then_inc(Z["ld"], 1)
                dve.wait_ge(Z["ld"], 1)
                dve.scalar_tensor_tensor(lot[:], lot[:], self.parc("mu_lo"), lraw[:, 1:1 + T], ALU.mult, ALU.add).then_inc(Z["ld"], 1)
                dve.wait_ge(Z["lt"], 2)

                def body(p, hf, W):
                    dve.tensor_copy(pp[:], self.par[:, bass.ds(p * 10 + PAR["rwkv"], 10)]).then_inc(S["pp"], 1)
                    keep = self.cons[:, bass.ds(hf + CON["keep"][0], 1)]
                    dve.tensor_tensor(raw[:, :, 0], car[:], keep.to_broadcast([P, 3]), ALU.mult).then_inc(S["car"], 1)
                    dve.tensor_tensor(st[:, 0, :], st[:, NCH, :], keep.to_broadcast([P, P]), ALU.mult).then_inc(S["m0"], 1)
                    W(dve, "raw", 3)
                    W(dve, "car", 1)
                    W(dve, "pp", 1)
                    dve.tensor_tensor(xs[:], raw[:, :, 0:H], raw[:, :, 1:1 + H], ALU.subtract).then_inc(S["xs"], 1)
                    dve.tensor_copy(car[:], raw[:, :, H]).then_inc(S["car"], 1)
                    W(dve, "xs", 1)
                    for m in range(3):
                        dve.scalar_tensor_tensor(xs[:, m, :], xs[:, m, :], pp[:, m:m + 1], raw[:, m, 1:1 + H],
                                                 ALU.mult, ALU.add).then_inc(S["xs"], 1)
                    W(dve, "sg", 2)
                    dve.tensor_tensor_scan(cs[:], rm[:], sg[:], 0.0, ALU.mult, ALU.add).then_inc(S["cs"], 1)
                    W(dve, "xs", 4)
                    dve.tensor_scalar(k2[:], a[:], -1.0, pp[:, 6:7], ALU.add, ALU.mult).then_inc(S["kp"], 1)
                    dve.tensor_scalar(kk[:], xs[:, 1, :], pp[:, 5:6], None, ALU.mult).then_inc(S["kp"], 1)
                    W(dve, "cs", 1)
                    dve.tensor_tensor(ex[:], cs[:], sg[:], ALU.subtract).then_inc(S["ex"], 1)
                    c3 = cs[:].rearrange("p (c t) -> p c t", t=CR)
                    dve.tensor_tensor(te[:].rearrange("p (c t) -> p c t", t=CR), c3[:, :, CR - 1:CR].to_broadcast([P, NCH, CR]),
                                      c3, ALU.subtract).then_inc(S["ex"], 1)
                    W(dve, "kp", 2)
                    dve.scalar_tensor_tensor(k2[:], k2[:], 1.0, xs[:, 1, :], ALU.add, ALU.mult).then_inc(S["kp"], 1)
                    W(dve, "kp", 3)
                    dve.scalar_tensor_tensor(b[:], xs[:, 0, :], pp[:, 7:8], k2[:], ALU.mult, ALU.mult).then_inc(S["rk"], 1)
                    W(dve, "rs", 1)
                    dve.tensor_tensor(kk[:], kk[:], rs[:], ALU.mult).then_inc(S["kp"], 1)
                    W(dve, "bs", 1)
                    dve.tensor_tensor(bon[:], bank[7][:], xs[:, 2, :], ALU.mult).then_inc(S["bon"], 1)
                    W(dve, "kp", 4)
                    dve.tensor_tensor(b[:], kk[:], a[:], ALU.mult).then_inc(S["kp"], 1)
                    W(dve, "kp", 5)
                    W(dve, "px", 4)
                    ch = lambda x: x.rearrange("p (c t) -> p c t", t=CR)
                    for g in range(2):
                        plus = self.con("half")[:, g:g + 1]
                        minus = self.con("nhalf")[:, g:g + 1]
                        hcol = slice(g * CR, (g + 1) * CR)
                        for dst, src, sign, dec in ((kr[:, :, 0, hcol], kk[:], plus, pm), (kr[:, :, 1, hcol], xs[:, 0, :], plus, pt),
                                                    (ki[:, :, hcol], k2[:], plus, pin), (ni[:, :, hcol], b[:], minus, pin),
                                                    (kh[:, :, hcol], k2[:], plus, pe_), (nh[:, :, hcol], b[:], minus, pe_)):
                            dve.scalar_tensor_tensor(dst, ch(src), sign, ch(dec[:]), ALU.mult, ALU.mult).then_inc(S["bd"], 1)
                        dve.tensor_scalar(vb[:, :, hcol], ch(xs[:, 2, :]), plus, None, ALU.mult).then_inc(S["bd"], 1)
                    dve.tensor_copy(upd[:], self.con("ident").unsqueeze(1).to_broadcast([P, NCH, P])).then_inc(S["i_init"], 1)
                    for g in range(2):
                        W(dve, "tr", g + 1)
                        dve.tensor_copy(vt[:, 4 * g:4 * g + 4, :].rearrange("p a b -> p (a b)"), bank[g][:]).then_inc(S["tokv"], 1)
                    a0 = CON["up64_strict"][0]
                    mask = self.cons[:, a0:a0 + 2 * P].unsqueeze(1).to_broadcast([P, 2, 2 * P])
                    for n, dst in enumerate((ak, an)):
                        for g in range(4):
                            bk = (6, 7, 0, 1, 2, 3, 4, 5)[4 * n + g]
                            W(dve, "sc", 4 * n + g + 1)
                            dve.tensor_tensor(dst[:, 2 * g:2 * g + 2, :, :].rearrange("p a b c -> p a (b c)"),
                                              bank[bk][:].rearrange("p (a b) -> p a b", a=2), mask, ALU.mult).then_inc(S["am"], 1)
                    W(dve, "am", 8)
                    W(dve, "i_init", 1)
                    m0 = self.con("lev_up")[:, 0:P].bitcast(U32).unsqueeze(1).to_broadcast([P, 4, P])
                    for g in range(2):
                        self.pass_gate(dve)
                        dve.copy_predicated(upd[:, 4 * g:4 * g + 4, :], m0, an[:, 4 * g:4 * g + 4, 0, :]).then_inc(S["i_upd"], 1)
                    W(dve, "i_upd", 2)
                    self.invert_dve(dve, W, S, upd, "lev_up", 5)
                    for i in range(NCH):
                        W(dve, "c3", i + 1)
                        W(dve, "st", i) if i else W(dve, "m0", 1)
                        dve.scalar_tensor_tensor(st[:, i + 1, :], st[:, i, :], pt[:, i * CR + CR - 1:i * CR + CR], bank[0][:, 0:P],
                                                 ALU.mult, ALU.add).then_inc(S["st"], 1)
                    for g in range(2):
                        W(dve, "ot", g + 1)
                        dve.tensor_reduce(o[:, g * 256:(g + 1) * 256].rearrange("p (c t) -> p c t", t=CR),
                                          bank[1 + g][:].rearrange("p (c g t) -> p c t g", g=2, t=CR), AX, ALU.add).then_inc(S["o"], 1)
                    W(dve, "m1", 1)
                    dve.scalar_tensor_tensor(oc[:], bank[3][:], -1.0 / CR, o[:], ALU.mult, ALU.add).then_inc(S["oc"], 1)
                    W(dve, "oc", 1)
                    dve.tensor_tensor(osq[:], oc[:], oc[:], ALU.mult).then_inc(S["osq"], 1)
                    W(dve, "vr", 1)
                    dve.scalar_tensor_tensor(oc[:], oc[:], pp[:, 8:9], cs[:], ALU.mult, ALU.mult).then_inc(S["y"], 1)
                    W(dve, "y", 1)
                    dve.scalar_tensor_tensor(oc[:], oc[:], pp[:, 9:10], bon[:], ALU.add, ALU.add).then_inc(S["y"], 1)
                    W(dve, "y", 2)
                    dve.tensor_tensor(self.mixT[:, bass.ds(p, 1), bass.ds(hf * H, H)], oc[:].unsqueeze(1), gs[:].unsqueeze(1),
                                      ALU.mult).then_inc(S["mx"], 1)

                loops(dve, body)

    def route_stage(self):
        nc = self.nc
        with ExitStack() as c:
            f = lambda n, shape, dt=F32: self.sb(c, "rt_" + n, [P] + shape, dt)
            wo = f("w_out", [KT, D])
            x2 = self.x2
            h2 = f("h2", [2, D])
            h2t = f("h2t", [2, KT, P])
            sq = f("sq", [D])
            gain = f("gain", [D])
            wr = f("w_router", [KT, 36])
            mb = f("bias", [36])
            ss, rs = f("ss", [NT]), f("rs", [NT])
            lg = f("logits", [NT, 36])
            S = {n: self.sem(c, "rt_" + n) for n in (
                "w", "x", "small", "prod", "x2", "ss", "ms", "rc", "rt", "h2", "turn", "turned", "log", "lg",
                "step", "ex", "cum", "oh", "slot", "gd", "vd")}
            ST = [self.sem(c, f"rt_stored{j}") for j in range(2)]
            sm = f("small", [24, NT])
            g4 = f("g4", [4, NT, 4])
            me = f("masked", [NT, 4, 8])
            el = f("el", [NT, 8])
            top = f("top", [NT, 8])
            topi = f("topi", [NT, 8], U32)
            eid = f("eid", [NT, 2])
            oh = f("onehot", [NT, 2, E])
            ohs = f("onehots", [NT, E])
            run = f("run", [NT + 1, E])
            rank = f("rank", [NT, E])
            tmp = f("tmp", [NT, 2, E])
            ov = f("ov", [8, E])
            cmp7 = f("cmp7", [E, 7])
            cmpb = f("cmpb", [NOV, E])
            dst = f("dst", [NT * 2])
            dsti = f("dsti", [NT * 2], U32)
            blki = f("blki", [NT * 2], U32)
            sloti = f("sloti", [NT * 2], U32)
            blkf, slotf, val = f("blkf", [NT * 2]), f("slotf", [NT * 2]), f("val", [NT * 2])
            rr = f("slot_onehot", [4, P])
            bt = f("blk_onehot", [4, NBLK])
            vs = f("vs", [2, NBLK])
            bef = f("bef", [NOV + 1])
            block = c.enter_context(nc.Block())
            bank = self.bank
            xv = self.i["x"].rearrange("(i p) d -> p i d", p=P)

            @block.sync
            def _(sp):
                wv = self.i["w_out"].rearrange("(kt p) n -> p kt n", p=P)
                for q in range(4):
                    sp.dma_start(wo[:, 2 * q:2 * q + 2, :], wv[:, 2 * q:2 * q + 2, :]).then_inc(S["w"], 16)
                for q in range(2):
                    sp.dma_start(x2[:, 4 * q:4 * q + 4, :], xv[:, 4 * q:4 * q + 4, :]).then_inc(S["x"], 16)
                sp.dma_start(gain[:], self.i["norm_ffn_row"].partition_broadcast(P)).then_inc(S["small"], 16)
                sp.dma_start(mb[:], self.i["moe_b"].partition_broadcast(P)).then_inc(S["small"], 16)
                sp.dma_start(wr[:, :, 0:4], self.i["moe_w_group"].rearrange("(kt p) n -> p kt n", p=P)).then_inc(S["small"], 16)
                sp.dma_start(wr[:, :, 4:36], self.i["moe_w_expert"].rearrange("(kt p) n -> p kt n", p=P)).then_inc(S["small"], 16)
                for i in range(NT):
                    sp.wait_ge(S["h2"], i + 1)
                    sp.dma_start(self.h2d[i * P:(i + 1) * P, :], h2[:, i % 2, :]).then_inc(ST[i % 2], 16)
                for j in range(2):
                    sp.wait_ge(ST[j], 16 * (NT // 2))

            @block.tensor
            def _(pe):
                pe.wait_ge(S["w"], 64)

                def turn(i):
                    pe.wait_ge(S["h2"], i + 1)
                    if i:
                        pe.wait_ge(S["turned"], 2 * i)
                    for kt in range(KT):
                        ins = pe.transpose(bank[4 + kt // 4][:, kt % 4 * P:(kt % 4 + 1) * P], h2[:, i % 2, kt * P:(kt + 1) * P],
                                           self.con("ident"))
                        if kt % 4 == 3:
                            ins.then_inc(S["turn"], 1)

                def logits(i):
                    pe.wait_ge(S["small"], 64)
                    pe.wait_ge(S["turned"], 2 * i + 2)
                    if i >= 2:
                        pe.wait_ge(S["lg"], i - 1)
                    for kt in range(KT):
                        ins = pe.matmul(bank[6 + i % 2][:, 0:36], h2t[:, i % 2, kt, :], wr[:, kt, :], start=kt == 0, stop=kt == KT - 1)
                    ins.then_inc(S["log"], 1)

                for i in range(NT + 3):
                    if i < NT:
                        for kt in range(KT):
                            for half in range(2):
                                if kt == 0 and i >= 2:
                                    pe.wait_ge(S["x2"], 2 * (i - 2) + half + 1)
                                ins = pe.matmul(bank[2 * (i % 2) + half][:], self.mixT[:, kt, i * P:(i + 1) * P],
                                                wo[:, kt, half * HALF:(half + 1) * HALF], start=kt == 0, stop=kt == KT - 1)
                        ins.then_inc(S["prod"], 1)
                    if 2 <= i < NT + 2:
                        turn(i - 2)
                    if i >= 3:
                        logits(i - 3)
                pe.wait_ge(S["oh"], 1)
                o = ohs[:].rearrange("p i e -> p (i e)")
                pe.matmul(bank[0][:, 0:NT * E], self.con("below"), o, start=True, stop=True)
                pe.matmul(bank[1][:, 0:NT * E], self.con("ones"), o, start=True, stop=True).then_inc(S["cum"], 1)
                for n in range(2 * NT):
                    pe.wait_ge(S["slot"], 2 * n + 2)
                    pe.matmul(bank[2][:, 0:NBLK], rr[:, n % 4, :], bt[:, n % 4, :], start=n == 0, stop=n == 2 * NT - 1).then_inc(S["cum"], 1)

            @block.scalar
            def _(act):
                for i in range(NT + 1):
                    if i < NT:
                        act.wait_ge(S["x2"], 2 * i + 2)
                        if i:
                            act.wait_ge(S["ss"], i)
                        act.activation(sq[:], x2[:, i, :], ACT.Square, accum_out=ss[:, i:i + 1]).then_inc(S["ss"], 1)
                        act.wait_ge(S["rc"], i + 1)
                        act.activation(rs[:, i:i + 1], rs[:, i:i + 1], ACT.Sqrt).then_inc(S["rt"], 1)
                    if i >= 1:
                        for b in range(2):
                            act.wait_ge(S["turn"], 2 * (i - 1) + b + 1)
                            if i >= 3:
                                act.wait_ge(S["log"], i - 2)
                            act.activation(h2t[:, (i - 1) % 2, 4 * b:4 * b + 4, :].rearrange("p a b -> p (a b)"), bank[4 + b][:],
                                           ACT.Copy).then_inc(S["turned"], 1)
                act.wait_ge(S["gd"], 1)
                act.activation(g4[:, 3, :, :], g4[:, 3, :, :], ACT.Exp).then_inc(S["ex"], 1)
                act.wait_ge(S["vd"], 1)
                act.activation(sm[:, 6, :], sm[:, 5, :], ACT.Exp).then_inc(S["ex"], 1)

            @block.vector
            def _(dve):
                dve.wait_ge(S["x"], 32)
                dve.wait_ge(S["small"], 64)

                def logits_out(i):
                    dve.wait_ge(S["log"], i + 1)
                    dve.tensor_tensor(lg[:, i, :], bank[6 + i % 2][:, 0:36], mb[:], ALU.add).then_inc(S["lg"], 1)

                for i in range(NT):
                    dve.wait_ge(S["prod"], i + 1)
                    for half in range(2):
                        xs = x2[:, i, half * HALF:(half + 1) * HALF]
                        dve.tensor_tensor(xs, bank[2 * (i % 2) + half][:], xs, ALU.add).then_inc(S["x2"], 1)
                    dve.wait_ge(S["ss"], i + 1)
                    dve.tensor_scalar(rs[:, i:i + 1], ss[:, i:i + 1], 1.0 / D, EPS, ALU.mult, ALU.add).then_inc(S["ms"], 1)
                    dve.wait_ge(S["ms"], i + 1)
                    dve.reciprocal(rs[:, i:i + 1], rs[:, i:i + 1]).then_inc(S["rc"], 1)
                    dve.wait_ge(S["rt"], i + 1)
                    if i >= 2:
                        dve.wait_ge(S["turn"], 2 * (i - 2) + 2)
                        dve.wait_ge(ST[i % 2], 16 * (i // 2))
                    dve.scalar_tensor_tensor(h2[:, i % 2, :], x2[:, i, :], rs[:, i:i + 1], gain[:], ALU.mult, ALU.mult).then_inc(S["h2"], 1)
                    if i >= 3:
                        logits_out(i - 3)
                for i in range(NT - 3, NT):
                    logits_out(i)
                dve.wait_ge(S["lg"], NT)
                step = Step(dve, S["step"])
                b4 = lambda a: a.unsqueeze(2).to_broadcast([P, NT, 4])
                grp = lg[:, :, 0:4]
                step(dve.tensor_reduce(sm[:, 0, :], grp, AX, ALU.max))
                dve.tensor_tensor(g4[:, 3, :, :], grp, b4(sm[:, 0, :]), ALU.subtract).then_inc(S["gd"], 1)
                step(dve.tensor_tensor(g4[:, 0, :, :], grp, b4(sm[:, 0, :]), ALU.is_equal))
                step(dve.tensor_tensor(g4[:, 1, :, :], g4[:, 0, :, :], self.con("idx4").unsqueeze(1).to_broadcast([P, NT, 4]), ALU.mult))
                step(dve.tensor_reduce(sm[:, 1, :], g4[:, 1, :, :], AX, ALU.max))
                step(dve.tensor_tensor(g4[:, 2, :, :], g4[:, 1, :, :], b4(sm[:, 1, :]), ALU.is_equal))
                step(dve.tensor_scalar(sm[:, 2, :], sm[:, 1, :], -8.0, 32.0, ALU.mult, ALU.add))
                step(dve.tensor_tensor(me[:], lg[:, :, 4:36].rearrange("p i (g e) -> p i g e", g=4),
                                       g4[:, 2, :, :].unsqueeze(3).to_broadcast([P, NT, 4, 8]), ALU.mult))
                step(dve.tensor_reduce(el[:], me[:].rearrange("p i g e -> p i e g"), AX, ALU.add))
                for i in range(NT):
                    step.inc(dve.max(top[:, i, :], el[:, i, :]))
                step.wait()
                dve.tensor_tensor(sm[:, 5, :], top[:, :, 1], top[:, :, 0], ALU.subtract).then_inc(S["vd"], 1)
                for i in range(NT):
                    step.inc(dve.max_index(topi[:, i, :], top[:, i, :], el[:, i, :]))
                step.wait()
                step(dve.tensor_copy(eid[:], topi[:, :, 0:2]))
                step(dve.tensor_tensor(eid[:], eid[:], sm[:, 2, :].unsqueeze(2).to_broadcast([P, NT, 2]), ALU.add))
                step(dve.tensor_tensor(oh[:].rearrange("p i k e -> p (i k) e"), self.con("iota_e").unsqueeze(1).to_broadcast([P, 2 * NT, E]),
                                       eid[:].rearrange("p i k -> p (i k)").unsqueeze(2).to_broadcast([P, 2 * NT, E]), ALU.is_equal))
                dve.tensor_tensor(ohs[:], oh[:, :, 0, :], oh[:, :, 1, :], ALU.add).then_inc(S["oh"], 1)
                dve.wait_ge(S["ex"], 2)
                step(dve.tensor_reduce(sm[:, 7, :], g4[:, 3, :, :], AX, ALU.add))
                step(dve.tensor_scalar(sm[:, 8, :], sm[:, 6, :], 1.0, None, ALU.add))
                step(dve.tensor_tensor(sm[:, 8, :], sm[:, 8, :], sm[:, 7, :], ALU.mult))
                step(dve.reciprocal(self.gates12[:, 0, :], sm[:, 8, :]))
                step(dve.tensor_tensor(self.gates12[:, 1, :], self.gates12[:, 0, :], sm[:, 6, :], ALU.mult))
                dve.wait_ge(S["cum"], 1)
                step(dve.memset(run[:, 0, :], 0.0))
                for i in range(NT):
                    step(dve.tensor_tensor(run[:, i + 1, :], run[:, i, :], bank[1][:, i * E:(i + 1) * E], ALU.add))
                step(dve.tensor_tensor(rank[:], run[:, 0:NT, :], bank[0][:, 0:NT * E].rearrange("p (i e) -> p i e", e=E), ALU.add))
                cnt = run[:, NT, :]
                step(dve.tensor_tensor(cmp7[:], cnt.unsqueeze(2).to_broadcast([P, E, 7]), self.con("j128").unsqueeze(1).to_broadcast([P, E, 7]),
                                       ALU.is_gt))
                step(dve.tensor_reduce(ov[:, 0, :], cmp7[:], AX, ALU.add))
                step(dve.tensor_tensor_scan(ov[:, 1, :], self.con("ones")[:, 0:E], ov[:, 0, :], 0.0, ALU.mult, ALU.add))
                step(dve.tensor_tensor(ov[:, 2, :], ov[:, 1, :], ov[:, 0, :], ALU.subtract))
                step(dve.tensor_scalar(ov[:, 3, :], ov[:, 2, :], float(P), float(P * (E - 1)), ALU.mult, ALU.add))
                step(dve.tensor_tensor(ov[:, 3, :], ov[:, 3, :], self.con("iota_e128"), ALU.subtract))
                step(dve.tensor_scalar(tmp[:, :, 0, :], rank[:], float(P), None, ALU.is_ge))
                step(dve.tensor_tensor(tmp[:, :, 0, :], tmp[:, :, 0, :], ov[:, 3, :].unsqueeze(1).to_broadcast([P, NT, E]), ALU.mult))
                step(dve.tensor_tensor(rank[:], rank[:], tmp[:, :, 0, :], ALU.add))
                step(dve.tensor_tensor(rank[:], rank[:], self.con("iota_e128").unsqueeze(1).to_broadcast([P, NT, E]), ALU.add))
                step(dve.tensor_tensor(tmp[:], oh[:], rank[:].unsqueeze(2).to_broadcast([P, NT, 2, E]), ALU.mult))
                step(dve.tensor_reduce(dst[:], tmp[:].rearrange("p i k e -> p (i k) e"), AX, ALU.add))
                step(dve.tensor_copy(dsti[:], dst[:]))
                step(dve.tensor_scalar(blki[:], dsti[:], 7, None, ALU.logical_shift_right))
                step(dve.tensor_scalar(sloti[:], dsti[:], P - 1, None, ALU.bitwise_and))
                step(dve.tensor_copy(blkf[:], blki[:]))
                step(dve.tensor_copy(slotf[:], sloti[:]))
                for k in range(2):
                    step(dve.tensor_scalar(val[:].rearrange("p (i k) -> p i k", k=2)[:, :, k], self.con("iota_tok"), 2.0, 1.0 + k, ALU.mult, ALU.add))
                for n in range(2 * NT):
                    if n >= 4:
                        dve.wait_ge(S["cum"], n - 2)
                    dve.tensor_scalar(rr[:, n % 4, :], self.con("iota128"), slotf[:, n:n + 1], None, ALU.is_equal).then_inc(S["slot"], 1)
                    dve.tensor_scalar(bt[:, n % 4, :], self.con("iota_blk"), blkf[:, n:n + 1], val[:, n:n + 1], ALU.is_equal,
                                      ALU.mult).then_inc(S["slot"], 1)
                step(dve.tensor_tensor(cmpb[:], ov[:, 1, :].unsqueeze(1).to_broadcast([P, NOV, E]),
                                       self.con("iota_blk")[:, 0:NOV].unsqueeze(2).to_broadcast([P, NOV, E]), ALU.is_le))
                step(dve.tensor_reduce(bef[:, 0:NOV], cmpb[:], AX, ALU.add))
                step(dve.tensor_scalar(bef[:, 0:NOV], bef[:, 0:NOV], float(E - 1), None, ALU.min))
                step(dve.tensor_copy(bef[:, NOV:NOV + 1], ov[:, 1, E - 1:E]))
                step(dve.tensor_copy(self.extra[:], bef[:]))
                dve.wait_ge(S["cum"], 1 + 2 * NT)
                step(dve.tensor_scalar(vs[:, 0, :], bank[2][:, 0:NBLK], 0.0, 8192.0, ALU.is_equal, ALU.mult))
                step(dve.scalar_tensor_tensor(vs[:, 1, :], bank[2][:, 0:NBLK], -1.0, vs[:, 0, :], ALU.add, ALU.add))
                step(dve.tensor_copy(self.slot_to[:], vs[:, 1, :]))
                step(dve.tensor_scalar(self.slot_from[:], self.slot_to[:], 1, None, ALU.logical_shift_right))

    def expert_stage(self):
        nc = self.nc
        NR = 4
        with ExitStack() as c:
            f = lambda n, shape, dt=F32: self.sb(c, "ex_" + n, [P] + shape, dt)
            wgu = f("w_gate_up", [NR, KT, 2 * DE])
            wd = f("w_down", [NR, 2, D])
            xg, xt = f("x", [2, D]), f("xt", [2, KT, P])
            si, hid, ht, yo = f("silu", [DE]), f("hid", [DE]), f("hid_t", [2, P]), f("y", [2, D])
            ifrom, ito = f("from", [2], U32), f("to", [2], U32)
            names = ("turn", "ta", "tv", "gu", "si", "hid", "ht", "htc", "dn", "ya", "yv", "ix", "init")
            S = {n: self.sem(c, "ex_" + n) for n in names}
            WL = [self.sem(c, f"ex_w{j}") for j in range(NR)]
            GA = [self.sem(c, f"ex_gathered{j}") for j in range(2)]
            SC = [self.sem(c, f"ex_scattered{j}") for j in range(2)]
            V = {n: self.sem(c, "ov_" + n) for n in names + ("w", "ga", "sc")}
            block = c.enter_context(nc.Block())
            bank = self.bank

            def load(eng, e, j, sem):
                for name, dst in (("moe_w_gate", wgu[:, j, :, 0:DE]), ("moe_w_up", wgu[:, j, :, DE:2 * DE]), ("moe_w_down", wd[:, j, :, :])):
                    eng.dma_start(dst, self.i[name][bass.ds(e, 1), :, :].rearrange("o (kt p) n -> p (o kt) n", p=P)).then_inc(sem, 16)

            def gather(pool, b, sem):
                pool.indirect_dma_start(xg[:, b, :], None, self.h2d, bass.IndirectOffsetOnAxis(ap=ifrom[:, b:b + 1], axis=0),
                                        bounds_check=T - 1, oob_is_err=False).then_inc(sem, 16)

            def scatter(pool, b, sem):
                pool.indirect_dma_start(self.yd, bass.IndirectOffsetOnAxis(ap=ito[:, b:b + 1], axis=0), yo[:, b, :], None,
                                        bounds_check=2 * T - 1, oob_is_err=False).then_inc(sem, 16)

            def turns(eng, body):
                body(0)
                with eng.Fori(1, E // NR) as it:
                    body(it)

            def further(eng, body):
                n = eng.value_load(self.extra[0:1, NOV:NOV + 1], min_val=0, max_val=NOV)
                with eng.If(n > 0):
                    with eng.Fori(0, NOV) as b:
                        body(b)

            @block.sync
            def _(sp):
                for j in range(NR):
                    load(sp, j, j, WL[j])
                with sp.Fori(1, E // NR) as it:
                    for j in range(NR):
                        sp.wait_ge(S["dn"], (it - 1) * (2 * NR) + 2 * j + 2)
                        load(sp, it * NR + j, j, WL[j])

                def body(b):
                    e = sp.value_load(self.extra[0:1, bass.ds(b, 1)], min_val=0, max_val=E - 1)
                    load(sp, e, 0, V["w"])
                    sp.wait_ge(V["dn"], b * 2 + 2)
                    self.pass_gate(sp)

                sp.wait_ge(S["dn"], 2 * E)
                further(sp, body)

            @block.gpsimd
            def _(pool):
                pool.memset(xg[:], 0.0).then_inc(S["init"], 1)
                pool.wait_ge(S["init"], 1)
                for b in range(2):
                    pool.tensor_copy(ifrom[:, b:b + 1], self.slot_from[:, b:b + 1]).then_inc(S["ix"], 1)
                    pool.wait_ge(S["ix"], b + 1)
                    gather(pool, b, GA[b])

                def body(it):
                    for j in range(NR):
                        e, b = it * NR + j, j % 2
                        pool.wait_ge(S["turn"], (e + 1) * 2)
                        pool.wait_ge(GA[b], 16 * (it * 2 + j // 2 + 1))
                        pool.tensor_copy(ifrom[:, b:b + 1], self.slot_from[:, bass.ds(e + 2, 1)]).then_inc(S["ix"], 1)
                        pool.wait_ge(S["ix"], 2 * e + 3)
                        self.pass_gate(pool)
                        gather(pool, b, GA[b])
                        pool.tensor_copy(ito[:, b:b + 1], self.slot_to[:, bass.ds(e, 1)]).then_inc(S["ix"], 1)
                        pool.wait_ge(S["ix"], 2 * e + 4)
                        self.pass_gate(pool)
                        pool.wait_ge(S["ya"], e + 1)
                        pool.wait_ge(S["yv"], e + 1)
                        self.pass_gate(pool)
                        scatter(pool, b, SC[b])
                        pool.wait_ge(SC[b], 16 * (it * 2 + j // 2 + 1))
                        self.pass_gate(pool)

                turns(pool, body)
                for b in range(2):
                    pool.wait_ge(GA[b], 16 * (E // 2 + 1))

                def over(b):
                    pool.tensor_copy(ifrom[:, 0:1], self.slot_from[:, bass.ds(b + E, 1)]).then_inc(V["ix"], 1)
                    pool.tensor_copy(ito[:, 0:1], self.slot_to[:, bass.ds(b + E, 1)]).then_inc(V["ix"], 1)
                    pool.wait_ge(V["ix"], 2 * b + 2)
                    self.pass_gate(pool)
                    gather(pool, 0, V["ga"])
                    pool.wait_ge(V["ya"], b + 1)
                    pool.wait_ge(V["yv"], b + 1)
                    self.pass_gate(pool)
                    scatter(pool, 0, V["sc"])
                    pool.wait_ge(V["sc"], 16 * b + 16)
                    pool.wait_ge(V["ga"], 16 * b + 16)
                    self.pass_gate(pool)

                pool.wait_ge(S["turn"], 2 * E + 2)
                further(pool, over)

            def pe_turn(pe, b, sem):
                for kt in range(KT):
                    ins = pe.transpose(bank[4 + kt // 4][:, kt % 4 * P:(kt % 4 + 1) * P], xg[:, b, kt * P:(kt + 1) * P], self.con("ident"))
                    if kt % 4 == 3:
                        ins.then_inc(sem, 1)

            def pe_up(pe, b, w, gb, sem):
                for kt in range(KT):
                    ins = pe.matmul(bank[gb][:], xt[:, b, kt, :], wgu[:, w, kt, :], start=kt == 0, stop=kt == KT - 1)
                ins.then_inc(sem, 1)

            def pe_hid(pe, sem):
                for q in range(2):
                    ins = pe.transpose(bank[6][:, q * P:(q + 1) * P], hid[:, q * P:(q + 1) * P], self.con("ident"))
                ins.then_inc(sem, 1)

            def pe_down(pe, w, sem):
                for half in range(2):
                    for q in range(2):
                        ins = pe.matmul(bank[2 + half][:], ht[:, q, :], wd[:, w, q, half * HALF:(half + 1) * HALF], start=q == 0, stop=q == 1)
                    ins.then_inc(sem, 1)

            @block.tensor
            def _(pe):
                pe.wait_ge(GA[0], 16)
                pe_turn(pe, 0, S["turn"])

                def body(it):
                    for j in range(NR):
                        e = it * NR + j
                        pe.wait_ge(WL[j], 48 * (it + 1))
                        pe.wait_ge(S["ta"], e + 1)
                        pe.wait_ge(S["tv"], e + 1)
                        pe_up(pe, j % 2, j, j % 2, S["gu"])
                        pe.wait_ge(GA[(j + 1) % 2], 16 * (it * 2 + (j + 1) // 2 + 1))
                        pe_turn(pe, (j + 1) % 2, S["turn"])
                        pe.wait_ge(S["hid"], e + 1)
                        pe_hid(pe, S["ht"])
                        pe.wait_ge(S["htc"], e + 1)
                        if not (isinstance(e, int) and e == 0):
                            pe.wait_ge(S["ya"], e)
                            pe.wait_ge(S["yv"], e)
                        pe_down(pe, j, S["dn"])

                turns(pe, body)
                pe.wait_ge(S["ya"], E)
                pe.wait_ge(S["yv"], E)
                pe.wait_ge(S["ta"], E + 1)
                pe.wait_ge(S["tv"], E + 1)

                def over(b):
                    pe.wait_ge(V["ga"], 16 * b + 16)
                    pe_turn(pe, 0, V["turn"])
                    pe.wait_ge(V["w"], 48 * b + 48)
                    pe.wait_ge(V["ta"], b + 1)
                    pe.wait_ge(V["tv"], b + 1)
                    pe_up(pe, 0, 0, 0, V["gu"])
                    pe.wait_ge(V["hid"], b + 1)
                    pe_hid(pe, V["ht"])
                    pe.wait_ge(V["htc"], b + 1)
                    pe_down(pe, 0, V["dn"])
                    pe.wait_ge(V["ya"], b + 1)
                    pe.wait_ge(V["yv"], b + 1)
                    self.pass_gate(pe)

                further(pe, over)

            def act_turned(act, b, q, n, SS):
                act.wait_ge(SS["turn"], n)
                act.activation(xt[:, b, 0:4, :].rearrange("p a b -> p (a b)"), bank[4][:], ACT.Copy).then_inc(SS["ta"], 1)

            @block.scalar
            def _(act):
                act_turned(act, 0, 0, 1, S)

                def body(it):
                    for j in range(NR):
                        e = it * NR + j
                        act.wait_ge(S["gu"], e + 1)
                        act.activation(si[:], bank[j % 2][:, 0:DE], ACT.Silu).then_inc(S["si"], 1)
                        act_turned(act, (j + 1) % 2, 0, 2 * e + 3, S)
                        act.wait_ge(S["dn"], 2 * e + 1)
                        if not (isinstance(e, int) and e < 2):
                            act.wait_ge(SC[j % 2], 16 * (it * 2 + j // 2))
                        act.activation(yo[:, j % 2, 0:HALF], bank[2][:], ACT.Copy).then_inc(S["ya"], 1)

                turns(act, body)

                def over(b):
                    act_turned(act, 0, 0, 2 * b + 1, V)
                    act.wait_ge(V["gu"], b + 1)
                    act.activation(si[:], bank[0][:, 0:DE], ACT.Silu).then_inc(V["si"], 1)
                    act.wait_ge(V["dn"], 2 * b + 1)
                    act.activation(yo[:, 0, 0:HALF], bank[2][:], ACT.Copy).then_inc(V["ya"], 1)

                act.wait_ge(SC[0], 16 * (E // 2))
                further(act, over)

            def dve_turned(dve, b, n, SS):
                dve.wait_ge(SS["turn"], n)
                dve.tensor_copy(xt[:, b, 4:8, :].rearrange("p a b -> p (a b)"), bank[5][:]).then_inc(SS["tv"], 1)

            def dve_hid(dve, gb, n, SS):
                dve.wait_ge(SS["si"], n)
                dve.tensor_tensor(hid[:], si[:], bank[gb][:, DE:2 * DE], ALU.mult).then_inc(SS["hid"], 1)

            @block.vector
            def _(dve):
                dve_turned(dve, 0, 2, S)

                def body(it):
                    for j in range(NR):
                        e = it * NR + j
                        dve_hid(dve, j % 2, e + 1, S)
                        dve_turned(dve, (j + 1) % 2, 2 * e + 4, S)
                        dve.wait_ge(S["ht"], e + 1)
                        dve.tensor_copy(ht[:].rearrange("p a b -> p (a b)"), bank[6][:, 0:2 * P]).then_inc(S["htc"], 1)
                        dve.wait_ge(S["dn"], 2 * e + 2)
                        if not (isinstance(e, int) and e < 2):
                            dve.wait_ge(SC[j % 2], 16 * (it * 2 + j // 2))
                        dve.tensor_copy(yo[:, j % 2, HALF:D], bank[3][:]).then_inc(S["yv"], 1)

                turns(dve, body)

                def over(b):
                    dve_turned(dve, 0, 2 * b + 2, V)
                    dve_hid(dve, 0, b + 1, V)
                    dve.wait_ge(V["ht"], b + 1)
                    dve.tensor_copy(ht[:].rearrange("p a b -> p (a b)"), bank[6][:, 0:2 * P]).then_inc(V["htc"], 1)
                    dve.wait_ge(V["dn"], 2 * b + 2)
                    dve.tensor_copy(yo[:, 0, HALF:D], bank[3][:]).then_inc(V["yv"], 1)

                dve.wait_ge(SC[0], 16 * (E // 2))
                further(dve, over)

    def final_stage(self):
        nc = self.nc
        with ExitStack() as c:
            y = self.sb(c, "fin_y", [P, NT, 2, D])
            gain = self.sb(c, "fin_gain", [P, D])
            sq = self.sb(c, "fin_sq", [P, D])
            ss = self.sb(c, "fin_ss", [P, NT])
            x2 = self.x2
            S = {n: self.sem(c, "fin_" + n) for n in ("g", "a", "b", "ss", "ms", "rc", "rt", "o", "out")}
            Y = [self.sem(c, f"fin_y{i}") for i in range(NT)]
            block = c.enter_context(nc.Block())
            yv = self.yd.rearrange("(i p k) d -> p i k d", p=P, k=2)

            @block.sync
            def _(sp):
                for i in range(NT):
                    sp.dma_start(y[:, i, :, :], yv[:, i, :, :]).then_inc(Y[i], 16)
                    if i == 0:
                        sp.dma_start(gain[:], self.i["norm_final"].partition_broadcast(P)).then_inc(S["g"], 16)
                for i in range(NT):
                    sp.wait_ge(S["o"], i + 1)
                    sp.dma_start(self.out[i * P:(i + 1) * P, :], x2[:, i, :]).then_inc(S["out"], 16)
                sp.wait_ge(S["out"], 16 * NT)

            @block.scalar
            def _(act):
                for i in range(NT):
                    act.wait_ge(S["b"], i + 1)
                    if i:
                        act.wait_ge(S["ss"], i)
                    act.activation(sq[:], x2[:, i, :], ACT.Square, accum_out=ss[:, i:i + 1]).then_inc(S["ss"], 1)
                    act.wait_ge(S["rc"], i + 1)
                    act.activation(ss[:, i:i + 1], ss[:, i:i + 1], ACT.Sqrt).then_inc(S["rt"], 1)

            @block.vector
            def _(dve):
                def first(i):
                    dve.wait_ge(Y[i], 16)
                    dve.scalar_tensor_tensor(x2[:, i, :], y[:, i, 0, :], self.gates12[:, 0, i:i + 1], x2[:, i, :], ALU.mult, ALU.add).then_inc(S["a"], 1)
                    dve.wait_ge(S["a"], i + 1)
                    dve.scalar_tensor_tensor(x2[:, i, :], y[:, i, 1, :], self.gates12[:, 1, i:i + 1], x2[:, i, :], ALU.mult, ALU.add).then_inc(S["b"], 1)

                first(0)
                dve.wait_ge(S["g"], 16)
                for i in range(NT):
                    dve.wait_ge(S["ss"], i + 1)
                    dve.tensor_scalar(ss[:, i:i + 1], ss[:, i:i + 1], 1.0 / D, EPS, ALU.mult, ALU.add).then_inc(S["ms"], 1)
                    dve.wait_ge(S["ms"], i + 1)
                    dve.reciprocal(ss[:, i:i + 1], ss[:, i:i + 1]).then_inc(S["rc"], 1)
                    if i + 1 < NT:
                        first(i + 1)
                    dve.wait_ge(S["rt"], i + 1)
                    dve.scalar_tensor_tensor(x2[:, i, :], x2[:, i, :], ss[:, i:i + 1], gain[:], ALU.mult, ALU.mult).then_inc(S["o"], 1)

    def build(self):
        nc = self.nc
        with self.ctx as c:
            self.bank = [c.enter_context(nc.psum_tensor(f"bank{n}", [P, HALF], F32)) for n in range(8)]
            self.gates = {e.engine: self.sem(c, f"gate_{n}") for n, e in (
                ("dve", nc.vector), ("sp", nc.sync), ("pe", nc.tensor), ("pool", nc.gpsimd))}
            self.cons = self.sb(c, "cons_sb", [P, NCON])
            self.par = self.sb(c, "par_cols", [P, P])
            self.hT = self.x2 = self.sb(c, "hT_or_x2", [P, KT, T])
            self.gates12 = self.sb(c, "gates12", [P, 2, NT])
            self.slot_from = self.sb(c, "slot_from", [P, NBLK], U32)
            self.slot_to = self.sb(c, "slot_to", [P, NBLK], U32)
            self.extra = self.sb(c, "extra_blocks", [P, NOV + 1], I32)
            self.h2d = nc.dram_tensor("h2_rows", (T, D), F32, kind="Internal").ap()
            self.yd = nc.dram_tensor("expert_rows", (2 * T, D), F32, kind="Internal").ap()
            flat = lambda t: t.rearrange("p a b -> p (a b)")
            with ExitStack() as m:
                self.mixT = self.sb(m, "mixT", [P, KT, T])
                self.run_stage(self.norm_stage)
                self.run_stage(self.lru_stage)
                self.run_stage(self.rwkv_stage)
                self.run_stage(self.gdn_stage)
                self.run_stage(self.route_stage)
            self.run_stage(self.expert_stage)
            self.run_stage(self.final_stage)


def build_program(nc, ins, out):
    Build(nc, ins, out).build()


def layout(inputs):
    f = {k: np.ascontiguousarray(v) for k, v in inputs.items()}
    rows = lambda a: a.reshape(-1, P)
    per = [f[n][0].reshape(2, P) for n in ("rwkv_w0", "rwkv_a0", "rwkv_k_k", "rwkv_k_a", "rwkv_r_k", "rwkv_lnx_w", "rwkv_lnx_b")]
    mu = f["rwkv_mu"][0].reshape(7, P)
    rwkv = np.stack([mu[0:2], mu[2:4], mu[4:6]] + per, 1).reshape(20, P)
    conv = f["gdn_conv_w"][0].reshape(4, 3, GH, P).transpose(2, 1, 0, 3).reshape(48, P)
    lru = f["lru_conv_w"][0].reshape(4, 2, P).transpose(1, 0, 2).reshape(8, P)
    par = np.concatenate([rows(f["norm_mix"]), rows(f["norm_ffn"]), mu[6:7], rwkv, conv, lru,
                          rows(f["lru_conv_b"]), rows(f["lru_b_a"]), rows(f["lru_b_x"]), rows(f["lru_lambda"]),
                          rows(f["gdn_norm_w"])], 0)
    return {
        "x": f["x"][0], "par_rows": np.ascontiguousarray(par), "cons": constants(),
        "w_in": f["w_in"][0], "w_out": f["w_out"][0],
        "rwkv_w2": f["rwkv_w2"][0], "rwkv_a2": f["rwkv_a2"][0], "rwkv_g2": f["rwkv_g2"][0],
        "gdn_ab": np.ascontiguousarray(np.concatenate([f["gdn_a_log"], f["gdn_dt_bias"]], 1)),
        "lru_w_a": f["lru_w_a"][0], "lru_w_x": f["lru_w_x"][0],
        "norm_ffn_row": f["norm_ffn"], "norm_final": f["norm_final"][None, :],
        "moe_b": np.ascontiguousarray(np.concatenate([f["moe_b_group"], f["moe_b_expert"]], 1)),
        "moe_w_group": f["moe_w_group"][0], "moe_w_expert": f["moe_w_expert"][0],
        "moe_w_gate": f["moe_w_gate"][0], "moe_w_up": f["moe_w_up"][0], "moe_w_down": f["moe_w_down"][0],
    }


def kernel(**inputs):
    from concourse import bacc, mybir as _mybir
    from concourse.bass_utils import run_bass_kernel_spmd as run

    arrays = layout(inputs)
    nc = bacc.Bacc("TRN2", target_bir_lowering=False, num_devices=1)
    ins = {k: nc.dram_tensor(k, a.shape, _mybir.dt.from_np(a.dtype), kind="ExternalInput").ap() for k, a in arrays.items()}
    out = nc.dram_tensor("out", (T, D), F32, kind="ExternalOutput").ap()
    build_program(nc, ins, out)
    r = run(nc, [arrays], core_ids=[0])
    return r.results[0]["out"].reshape(1, T, D)
```

```python
from contextlib import ExitStack

import numpy as np

import concourse.bass as bass
from concourse import mybir

F32 = mybir.dt.float32
I32 = mybir.dt.int32
U32 = mybir.dt.uint32
ALU = mybir.AluOpType
ACT = mybir.ActivationFunctionType
AX = mybir.AxisListType.X

P = 128
T = 1024
D = 1024
NT = T // P
KT = D // P
HALF = 512
EPS = 1e-6

DA, DB, DC = D // 4, D // 2, D // 4
A_COLS = 3 * DA + 32 + 32 + 64
B_COLS = 4 * DB + 8
COL_B = A_COLS
COL_BETA = COL_B + 4 * DB
COL_C = A_COLS + B_COLS
GN_EPS = 64e-5
EM05 = float(np.exp(-0.5))

GH = 4
NG = T // P
CR = 64
NCR = T // CR

E = 32
DE = D // 4
NOV = 15
NBLK = E + NOV
NR = 4
NEARLY = 2

PAR = {}
_n = 0
for _name, _rows in (("norm_mix", 8), ("norm_ffn", 8), ("mu_lo", 1), ("rwkv", 20), ("gdn_conv", 48),
                     ("lru_conv", 8), ("lru_conv_b", 2), ("lru_b_a", 2), ("lru_b_x", 2),
                     ("lru_lambda", 2), ("gdn_norm", 1)):
    PAR[_name] = _n
    _n += _rows
NPAR = _n

CON = {}
_n = 0
for _name, _cols in (("ident", P), ("ones", P), ("ones64", P), ("upper", P), ("below", P), ("low", P),
                     ("low_strict", P), ("up64_strict", P), ("up64", P), ("lev_low", 7 * P),
                     ("lev_up", 6 * P), ("iota128", P), ("iota_blk", NBLK), ("iota_tok", NT),
                     ("iota_e", E), ("iota_e128", E), ("half", 2), ("j128", 7), ("iota_p", 1), ("idx4", 4),
                     ("keep", 2), ("nhalf", 2)):
    CON[_name] = (_n, _cols)
    _n += _cols
NCON = _n


def constants():
    c = np.zeros((P, NCON), np.float32)
    i, j = np.arange(P)[:, None], np.arange(P)[None, :]

    def put(name, value):
        a, n = CON[name]
        c[:, a:a + n] = value

    put("ident", i == j)
    put("ones", 1)
    put("ones64", i // 64 == j // 64)
    put("upper", i <= j)
    put("below", i < j)
    put("low", i >= j)
    put("low_strict", i > j)
    put("up64_strict", (i < j) & (i // 64 == j // 64))
    put("up64", (i <= j) & (i // 64 == j // 64))
    lev = [(i // (2 * s) == j // (2 * s)) & (i % (2 * s) >= s) & (j % (2 * s) < s) for s in (1, 2, 4, 8, 16, 32, 64)]
    put("lev_low", np.concatenate(lev, 1))
    put("lev_up", np.concatenate([m.T for m in lev[:6]], 1))
    put("iota128", j)
    put("iota_blk", np.arange(NBLK)[None, :])
    put("iota_tok", i + P * np.arange(NT)[None, :])
    put("iota_e", np.arange(E)[None, :])
    put("iota_e128", P * np.arange(E)[None, :])
    put("half", i // 64 == np.arange(2)[None, :])
    put("j128", P * np.arange(1, 8)[None, :])
    put("iota_p", i)
    put("idx4", 4 - np.arange(4)[None, :])
    put("keep", np.arange(2)[None, :])
    put("nhalf", -1.0 * (i // 64 == np.arange(2)[None, :]))
    return c


class Step:

    def __init__(self, eng, sem, base=0):
        self.eng, self.sem, self.base, self.n = eng, sem, base, 0

    def inc(self, ins):
        ins.then_inc(self.sem, 1)
        self.n += 1

    def wait(self):
        self.eng.wait_ge(self.sem, self.base + self.n)

    def __call__(self, ins):
        self.inc(ins)
        self.wait()


class Build:
    def __init__(self, nc, ins, out):
        self.nc, self.i, self.out = nc, ins, out
        self.ctx = ExitStack()

    def sb(self, ctx, name, shape, dt=F32):
        return ctx.enter_context(self.nc.sbuf_tensor(name, shape, dt))

    def sem(self, ctx, name):
        return self.nc.alloc_semaphore(name)

    def run_stage(self, stage):
        before = self.nc.snapshot_sems()
        stage()
        self.nc.clear_and_free_semaphores(self.nc.allocated_since(before))
        self.nc.all_engine_barrier()

    def con(self, name):
        a, n = CON[name]
        return self.cons[:, a:a + n]

    def parc(self, name, k=0, n=1):
        return self.par[:, PAR[name] + k:PAR[name] + k + n]

    def pass_gate(self, eng):
        eng.sem_inc(self.gates[eng.engine], 1)

    def norm_stage(self):
        nc = self.nc
        with ExitStack() as c:
            x = self.sb(c, "x_in", [P, NT, D])
            sq = self.sb(c, "x_sq", [P, D])
            prow = self.sb(c, "par_rows_sb", [P, P])
            ss = self.sb(c, "x_ss", [P, NT])
            rs = self.sb(c, "x_rs", [P, NT])
            s_par, s_con, s_x, s_ss, s_v, s_rs, s_xn, s_tr, s_par_t, s_par_ok = (
                self.sem(c, n) for n in ("par_landed", "cons_landed", "x_landed", "x_squared", "norm_dve", "norm_root", "x_scaled", "x_turned", "par_turned", "par_ready"))
            s_ev = [self.sem(c, "turned_out_dve"), self.sem(c, "turned_out_act")]
            block = c.enter_context(nc.Block())
            xv = self.i["x"].rearrange("(i p) d -> p i d", p=P)

            @block.sync
            def _(sp):
                sp.dma_start(x[:, 0, :], xv[:, 0, :]).then_inc(s_x, 16)
                sp.dma_start(prow[0:NPAR, :], self.i["par_rows"]).then_inc(s_par, 16)
                sp.dma_start(self.cons[:], self.i["cons"]).then_inc(s_con, 16)
                for i in range(1, NT):
                    sp.wait_ge(s_x, 16 * i)
                    sp.dma_start(x[:, i, :], xv[:, i, :]).then_inc(s_x, 16)

            @block.scalar
            def _(act):
                for i in range(NT):
                    act.wait_ge(s_x, 16 * (i + 1))
                    if i:
                        act.wait_ge(s_ss, i)
                    act.activation(sq[:], x[:, i, :], ACT.Square, accum_out=ss[:, i:i + 1]).then_inc(s_ss, 1)
                act.wait_ge(s_v, 2)
                act.activation(rs[:], rs[:], ACT.Sqrt).then_inc(s_rs, 1)
                act.wait_ge(s_par_ok, 1)
                for t in range(1, 2 * KT, 2):
                    self.norm_out(act, t, s_tr, s_ev)

            @block.vector
            def _(dve):
                dve.wait_ge(s_ss, NT)
                dve.tensor_scalar(rs[:], ss[:], 1.0 / D, EPS, ALU.mult, ALU.add).then_inc(s_v, 1)
                dve.wait_ge(s_v, 1)
                dve.reciprocal(rs[:], rs[:]).then_inc(s_v, 1)
                dve.wait_ge(s_rs, 1)
                for i in range(NT):
                    dve.tensor_scalar(x[:, i, :], x[:, i, :], rs[:, i:i + 1], None, ALU.mult).then_inc(s_xn, 1)
                dve.wait_ge(s_par_t, 1)
                dve.tensor_copy(self.par[:, 0:NPAR], self.bank[7][:, 0:NPAR]).then_inc(s_par_ok, 1)
                dve.wait_ge(s_par_ok, 1)
                for t in range(0, 2 * KT, 2):
                    self.norm_out(dve, t, s_tr, s_ev)

            @block.tensor
            def _(pe):
                pe.wait_ge(s_par, 16)
                pe.wait_ge(s_con, 16)
                pe.transpose(self.bank[7][:, 0:NPAR], prow[0:NPAR, :], self.con("ident")[0:NPAR, 0:NPAR]).then_inc(s_par_t, 1)
                for t in range(2 * KT):
                    kt, half = t // 2, t % 2
                    pe.wait_ge(s_xn, 4 * half + 4)
                    if t >= 6:
                        pe.wait_ge(s_ev[t % 2], (t - 6) // 2 + 1)
                    for q in range(4):
                        ins = pe.transpose(self.bank[t % 6][:, q * P:(q + 1) * P],
                                           x[:, 4 * half + q, kt * P:(kt + 1) * P], self.con("ident"))
                    ins.then_inc(s_tr, 1)

    def norm_out(self, eng, t, s_tr, s_ev):
        kt, half = t // 2, t % 2
        eng.wait_ge(s_tr, t + 1)
        dst = self.hT[:, kt, half * HALF:(half + 1) * HALF]
        gain = self.parc("norm_mix", kt)
        if t % 2 == 0:
            eng.tensor_scalar(dst, self.bank[t % 6][:], gain, None, ALU.mult).then_inc(s_ev[0], 1)
        else:
            eng.activation(dst, self.bank[t % 6][:], ACT.Copy, scale=gain).then_inc(s_ev[1], 1)

    def lru_stage(self):
        nc = self.nc
        with ExitStack() as c:
            w = self.sb(c, "lru_w", [P, KT, 2 * DC])
            wg = self.sb(c, "lru_gate_w", [P, 2, 2, P])
            raw = self.sb(c, "lru_raw", [P, 2, 3 + T])
            xb = self.sb(c, "lru_xb", [P, 2, T])
            gg = self.sb(c, "lru_gelu", [P, 2, T])
            r = self.sb(c, "lru_r", [P, 2, T])
            ig = self.sb(c, "lru_i", [P, 2, T])
            a = self.sb(c, "lru_a", [P, 2, T])
            th = self.sb(c, "lru_tanh", [P, 2, T])
            lt = self.sb(c, "lru_ln", [P, 2, T])
            v = self.sb(c, "lru_small", [P, 12, 2])
            S = {n: self.sem(c, "lru_" + n) for n in (
                "w", "wz", "wg", "proj", "raw", "gelu", "conv", "gates", "sig", "spe", "spd", "act", "step", "init", "out")}
            block = c.enter_context(nc.Block())

            @block.sync
            def _(sp):
                for kt in range(KT):
                    sp.dma_start(w[:, kt, :], self.i["w_in"][kt * P:(kt + 1) * P, COL_C:COL_C + 2 * DC]).then_inc(S["w"], 16)
                sp.wait_ge(S["wz"], 1)
                for g, name in enumerate(("lru_w_a", "lru_w_x")):
                    for b in range(4):
                        o = 64 * (b % 2)
                        sp.dma_start(wg[o:o + 64, g, b // 2, o:o + 64], self.i[name][b]).then_inc(S["wg"], 16)

            @block.gpsimd
            def _(pool):
                pool.memset(wg[:], 0.0).then_inc(S["wz"], 1)
                pool.memset(raw[:, :, 0:3], 0.0).then_inc(S["init"], 1)

            @block.tensor
            def _(pe):
                pe.wait_ge(S["w"], 16 * KT)
                for m in range(4):
                    for kt in range(KT):
                        for half in range(2):
                            ins = pe.matmul(self.bank[2 * m + half][:], w[:, kt, m * P:(m + 1) * P],
                                            self.hT[:, kt, half * HALF:(half + 1) * HALF], start=kt == 0, stop=kt == KT - 1)
                    ins.then_inc(S["proj"], 1)
                pe.wait_ge(S["wg"], 16 * 8)
                pe.wait_ge(S["raw"], 4)
                pe.wait_ge(S["conv"], 8)
                for g in range(2):
                    if g:
                        pe.wait_ge(S["gelu"], 4)
                    for j in range(2):
                        for half in range(2):
                            pe.matmul(self.bank[4 * g + 2 * j + half][:], wg[:, g, j, :],
                                      xb[:, j, half * HALF:(half + 1) * HALF], start=True, stop=True).then_inc(S["gates"], 1)

            @block.scalar
            def _(act):
                act.wait_ge(S["spd"], 2)
                act.activation(v[:, 2, :], v[:, 1, :], ACT.Exp, scale=-1.0).then_inc(S["spe"], 1)
                act.wait_ge(S["spd"], 3)
                act.activation(v[:, 4, :], v[:, 3, :], ACT.Ln).then_inc(S["spe"], 1)
                for m in range(2):
                    act.wait_ge(S["proj"], m + 1)
                    for half in range(2):
                        act.activation(raw[:, m, 3 + half * HALF:3 + (half + 1) * HALF], self.bank[2 * m + half][:],
                                       ACT.Copy).then_inc(S["raw"], 1)
                for m in range(2):
                    act.wait_ge(S["proj"], m + 3)
                    for half in range(2):
                        act.activation(gg[:, m, half * HALF:(half + 1) * HALF], self.bank[4 + 2 * m + half][:],
                                       ACT.Gelu_apprx_tanh).then_inc(S["gelu"], 1)
                for g, dst, bias in ((0, r, "lru_b_a"), (1, ig, "lru_b_x")):
                    for j in range(2):
                        for half in range(2):
                            act.wait_ge(S["gates"], 4 * g + 2 * j + half + 1)
                            act.activation(dst[:, j, half * HALF:(half + 1) * HALF], self.bank[4 * g + 2 * j + half][:],
                                           ACT.Sigmoid, bias=self.parc(bias, j)).then_inc(S["sig"], 1)
                act.wait_ge(S["spd"], 13)
                act.wait_ge(S["sig"], 8)
                for j in range(2):
                    act.activation(a[:, j, :], r[:, j, :], ACT.Exp, scale=v[:, 11, j:j + 1]).then_inc(S["act"], 1)
                    act.activation(th[:, j, :], r[:, j, :], ACT.Tanh, scale=v[:, 11, j:j + 1]).then_inc(S["act"], 1)
                act.wait_ge(S["act"], 4)
                act.activation(lt[:], th[:], ACT.Ln, scale=-1.0, bias=1.0).then_inc(S["act"], 1)
                act.activation(r[:], th[:], ACT.Sqrt, scale=-2.0).then_inc(S["act"], 1)
                act.wait_ge(S["act"], 6)
                act.activation(lt[:], lt[:], ACT.Exp, scale=-0.5).then_inc(S["act"], 1)

            @block.vector
            def _(dve):
                step = Step(dve, S["step"])
                lam = self.parc("lru_lambda", 0, 2)
                dve.tensor_scalar(v[:, 0, :], lam, -1.0, None, ALU.mult).then_inc(S["spd"], 1)
                dve.wait_ge(S["spd"], 1)
                dve.tensor_tensor(v[:, 1, :], v[:, 0, :], lam, ALU.max).then_inc(S["spd"], 1)
                dve.wait_ge(S["spe"], 1)
                dve.tensor_scalar(v[:, 3, :], v[:, 2, :], 1.0, None, ALU.add).then_inc(S["spd"], 1)
                dve.wait_ge(S["spe"], 2)
                sp = Step(dve, S["spd"])
                sp.n = 3
                sp.wait()
                sp(dve.tensor_scalar(v[:, 5, :], v[:, 3, :], -1.0, None, ALU.add))
                sp(dve.tensor_scalar(v[:, 6, :], v[:, 5, :], 1e-30, None, ALU.max))
                sp(dve.reciprocal(v[:, 7, :], v[:, 6, :]))
                sp(dve.tensor_tensor(v[:, 8, :], v[:, 4, :], v[:, 2, :], ALU.mult))
                sp(dve.tensor_tensor(v[:, 8, :], v[:, 8, :], v[:, 7, :], ALU.mult))
                sp(dve.tensor_scalar(v[:, 9, :], v[:, 5, :], 0.0, None, ALU.is_equal))
                sp(dve.tensor_tensor(v[:, 9, :], v[:, 9, :], v[:, 2, :], ALU.mult))
                sp(dve.tensor_tensor(v[:, 8, :], v[:, 8, :], v[:, 9, :], ALU.add))
                sp(dve.tensor_scalar(v[:, 10, :], v[:, 0, :], 0.0, None, ALU.max))
                dve.tensor_tensor(v[:, 10, :], v[:, 10, :], v[:, 8, :], ALU.add).then_inc(S["step"], 1)
                step.n = 1
                step.wait()
                sp.inc(dve.tensor_scalar(v[:, 11, :], v[:, 10, :], -8.0, None, ALU.mult))
                dve.wait_ge(S["raw"], 4)
                dve.wait_ge(S["init"], 1)
                for j in range(2):
                    taps = [self.parc("lru_conv", 4 * j + t) for t in range(4)]
                    dve.tensor_scalar(xb[:, j, :], raw[:, j, 3:3 + T], taps[3], self.parc("lru_conv_b", j),
                                      ALU.mult, ALU.add).then_inc(S["conv"], 1)
                    for t in (2, 1, 0):
                        dve.wait_ge(S["conv"], 4 * j + 3 - t)
                        dve.scalar_tensor_tensor(xb[:, j, :], raw[:, j, t:t + T], taps[t], xb[:, j, :],
                                                 ALU.mult, ALU.add).then_inc(S["conv"], 1)
                dve.wait_ge(S["sig"], 8)
                dve.wait_ge(S["conv"], 8)
                step(dve.tensor_tensor(xb[:], xb[:], ig[:], ALU.mult))
                dve.wait_ge(S["act"], 7)
                step(dve.tensor_tensor(lt[:], lt[:], r[:], ALU.mult))
                step(dve.memset(lt[:, :, 0:1], 1.0))
                step(dve.tensor_tensor(xb[:], xb[:], lt[:], ALU.mult))
                for j in range(2):
                    step.inc(dve.tensor_tensor_scan(th[:, j, :], a[:, j, :], xb[:, j, :], 0.0, ALU.mult, ALU.add))
                step.wait()
                dve.wait_ge(S["gelu"], 4)
                dve.tensor_tensor(self.mixT[:, 6:8, :], th[:], gg[:], ALU.mult).then_inc(S["out"], 1)

    def invert_pe(self, pe, W, S, lhs, upd, tur, ye, levels, final_turn, between=None):
        for lv in range(levels + (1 if final_turn else 0)):
            if lv == 1 and between:
                between()
            for g in range(2):
                W(pe, "i_upd", 2 * lv + g + 1)
                for q in range(4):
                    ins = pe.transpose(self.bank[g][:, q * P:(q + 1) * P], upd[:, 4 * g + q, :], self.con("ident"))
                ins.then_inc(S["i_turn"], 1)
            if lv == levels:
                break
            for g in range(2):
                W(pe, "i_tur", 2 * lv + g + 1)
                for q in range(4):
                    ins = pe.matmul(self.bank[2 + g][:, q * P:(q + 1) * P], lhs[:, 4 * g + q, :], tur[:, 4 * g + q, :],
                                    start=True, stop=True)
                ins.then_inc(S["i_y"], 1)
            for g in range(2):
                W(pe, "i_ye", 2 * lv + g + 1)
                for q in range(4):
                    ins = pe.matmul(self.bank[4 + g][:, q * P:(q + 1) * P], ye[:, 4 * g + q, :], upd[:, 4 * g + q, :],
                                    start=True, stop=True)
                ins.then_inc(S["i_w"], 1)

    def invert_act(self, act, W, S, tur, ye, levels, final_turn, between=None):
        flat = lambda t, g: t[:, 4 * g:4 * g + 4, :].rearrange("p a b -> p (a b)")
        for lv in range(levels + (1 if final_turn else 0)):
            if lv == 1 and between:
                between()
            for g in range(2):
                W(act, "i_turn", 2 * lv + g + 1)
                act.activation(flat(tur, g), self.bank[g][:], ACT.Copy).then_inc(S["i_tur"], 1)
            if lv == levels:
                break
            for g in range(2):
                W(act, "i_y", 2 * lv + g + 1)
                act.activation(flat(ye, g), self.bank[2 + g][:], ACT.Copy).then_inc(S["i_ye"], 1)

    def invert_dve(self, dve, W, S, upd, masks, levels):
        for lv in range(levels):
            m = self.cons[:, CON[masks][0] + (lv + 1) * P:CON[masks][0] + (lv + 2) * P].bitcast(U32)
            for g in range(2):
                W(dve, "i_w", 2 * lv + g + 1)
                self.pass_gate(dve)
                dve.copy_predicated(upd[:, 4 * g:4 * g + 4, :], m.unsqueeze(1).to_broadcast([P, 4, P]),
                                    self.bank[4 + g][:].rearrange("p (a b) -> p a b", a=4)).then_inc(S["i_upd"], 1)

    def gdn_stage(self):
        nc = self.nc
        K = dict(w0=16, w1=16, w2=16, proj=3, raw=6, sil=3, sq=2, ss=4, ln=4, rs=2, qn=2, gcr=2, gr=8, ge=2, gm=4, trv=2, trk=2,
                 kv=6, kk=2, qk=2, nn=8, am=2, at=2, ate=2, i_init=1, i_turn=14, i_tur=14, i_y=12, i_ye=12, i_w=12,
                 i_upd=14, u=2, ue=2, wt=2, wte=2, ws=8, vn=8, sk=8, st=9, qs=2, av=2, t1=2, o=2, osq=3, ol=2, og=2,
                 ot=2, mx=2, hs=2, taps=1, conv=12)
        with ExitStack() as c:
            zw = self.sb(c, "gdn_work", [P, 18624])
            raw = self.sb(c, "gdn_raw", [P, 3, 3 + T])
            wqkv = self.sb(c, "gdn_w", [P, 3, KT, P])
            zs = self.sb(c, "gdn_z", [P, GH, NG, P])
            scal = self.sb(c, "gdn_scal", [P, GH, 8, NG])
            hs = self.sb(c, "gdn_head_scal", [P, 8, NG])
            taps = self.sb(c, "gdn_taps", [P, 12])
            wb = self.sb(c, "gdn_w_beta", [P, KT, 8])
            ab = self.sb(c, "gdn_ab_sb", [P, 8])
            ba = self.sb(c, "gdn_ba", [P, NT, 8])
            sm = self.sb(c, "gdn_small", [P, 6, GH, NG])
            ev = self.sb(c, "gdn_ea", [P, GH])
            ssum = self.sb(c, "gdn_ssum", [P, 3, NG])
            off = [0]

            def carve(n, shape=None):
                a = zw[:, off[0]:off[0] + n]
                off[0] += n
                return a

            v3 = lambda a, k: a.rearrange("p (a b) -> p a b", a=k)
            r1 = carve(3 * T)
            e, ei, es = (v3(r1[:, k * T:(k + 1) * T], NG) for k in range(3))
            osb, osq, og = e, ei, es
            r2 = carve(3 * T)
            cv = v3(r2, 3)
            nn, am, at = (v3(r2[:, k * T:(k + 1) * T], NG) for k in range(3))
            r3 = carve(2 * T)
            sq = v3(r3, 2)
            upd, tur = (v3(r3[:, k * T:(k + 1) * T], NG) for k in range(2))
            qn, kn = (v3(carve(T), NG) for _ in range(2))
            kd, kbg, vb = (v3(carve(T), NG) for _ in range(3))
            r6 = carve(T)
            glb = ye = v3(r6, NG)
            u, wt = v3(carve(T), NG), v3(carve(T), NG)
            vn = v3(carve(T), NG)
            st = v3(carve(9 * P), 9)
            wz = v3(zw[:, 0:KT * DB], KT)
            flat = lambda t, a, b: t[:, a:b, :].rearrange("p a b -> p (a b)")
            S = {n: self.sem(c, "gdn_" + n) for n in K}
            Z = {n: self.sem(c, "gdnz_" + n) for n in ("w", "z", "zs", "ba", "d", "a", "pe", "pad")}
            block = c.enter_context(nc.Block())
            win = self.i["w_in"].rearrange("(kt p) c -> p kt c", p=P)

            def waits(h):
                return lambda eng, name, n: eng.wait_ge(S[name], h * K[name] + n)

            @block.sync
            def _(sp):
                for kt in range(KT):
                    sp.dma_start(wz[:, kt, :], win[:, kt, COL_B + 3 * DB:COL_B + 4 * DB]).then_inc(Z["w"], 16)
                sp.dma_start(wb[:], win[:, :, COL_BETA:COL_BETA + 8]).then_inc(Z["w"], 16)
                sp.dma_start(ab[:], self.i["gdn_ab"].partition_broadcast(P)).then_inc(Z["w"], 16)
                for m in range(3):
                    sp.dma_start(wqkv[:, m, :, :], win[:, :, COL_B + m * DB:COL_B + m * DB + P]).then_inc(S[f"w{m}"], 16)
                with sp.Fori(1, GH) as h:
                    for m in range(3):
                        waits(h - 1)(sp, "proj", m + 1)
                        self.pass_gate(sp)
                        sp.dma_start(wqkv[:, m, :, :], win[:, :, bass.ds(h * P + (COL_B + m * DB), P)]).then_inc(S[f"w{m}"], 16)

            @block.gpsimd
            def _(pool):
                low = self.con("low").unsqueeze(1).to_broadcast([P, 4, P])
                lows = self.con("low_strict").unsqueeze(1).to_broadcast([P, 4, P])
                with pool.Fori(0, GH) as h:
                    W = waits(h)
                    for g in range(2):
                        W(pool, "ge", g + 1)
                        pool.tensor_tensor(es[:, 4 * g:4 * g + 4, :], e[:, 4 * g:4 * g + 4, :], lows, ALU.mult).then_inc(S["gm"], 1)
                        pool.tensor_tensor(ei[:, 4 * g:4 * g + 4, :], e[:, 4 * g:4 * g + 4, :], low, ALU.mult).then_inc(S["gm"], 1)

            @block.tensor
            def _(pe):
                pe.wait_ge(Z["w"], 160)
                for i in range(NT):
                    for kt in range(KT):
                        ins = pe.matmul(self.bank[i % 7][:], self.hT[:, kt, i * P:(i + 1) * P], wz[:, kt, :],
                                        start=kt == 0, stop=kt == KT - 1)
                        if i == 7 and kt == 0:
                            pass
                    ins.then_inc(Z["z"], 1)
                    for kt in range(KT):
                        ins = pe.matmul(self.bank[7][:, 8 * i:8 * i + 8], self.hT[:, kt, i * P:(i + 1) * P], wb[:, kt, :],
                                        start=kt == 0, stop=kt == KT - 1)
                    if i == 6:
                        pe.wait_ge(Z["zs"], 1)
                ins.then_inc(Z["ba"], 1)
                pe.wait_ge(Z["d"], 8)
                pe.wait_ge(Z["zs"], 8)
                gl = scal[:, :, 7, :]
                pe.matmul(self.bank[6][:, 0:32], self.con("upper"), gl, start=True, stop=True)
                pe.matmul(self.bank[6][:, 32:64], self.con("ones"), gl, start=True, stop=True).then_inc(Z["pe"], 1)
                pe.wait_ge(Z["d"], 14)
                tiles = dict(raw=raw, sq=sq, qn=qn, kn=kn, cv=cv, glb=glb, am=am, nn=nn, upd=upd, tur=tur, ye=ye, vb=vb,
                             kd=kd, kbg=kbg, wt=wt, st=st, vn=vn, at=at, og=og, wqkv=wqkv)
                for m, b0 in enumerate((4, 6, 2)):
                    waits(0)(pe, f"w{m}", 16)
                    for n in range(2 * KT):
                        self.gdn_project(pe, S, wqkv, m, b0, n)
                self.heads(pe, lambda h, last: self.gdn_pe(pe, waits(h), waits(h + 1), last, S, tiles))

            @block.scalar
            def _(act):
                for i in range(NT):
                    act.wait_ge(Z["z"], i + 1)
                    act.activation(zs[:, :, i, :], self.bank[i % 7][:].rearrange("p (h v) -> p h v", h=GH), ACT.Silu).then_inc(Z["zs"], 1)
                act.wait_ge(Z["d"], 1)
                act.activation(scal[:, :, 4, :], ba[:, :, 0:4].rearrange("p i h -> p h i"), ACT.Sigmoid).then_inc(Z["a"], 1)
                act.wait_ge(Z["d"], 4)
                act.activation(sm[:, 2, :, :], sm[:, 1, :, :], ACT.Exp, scale=-1.0).then_inc(Z["a"], 1)
                act.activation(ev[:], ab[:, 0:4], ACT.Exp).then_inc(Z["a"], 1)
                act.wait_ge(Z["a"], 3)
                act.activation(sm[:, 3, :, :], sm[:, 2, :, :], ACT.Ln, bias=1.0).then_inc(Z["a"], 1)
                act.wait_ge(Z["d"], 11)
                act.activation(scal[:, :, 1, :], scal[:, :, 0, :], ACT.Exp).then_inc(Z["a"], 1)
                act.activation(scal[:, :, 6, :], sm[:, 4, :, :], ACT.Exp).then_inc(Z["a"], 1)
                act.activation(scal[:, :, 2, :], sm[:, 5, :, :], ACT.Exp).then_inc(Z["a"], 1)

                def raw_out(W, m):
                    W(act, "proj", m + 1)
                    for half in range(2):
                        act.activation(raw[:, m, 3 + half * HALF:3 + (half + 1) * HALF], self.bank[(4, 6, 2)[m] + half][:],
                                       ACT.Copy).then_inc(S["raw"], 1)

                def silu(W, m):
                    W(act, "conv", 4 * (m + 1))
                    act.activation(cv[:, m, :], cv[:, m, :], ACT.Silu).then_inc(S["sil"], 1)

                def body(h, last):
                    W, W1 = waits(h), waits(h + 1)
                    for m in range(2):
                        W(act, "sil", m + 1)
                        act.activation(sq[:, m, :], cv[:, m, :], ACT.Square).then_inc(S["sq"], 1)
                    for b in range(4):
                        W(act, "ss", b + 1)
                        act.activation(sq[:, b // 2, b % 2 * HALF:(b % 2 + 1) * HALF], self.bank[b][:], ACT.Ln, bias=EPS).then_inc(S["ln"], 1)
                    for m in range(2):
                        W(act, "ln", 2 * m + 2)
                        act.activation(sq[:, m, :], sq[:, m, :], ACT.Exp, scale=-0.5).then_inc(S["rs"], 1)
                    for g in range(2):
                        W(act, "gr", 4 * g + 4)
                        act.activation(flat(e, 4 * g, 4 * g + 4), flat(e, 4 * g, 4 * g + 4), ACT.Exp, scale=-1.0).then_inc(S["ge"], 1)
                    silu(W, 2)

                    def scores_out():
                        for g in range(2):
                            W(act, "at", g + 1)
                            act.activation(flat(at, 4 * g, 4 * g + 4), self.bank[6 + g][:], ACT.Copy).then_inc(S["ate"], 1)

                    self.invert_act(act, W, S, tur, ye, 6, True, scores_out)
                    for g in range(2):
                        W(act, "u", g + 1)
                        act.activation(flat(u, 4 * g, 4 * g + 4), self.bank[2 + g][:], ACT.Copy).then_inc(S["ue"], 1)
                    if not last:
                        raw_out(W1, 0)
                    W(act, "osq", 3)
                    act.activation(ssum[:, 1, :], ssum[:, 1, :], ACT.Ln).then_inc(S["ol"], 1)
                    W(act, "ol", 1)
                    act.activation(ssum[:, 2, :], ssum[:, 1, :], ACT.Exp, scale=-0.5).then_inc(S["ol"], 1)
                    if not last:
                        raw_out(W1, 1)
                        silu(W1, 0)
                    for g in range(2):
                        W(act, "ot", g + 1)
                        act.activation(self.mixT[:, bass.ds(h + 2, 1), g * HALF:(g + 1) * HALF],
                                       self.bank[g][:].unsqueeze(1), ACT.Copy, scale=self.parc("gdn_norm")).then_inc(S["mx"], 1)
                    if not last:
                        silu(W1, 1)
                        raw_out(W1, 2)

                for m in range(3):
                    raw_out(waits(0), m)
                for m in range(2):
                    silu(waits(0), m)
                self.heads(act, body)

            @block.vector
            def _(dve):
                zd = Step(dve, Z["d"])
                dve.wait_ge(Z["ba"], 1)
                zd(dve.tensor_copy(ba[:].rearrange("p i h -> p (i h)"), self.bank[7][:, 0:64]))
                dt = ab[:, 4:8].unsqueeze(2).to_broadcast([P, GH, NG])
                zd(dve.tensor_tensor(sm[:, 0, :, :], ba[:, :, 4:8].rearrange("p i h -> p h i"), dt, ALU.add))
                zd(dve.tensor_scalar(sm[:, 1, :, :], sm[:, 0, :, :], -1.0, None, ALU.mult))
                zd(dve.tensor_tensor(sm[:, 1, :, :], sm[:, 0, :, :], sm[:, 1, :, :], ALU.max))
                dve.wait_ge(Z["a"], 4)
                zd(dve.tensor_scalar(sm[:, 0, :, :], sm[:, 0, :, :], 0.0, None, ALU.max))
                zd(dve.tensor_tensor(sm[:, 0, :, :], sm[:, 0, :, :], sm[:, 3, :, :], ALU.add))
                zd(dve.tensor_tensor(sm[:, 0, :, :], sm[:, 0, :, :], ev[:].unsqueeze(2).to_broadcast([P, GH, NG]), ALU.mult))
                zd(dve.tensor_scalar(scal[:, :, 7, :], sm[:, 0, :, :], -1.0, None, ALU.mult))
                dve.wait_ge(Z["pe"], 1)
                v4 = lambda a: a.rearrange("p (h i) -> p h i", h=GH)
                zd(dve.tensor_copy(scal[:, :, 0, :], v4(self.bank[6][:, 0:32])))
                zd(dve.tensor_copy(sm[:, 4, :, :], v4(self.bank[6][:, 32:64])))
                zd(dve.tensor_tensor(sm[:, 5, :, :], sm[:, 4, :, :], scal[:, :, 0, :], ALU.subtract))
                dve.wait_ge(Z["a"], 7)
                zd(dve.tensor_tensor(scal[:, :, 3, :], scal[:, :, 4, :], scal[:, :, 1, :], ALU.mult))
                zd(dve.tensor_scalar(scal[:, :, 5, :], scal[:, :, 4, :], -1.0, None, ALU.mult))
                zd(dve.memset(st[:, 0, :], 0.0))
                dve.memset(raw[:, :, 0:3], 0.0).then_inc(Z["pad"], 1)
                dve.wait_ge(Z["pad"], 1)
                tiles = dict(raw=raw, sq=sq, qn=qn, kn=kn, cv=cv, glb=glb, am=am, nn=nn, upd=upd, vb=vb, kd=kd, kbg=kbg,
                             wt=wt, st=st, vn=vn, u=u, e=e, ei=ei, es=es, osb=osb, osq=osq, og=og, zs=zs, scal=scal, hs=hs,
                             taps=taps, ssum=ssum)
                self.gdn_taps(dve, 0, waits(0), S, tiles)
                for m in range(2):
                    self.gdn_conv(dve, waits(0), S, tiles, m)
                self.heads(dve, lambda h, last: self.gdn_dve(dve, h, waits(h), waits(h + 1), last, S, tiles))

    def heads(self, eng, body):
        with eng.Fori(0, GH - 1) as h:
            body(h, False)
        body(GH - 1, True)

    def gdn_project(self, pe, S, wqkv, m, b0, n):
        kt, half = n // 2, n % 2
        ins = pe.matmul(self.bank[b0 + half][:], wqkv[:, m, kt, :], self.hT[:, kt, half * HALF:(half + 1) * HALF],
                        start=kt == 0, stop=kt == KT - 1)
        if n == 2 * KT - 1:
            ins.then_inc(S["proj"], 1)

    def gdn_taps(self, dve, h, W, S, t):
        dve.tensor_copy(t["taps"][:], self.par[:, bass.ds(h * 12 + PAR["gdn_conv"], 12)]).then_inc(S["taps"], 1)
        W(dve, "taps", 1)

    def gdn_conv(self, dve, W, S, t, m):
        cv, raw = t["cv"], t["raw"]
        W(dve, "raw", 2 * m + 2)
        dve.tensor_scalar(cv[:, m, :], raw[:, m, 3:3 + T], t["taps"][:, 4 * m + 3:4 * m + 4], None, ALU.mult).then_inc(S["conv"], 1)
        for k in (2, 1, 0):
            W(dve, "conv", 4 * m + 3 - k)
            dve.scalar_tensor_tensor(cv[:, m, :], raw[:, m, k:k + T], t["taps"][:, 4 * m + k:4 * m + k + 1], cv[:, m, :],
                                     ALU.mult, ALU.add).then_inc(S["conv"], 1)

    def gdn_pe(self, pe, W, W1, last, S, t):
        bank = self.bank
        ident = self.con("ident")
        col = lambda q: slice(q * P, (q + 1) * P)
        W(pe, "raw", 6)
        W(pe, "hs", 2)
        for g in range(2):
            for q in range(4):
                ins = pe.matmul(bank[4 + g][:, col(q)], t["glb"][:, 4 * g + q, :], self.con("upper"), start=True, stop=True)
            ins.then_inc(S["gcr"], 1)
        for b in range(4):
            W(pe, "sq", b // 2 + 1)
            pe.matmul(bank[b][:], self.con("ones"), t["sq"][:, b // 2, b % 2 * HALF:(b % 2 + 1) * HALF],
                      start=True, stop=True).then_inc(S["ss"], 1)
        W(pe, "qn", 2)
        for g in range(2):
            for q in range(4):
                ins = pe.transpose(bank[g][:, col(q)], t["kn"][:, 4 * g + q, :], ident)
            ins.then_inc(S["trk"], 1)
        for g in range(2):
            for q in range(4):
                k = t["kn"][:, 4 * g + q, :]
                ins = pe.matmul(bank[2 + g][:, col(q)], k, k, start=True, stop=True)
            ins.then_inc(S["kk"], 1)
        W(pe, "gr", 8)
        for g in range(2):
            for q in range(4):
                ins = pe.matmul(bank[4 + g][:, col(q)], t["qn"][:, 4 * g + q, :], t["kn"][:, 4 * g + q, :], start=True, stop=True)
            ins.then_inc(S["qk"], 1)
        W(pe, "sil", 3)
        for g in range(2):
            for q in range(4):
                ins = pe.transpose(bank[6 + g][:, col(q)], t["cv"][:, 2, (4 * g + q) * P:(4 * g + q + 1) * P], ident)
            ins.then_inc(S["trv"], 1)

        def scores_turn():
            W(pe, "kv", 6)
            for g in range(2):
                W(pe, "am", g + 1)
                for q in range(4):
                    ins = pe.transpose(bank[6 + g][:, col(q)], t["am"][:, 4 * g + q, :], ident)
                ins.then_inc(S["at"], 1)

        W(pe, "kv", 4)
        self.invert_pe(pe, W, S, t["nn"], t["upd"], t["tur"], t["ye"], 6, True, scores_turn)
        for g in range(2):
            W(pe, "i_tur", 12 + g + 1)
            for q in range(4):
                ins = pe.matmul(bank[2 + g][:, col(q)], t["tur"][:, 4 * g + q, :], t["vb"][:, 4 * g + q, :], start=True, stop=True)
            ins.then_inc(S["u"], 1)
        for g in range(2):
            for q in range(4):
                ins = pe.matmul(bank[4 + g][:, col(q)], t["kbg"][:, 4 * g + q, :], t["tur"][:, 4 * g + q, :], start=True, stop=True)
            ins.then_inc(S["wt"], 1)
        W(pe, "ate", 2)
        W(pe, "wte", 2)
        if not last:
            W1(pe, "w0", 16)
        for i in range(NG):
            W(pe, "st", i + 1)
            pe.matmul(bank[6][:, 0:P], t["wt"][:, i, :], t["st"][:, i, :], start=True, stop=True).then_inc(S["ws"], 1)
            if not last:
                self.gdn_project(pe, S, t["wqkv"], 0, 4, 2 * i)
            W(pe, "vn", i + 1)
            pe.matmul(bank[7][:, 0:P], t["kd"][:, i, :], t["vn"][:, i, :], start=True, stop=True).then_inc(S["sk"], 1)
            if not last:
                self.gdn_project(pe, S, t["wqkv"], 0, 4, 2 * i + 1)
        for g in range(2):
            for q in range(4):
                ins = pe.matmul(bank[g][:, col(q)], t["qn"][:, 4 * g + q, :], t["st"][:, 4 * g + q, :], start=True, stop=True)
            ins.then_inc(S["qs"], 1)
            for q in range(4):
                ins = pe.matmul(bank[2 + g][:, col(q)], t["at"][:, 4 * g + q, :], t["vn"][:, 4 * g + q, :], start=True, stop=True)
            ins.then_inc(S["av"], 1)
        if not last:
            W(pe, "st", 9)
            W1(pe, "w1", 16)
            for n in range(2 * KT):
                self.gdn_project(pe, S, t["wqkv"], 1, 6, n)
        W(pe, "og", 2)
        for g in range(2):
            for q in range(4):
                ins = pe.transpose(bank[g][:, col(q)], t["og"][:, 4 * g + q, :], ident)
            ins.then_inc(S["ot"], 1)
        if not last:
            W1(pe, "w2", 16)
            for n in range(2 * KT):
                self.gdn_project(pe, S, t["wqkv"], 2, 2, n)
        W(pe, "mx", 2)

    def gdn_dve(self, dve, h, W, W1, last, S, t):
        bank = self.bank
        four = lambda b: bank[b][:].rearrange("p (a b) -> p a b", a=4)
        grp = lambda a, g: a[:, 4 * g:4 * g + 4, :]
        hs, cv, raw = t["hs"], t["cv"], t["raw"]
        wide = lambda kind, g: hs[:, kind, 4 * g:4 * g + 4].unsqueeze(2).to_broadcast([P, 4, P])
        dve.tensor_copy(hs[:].rearrange("p a b -> p (a b)"), t["scal"][:, bass.ds(h, 1), :, :].rearrange("p o a b -> p (o a b)")).then_inc(S["hs"], 1)
        W(dve, "hs", 1)
        dve.tensor_copy(t["glb"], hs[:, 7, :].unsqueeze(2).to_broadcast([P, NG, P])).then_inc(S["hs"], 1)
        self.gdn_conv(dve, W, S, t, 2)
        for i in range(NG):
            W(dve, "gcr", i // 4 + 1)
            dve.tensor_scalar(t["e"][:, i, :], bank[4 + i // 4][:, i % 4 * P:(i % 4 + 1) * P], hs[:, 0, i:i + 1], 0.0,
                              ALU.subtract, ALU.max).then_inc(S["gr"], 1)
        flat8 = lambda a: a.rearrange("p a b -> p (a b)")
        for m, dst, scale in ((0, t["qn"], float(P) ** -0.5), (1, t["kn"], 1.0)):
            W(dve, "rs", m + 1)
            dve.scalar_tensor_tensor(flat8(dst), cv[:, m, :], scale, t["sq"][:, m, :], ALU.mult, ALU.mult).then_inc(S["qn"], 1)
        W(dve, "qn", 2)
        for g in range(2):
            W(dve, "trk", g + 1)
            dve.tensor_tensor(grp(t["kd"], g), four(g), wide(2, g), ALU.mult).then_inc(S["kv"], 1)
            dve.tensor_tensor(grp(t["kbg"], g), four(g), wide(3, g), ALU.mult).then_inc(S["kv"], 1)
        dve.tensor_copy(t["upd"], self.con("ident").unsqueeze(1).to_broadcast([P, NG, P])).then_inc(S["i_init"], 1)
        for i in range(NG):
            W(dve, "kk", i // 4 + 1)
            W(dve, "gm", 2 * (i // 4) + 1)
            dve.scalar_tensor_tensor(t["nn"][:, i, :], bank[2 + i // 4][:, i % 4 * P:(i % 4 + 1) * P], hs[:, 5, i:i + 1],
                                     t["es"][:, i, :], ALU.mult, ALU.mult).then_inc(S["nn"], 1)
        for g in range(2):
            W(dve, "qk", g + 1)
            W(dve, "gm", 2 * g + 2)
            dve.tensor_tensor(grp(t["am"], g), four(4 + g), grp(t["ei"], g), ALU.mult).then_inc(S["am"], 1)
        W(dve, "i_init", 1)
        m0 = self.con("lev_low")[:, 0:P].bitcast(U32).unsqueeze(1).to_broadcast([P, 4, P])
        for g in range(2):
            W(dve, "nn", 4 * g + 4)
            self.pass_gate(dve)
            dve.copy_predicated(grp(t["upd"], g), m0, grp(t["nn"], g)).then_inc(S["i_upd"], 1)
        for g in range(2):
            W(dve, "trv", g + 1)
            dve.tensor_tensor(grp(t["vb"], g), four(6 + g), wide(4, g), ALU.mult).then_inc(S["kv"], 1)
        W(dve, "i_upd", 2)
        self.invert_dve(dve, W, S, t["upd"], "lev_low", 6)
        for g in range(2):
            W(dve, "wt", g + 1)
            dve.tensor_copy(t["wt"][:, 4 * g:4 * g + 4, :].rearrange("p a b -> p (a b)"), bank[4 + g][:]).then_inc(S["wte"], 1)
        dve.memset(t["st"][:, 0, :], 0.0).then_inc(S["st"], 1)
        W(dve, "ue", 2)
        for i in range(NG):
            W(dve, "ws", i + 1)
            dve.tensor_tensor(t["vn"][:, i, :], t["u"][:, i, :], bank[6][:, 0:P], ALU.subtract).then_inc(S["vn"], 1)
            W(dve, "st", i + 1)
            W(dve, "sk", i + 1)
            dve.scalar_tensor_tensor(t["st"][:, i + 1, :], t["st"][:, i, :], hs[:, 6, i:i + 1], bank[7][:, 0:P],
                                     ALU.mult, ALU.add).then_inc(S["st"], 1)
        for g in range(2):
            W(dve, "qs", g + 1)
            dve.tensor_tensor(grp(t["osb"], g), four(g), wide(1, g), ALU.mult).then_inc(S["t1"], 1)
            W(dve, "t1", g + 1)
            W(dve, "av", g + 1)
            dve.tensor_tensor(grp(t["osb"], g), grp(t["osb"], g), four(2 + g), ALU.add).then_inc(S["o"], 1)
        W(dve, "o", 2)
        dve.tensor_tensor(t["osq"], t["osb"], t["osb"], ALU.mult).then_inc(S["osq"], 1)
        W(dve, "osq", 1)
        dve.tensor_reduce(t["ssum"][:, 0, :], t["osq"], AX, ALU.add).then_inc(S["osq"], 1)
        W(dve, "osq", 2)
        dve.tensor_scalar(t["ssum"][:, 1, :], t["ssum"][:, 0, :], 1.0 / P, EPS, ALU.mult, ALU.add).then_inc(S["osq"], 1)
        if not last:
            self.gdn_taps(dve, h + 1, W1, S, t)
            self.gdn_conv(dve, W1, S, t, 0)
        W(dve, "ol", 2)
        dve.tensor_tensor(t["og"], t["osb"], t["ssum"][:, 2, :].unsqueeze(2).to_broadcast([P, NG, P]), ALU.mult).then_inc(S["og"], 1)
        W(dve, "og", 1)
        zh = t["zs"][:, bass.ds(h, 1), :, :].rearrange("p o i v -> p (o i) v")
        dve.tensor_tensor(t["og"], t["og"], zh, ALU.mult).then_inc(S["og"], 1)
        if not last:
            self.gdn_conv(dve, W1, S, t, 1)
        W(dve, "mx", 2)

    def rwkv_stage(self):
        nc = self.nc
        K = dict(lnx=1, proj=3, raw=3, lo=3, sg=3, pp=1, car=2, xs=4, sq=1, ss=1, ln=1, rs=1, cs=1, ex=2, px=4, kp=5, rk=1, bs=1,
                 bon=1, bd=14, tr=6, tok=4, tokv=2, sc=8, am=8, i_init=1, i_turn=10, i_tur=10, i_y=10, i_ye=10, i_w=10, i_upd=12,
                 m0=1, c1=8, rh=8, c2=8, u=8, c3=8, st=8, ot=2, o=2, m1=1, oc=1, osq=1, m2=1, vl=1, vr=1, y=2, mx=1)
        with ExitStack() as c:
            f = lambda n, shape: self.sb(c, "rwkv_" + n, [P] + shape)
            H = HALF
            NCH = H // CR
            w, lw, lot = f("w", [3, KT, P]), f("lora_w", [3, P]), f("lo", [T])
            raw, xs, pp, car = f("raw", [3, 1 + H]), f("xs", [3, H]), f("par", [10]), f("carry", [3])
            sg, a, gs, rs, cs, ex, te = (f(n, [H]) for n in ("sg", "a", "g", "rs", "cs", "ex", "te"))
            pt, pin, pm, pe_ = (f(n, [H]) for n in ("pt", "pin", "pm", "pend"))
            kk, k2, b, bon, rm = (f(n, [H]) for n in ("kk", "k2", "b", "bonus", "reset"))
            kr = f("kap_r", [NCH, 2, P])
            ki, ni, vb, kh, nh = (f(n, [NCH, P]) for n in ("ki", "ni", "vbd", "kh", "nh"))
            vt, kht, nht = (f(n, [NCH, P]) for n in ("vt", "kht", "nht"))
            ak, an = f("ak", [NCH, 2, P]), f("an", [NCH, 2, P])
            upd, tur, ye, us = f("upd", [NCH, P]), kh, nh, vb
            wlo = upd
            lraw = kr[:].rearrange("p a b c -> p (a b c)")[:, 0:1 + T]
            rhs = f("rhs", [2, P])
            lnx = f("lnx", [2])
            st = f("state", [NCH + 1, P])
            o, oc, osq = sg, ex, te
            S = {n: self.sem(c, "rwkv_" + n) for n in K}
            Z = {n: self.sem(c, "rwkvz_" + n) for n in ("w", "wl", "lz", "init", "lp", "lr", "ld", "lt")}
            block = c.enter_context(nc.Block())
            win = self.i["w_in"].rearrange("(kt p) c -> p kt c", p=P)
            bank = self.bank
            col = lambda q: slice(q * P, (q + 1) * P)

            def waits(n):
                return lambda e, name, k: e.wait_ge(S[name], n * K[name] + k)

            def loops(eng, body):
                with eng.Fori(0, 3) as n:
                    body(n, n >> 1, n & 1, waits(n), waits(n + 1), False)
                body(3, 1, 1, waits(3), waits(4), True)

            @block.sync
            def _(sp):
                sp.dma_start(wlo[:], win[:, :, 3 * DA:3 * DA + P]).then_inc(Z["wl"], 16)
                sp.wait_ge(Z["lz"], 1)
                with sp.Fori(0, 2) as p:
                    for m in range(3):
                        sp.dma_start(w[:, m, :, :], win[:, :, bass.ds(p * P + m * DA, P)]).then_inc(Z["w"], 16)
                    for m, (name, r0, r1) in enumerate((("rwkv_w2", 0, 32), ("rwkv_a2", 32, 64), ("rwkv_g2", 64, 128))):
                        sp.dma_start(lw[r0:r1, m, :], self.i[name][:, bass.ds(p * P, P)]).then_inc(Z["w"], 16)
                    sp.wait_ge(S["lo"], p * 6 + 6)
                    self.pass_gate(sp)

            @block.gpsimd
            def _(pool):
                pool.memset(lw[:], 0.0).then_inc(Z["lz"], 1)
                pool.memset(lraw[:, 0:1], 0.0).then_inc(Z["init"], 1)
                pool.memset(rm[:], 1.0).then_inc(Z["init"], 1)
                pool.wait_ge(Z["init"], 2)
                pool.memset(rm[:].rearrange("p (c t) -> p c t", t=CR)[:, :, 0:1], 0.0).then_inc(Z["init"], 1)
                pool.memset(car[:], 0.0).then_inc(Z["init"], 1)
                pool.memset(st[:, NCH, :], 0.0).then_inc(Z["init"], 1)

            @block.tensor
            def _(pe):
                pe.wait_ge(Z["wl"], 16)
                for kt in range(KT):
                    for half in range(2):
                        ins = pe.matmul(bank[6 + half][:], wlo[:, kt, :], self.hT[:, kt, half * H:(half + 1) * H],
                                        start=kt == 0, stop=kt == KT - 1)
                ins.then_inc(Z["lp"], 1)
                pe.wait_ge(Z["lt"], 2)

                def project(n, k):
                    m, kt = k // KT, k % KT
                    ins = pe.matmul(bank[3 + m][:], w[:, m, kt, :], self.hT[:, kt, bass.ds((n & 1) * H, H)], start=kt == 0, stop=kt == KT - 1)
                    if kt == KT - 1:
                        ins.then_inc(S["proj"], 1)

                def low_rank(n):
                    for m in range(3):
                        pe.matmul(bank[m][:], lw[:, m, :], lot[:, bass.ds((n & 1) * H, H)], start=True, stop=True).then_inc(S["lo"], 1)

                pe.wait_ge(Z["w"], 96)
                for k in range(3 * KT):
                    project(0, k)
                low_rank(0)

                def body(n, p, hf, W, W1, last):
                    W(pe, "sq", 1)
                    pe.matmul(bank[6][:], self.con("ones64"), rs[:], start=True, stop=True).then_inc(S["ss"], 1)
                    W(pe, "rk", 1)
                    pe.matmul(bank[7][:], self.con("ones64"), b[:], start=True, stop=True).then_inc(S["bs"], 1)
                    W(pe, "raw", 3)
                    W(pe, "sg", 3)
                    for s, src in enumerate((vb, kh, nh)):
                        W(pe, "bd", 2 * s + 2)
                        for g in range(2):
                            for q in range(4):
                                ins = pe.transpose(bank[2 * s + g][:, col(q)], src[:, 4 * g + q, :], self.con("ident"))
                            ins.then_inc(S["tr"], 1)
                    W(pe, "bon", 1)
                    W(pe, "ln", 1)
                    for s, src in enumerate((ki, ni)):
                        W(pe, "bd", 2 * s + 12)
                        for g in range(4):
                            bk = (6, 7, 0, 1, 2, 3, 4, 5)[4 * s + g]
                            if bk < 6:
                                W(pe, "tokv", bk + 1) if bk < 2 else W(pe, "tok", bk - 1)
                            for q in range(2):
                                i = 2 * g + q
                                ins = pe.matmul(bank[bk][:, q * 256:(q + 1) * 256], src[:, i, :],
                                                kr[:, i, :, :].rearrange("p a b -> p (a b)"), start=True, stop=True)
                            ins.then_inc(S["sc"], 1)
                    W(pe, "am", 8)
                    self.invert_pe(pe, W, S, an[:, :, 0, :], upd, tur, ye, 5, False)
                    W(pe, "i_upd", 12)
                    W(pe, "m0", 1)
                    if not last:
                        pe.wait_ge(Z["w"], ((n + 1) >> 1) * 96 + 96)
                    for i in range(NCH):
                        if i:
                            W(pe, "st", i)
                        pe.matmul(bank[6][:, 0:P], ak[:, i, 0, :], vt[:, i, :], start=True, stop=False)
                        pe.matmul(bank[6][:, 0:P], kr[:, i, 0, :], st[:, i, :], start=False, stop=True).then_inc(S["c1"], 1)
                        if not last:
                            project(n + 1, 2 * i)
                        W(pe, "rh", i + 1)
                        pe.matmul(bank[7][:, 0:P], upd[:, i, :], rhs[:, i % 2, :], start=True, stop=True).then_inc(S["c2"], 1)
                        pe.matmul(bank[0][:, 0:P], kht[:, i, :], vt[:, i, :], start=True, stop=False)
                        W(pe, "u", i + 1)
                        pe.matmul(bank[0][:, 0:P], nht[:, i, :], us[:, i, :], start=False, stop=True).then_inc(S["c3"], 1)
                        if not last:
                            project(n + 1, 2 * i + 1)
                    for g in range(2):
                        for q in range(4):
                            i = 4 * g + q
                            pe.matmul(bank[1 + g][:, col(q)], st[:, i, :], kr[:, i, 1, :], start=True, stop=False)
                            pe.matmul(bank[1 + g][:, col(q)], vt[:, i, :], ak[:, i, 1, :], start=False, stop=False)
                            ins = pe.matmul(bank[1 + g][:, col(q)], us[:, i, :], an[:, i, 1, :], start=False, stop=True)
                        ins.then_inc(S["ot"], 1)
                    if not last:
                        for k in range(2 * KT, 3 * KT):
                            project(n + 1, k)
                    W(pe, "o", 2)
                    pe.matmul(bank[6][:], self.con("ones64"), o[:], start=True, stop=True).then_inc(S["m1"], 1)
                    if not last:
                        W(pe, "st", 8)
                        low_rank(n + 1)
                    W(pe, "osq", 1)
                    pe.matmul(bank[7][:], self.con("ones64"), osq[:], start=True, stop=True).then_inc(S["m2"], 1)
                    W(pe, "mx", 1)

                loops(pe, body)

            @block.scalar
            def _(act):
                act.wait_ge(Z["lp"], 1)
                for half in range(2):
                    act.activation(lraw[:, 1 + half * H:1 + (half + 1) * H], bank[6 + half][:], ACT.Copy).then_inc(Z["lr"], 1)
                act.wait_ge(Z["ld"], 2)
                act.activation(lot[0:32, :], lot[0:32, :], ACT.Tanh).then_inc(Z["lt"], 1)
                act.activation(lot[64:128, :], lot[64:128, :], ACT.Sigmoid).then_inc(Z["lt"], 1)

                def raw_out(W, m):
                    W(act, "proj", m + 1)
                    act.activation(raw[:, m, 1:1 + H], bank[3 + m][:], ACT.Copy).then_inc(S["raw"], 1)

                def key_squares(W):
                    W(act, "xs", 4)
                    act.activation(rs[:], xs[:, 1, :], ACT.Square, scale=pp[:, 5:6]).then_inc(S["sq"], 1)

                for m in range(3):
                    raw_out(waits(0), m)
                key_squares(waits(0))

                def body(n, p, hf, W, W1, last):
                    W(act, "pp", 1)
                    for m, dst in enumerate((sg, a)):
                        W(act, "lo", m + 1)
                        act.activation(dst[:], bank[m][:], ACT.Sigmoid, bias=pp[:, 3 + m:4 + m]).then_inc(S["sg"], 1)
                    W(act, "lo", 3)
                    act.activation(gs[:], bank[2][:], ACT.Copy).then_inc(S["sg"], 1)
                    W(act, "ss", 1)
                    act.activation(rs[:], bank[6][:], ACT.Ln, bias=EPS).then_inc(S["ln"], 1)
                    W(act, "ln", 1)
                    act.activation(rs[:], rs[:], ACT.Exp, scale=-0.5).then_inc(S["rs"], 1)
                    W(act, "ex", 2)
                    act.activation(pt[:], cs[:], ACT.Exp, scale=-EM05).then_inc(S["px"], 1)
                    act.activation(pin[:], cs[:], ACT.Exp, scale=EM05).then_inc(S["px"], 1)
                    act.activation(pm[:], ex[:], ACT.Exp, scale=-EM05).then_inc(S["px"], 1)
                    act.activation(pe_[:], te[:], ACT.Exp, scale=-EM05).then_inc(S["px"], 1)
                    for s, dst in ((1, kht), (2, nht)):
                        for g in range(2):
                            W(act, "tr", 2 * s + g + 1)
                            act.activation(dst[:, 4 * g:4 * g + 4, :].rearrange("p a b -> p (a b)"), bank[2 * s + g][:],
                                           ACT.Copy).then_inc(S["tok"], 1)
                    self.invert_act(act, W, S, tur, ye, 5, False)
                    for i in range(NCH):
                        W(act, "c1", i + 1)
                        act.activation(rhs[:, i % 2, :], bank[6][:, 0:P], ACT.Copy).then_inc(S["rh"], 1)
                        W(act, "c2", i + 1)
                        act.activation(us[:, i, :], bank[7][:, 0:P], ACT.Copy).then_inc(S["u"], 1)
                    if not last:
                        for m in range(3):
                            raw_out(W1, m)
                    W(act, "m2", 1)
                    act.activation(cs[:], bank[7][:], ACT.Ln, scale=1.0 / CR, bias=GN_EPS).then_inc(S["vl"], 1)
                    W(act, "vl", 1)
                    act.activation(cs[:], cs[:], ACT.Exp, scale=-0.5).then_inc(S["vr"], 1)
                    if not last:
                        key_squares(W1)
                    W(act, "mx", 1)

                loops(act, body)

            @block.vector
            def _(dve):
                dve.wait_ge(Z["init"], 5)
                dve.wait_ge(Z["lr"], 2)
                dve.tensor_tensor(lot[:], lraw[:, 0:T], lraw[:, 1:1 + T], ALU.subtract).then_inc(Z["ld"], 1)
                dve.wait_ge(Z["ld"], 1)
                dve.scalar_tensor_tensor(lot[:], lot[:], self.parc("mu_lo"), lraw[:, 1:1 + T], ALU.mult, ALU.add).then_inc(Z["ld"], 1)
                dve.wait_ge(Z["lt"], 2)

                ch = lambda x: x.rearrange("p (c t) -> p c t", t=CR)

                def shift(n, W):
                    dve.tensor_copy(pp[:], self.par[:, bass.ds((n >> 1) * 10 + PAR["rwkv"], 10)]).then_inc(S["pp"], 1)
                    dve.tensor_tensor(raw[:, :, 0], car[:], keep(n).to_broadcast([P, 3]), ALU.mult).then_inc(S["car"], 1)
                    W(dve, "raw", 3)
                    W(dve, "car", 1)
                    W(dve, "pp", 1)
                    dve.tensor_tensor(xs[:], raw[:, :, 0:H], raw[:, :, 1:1 + H], ALU.subtract).then_inc(S["xs"], 1)
                    dve.tensor_copy(car[:], raw[:, :, H]).then_inc(S["car"], 1)
                    W(dve, "xs", 1)
                    for m in range(3):
                        dve.scalar_tensor_tensor(xs[:, m, :], xs[:, m, :], pp[:, m:m + 1], raw[:, m, 1:1 + H],
                                                 ALU.mult, ALU.add).then_inc(S["xs"], 1)

                def keep(n):
                    return self.cons[:, bass.ds((n & 1) + CON["keep"][0], 1)]

                shift(0, waits(0))

                def body(n, p, hf, W, W1, last):
                    dve.tensor_copy(lnx[:], pp[:, 8:10]).then_inc(S["lnx"], 1)
                    dve.tensor_tensor(st[:, 0, :], st[:, NCH, :], keep(n).to_broadcast([P, P]), ALU.mult).then_inc(S["m0"], 1)
                    for g in range(2):
                        W(dve, "xs", 4)
                        dve.tensor_scalar(vb[:, :, g * CR:(g + 1) * CR], ch(xs[:, 2, :]), self.con("half")[:, g:g + 1], None,
                                          ALU.mult).then_inc(S["bd"], 1)
                    W(dve, "sg", 2)
                    dve.tensor_tensor_scan(cs[:], rm[:], sg[:], 0.0, ALU.mult, ALU.add).then_inc(S["cs"], 1)
                    W(dve, "xs", 4)
                    dve.tensor_scalar(k2[:], a[:], -1.0, pp[:, 6:7], ALU.add, ALU.mult).then_inc(S["kp"], 1)
                    dve.tensor_scalar(kk[:], xs[:, 1, :], pp[:, 5:6], None, ALU.mult).then_inc(S["kp"], 1)
                    W(dve, "cs", 1)
                    dve.tensor_tensor(ex[:], cs[:], sg[:], ALU.subtract).then_inc(S["ex"], 1)
                    c3 = cs[:].rearrange("p (c t) -> p c t", t=CR)
                    dve.tensor_tensor(te[:].rearrange("p (c t) -> p c t", t=CR), c3[:, :, CR - 1:CR].to_broadcast([P, NCH, CR]),
                                      c3, ALU.subtract).then_inc(S["ex"], 1)
                    W(dve, "kp", 2)
                    dve.scalar_tensor_tensor(k2[:], k2[:], 1.0, xs[:, 1, :], ALU.add, ALU.mult).then_inc(S["kp"], 1)
                    W(dve, "kp", 3)
                    dve.scalar_tensor_tensor(b[:], xs[:, 0, :], pp[:, 7:8], k2[:], ALU.mult, ALU.mult).then_inc(S["rk"], 1)
                    W(dve, "rs", 1)
                    dve.tensor_tensor(kk[:], kk[:], rs[:], ALU.mult).then_inc(S["kp"], 1)
                    W(dve, "bs", 1)
                    dve.tensor_tensor(bon[:], bank[7][:], xs[:, 2, :], ALU.mult).then_inc(S["bon"], 1)
                    W(dve, "kp", 4)
                    dve.tensor_tensor(b[:], kk[:], a[:], ALU.mult).then_inc(S["kp"], 1)
                    W(dve, "kp", 5)
                    W(dve, "px", 4)
                    plus, minus = self.con("half"), self.con("nhalf")
                    for dst, src, sign, dec in ((kh, k2[:], plus, pe_), (nh, b[:], minus, pe_), (kr[:, :, 0, :], kk[:], plus, pm),
                                                (kr[:, :, 1, :], xs[:, 0, :], plus, pt), (ki, k2[:], plus, pin), (ni, b[:], minus, pin)):
                        for g in range(2):
                            dve.scalar_tensor_tensor(dst[:, :, g * CR:(g + 1) * CR], ch(src), sign[:, g:g + 1], ch(dec[:]),
                                                     ALU.mult, ALU.mult).then_inc(S["bd"], 1)
                    dve.tensor_copy(upd[:], self.con("ident").unsqueeze(1).to_broadcast([P, NCH, P])).then_inc(S["i_init"], 1)
                    for g in range(2):
                        W(dve, "tr", g + 1)
                        dve.tensor_copy(vt[:, 4 * g:4 * g + 4, :].rearrange("p a b -> p (a b)"), bank[g][:]).then_inc(S["tokv"], 1)
                    a0 = CON["up64_strict"][0]
                    mask = self.cons[:, a0:a0 + 2 * P].unsqueeze(1).to_broadcast([P, 2, 2 * P])
                    for s, dst in enumerate((ak, an)):
                        for g in range(4):
                            bk = (6, 7, 0, 1, 2, 3, 4, 5)[4 * s + g]
                            W(dve, "sc", 4 * s + g + 1)
                            dve.tensor_tensor(dst[:, 2 * g:2 * g + 2, :, :].rearrange("p a b c -> p a (b c)"),
                                              bank[bk][:].rearrange("p (a b) -> p a b", a=2), mask, ALU.mult).then_inc(S["am"], 1)
                    W(dve, "am", 8)
                    W(dve, "i_init", 1)
                    m0 = self.con("lev_up")[:, 0:P].bitcast(U32).unsqueeze(1).to_broadcast([P, 4, P])
                    for g in range(2):
                        self.pass_gate(dve)
                        dve.copy_predicated(upd[:, 4 * g:4 * g + 4, :], m0, an[:, 4 * g:4 * g + 4, 0, :]).then_inc(S["i_upd"], 1)
                    W(dve, "i_upd", 2)
                    self.invert_dve(dve, W, S, upd, "lev_up", 5)
                    for i in range(NCH):
                        W(dve, "c3", i + 1)
                        W(dve, "st", i) if i else W(dve, "m0", 1)
                        dve.scalar_tensor_tensor(st[:, i + 1, :], st[:, i, :], pt[:, i * CR + CR - 1:i * CR + CR], bank[0][:, 0:P],
                                                 ALU.mult, ALU.add).then_inc(S["st"], 1)
                    for g in range(2):
                        W(dve, "ot", g + 1)
                        dve.tensor_reduce(o[:, g * 256:(g + 1) * 256].rearrange("p (c t) -> p c t", t=CR),
                                          bank[1 + g][:].rearrange("p (c g t) -> p c t g", g=2, t=CR), AX, ALU.add).then_inc(S["o"], 1)
                    W(dve, "m1", 1)
                    dve.scalar_tensor_tensor(oc[:], bank[6][:], -1.0 / CR, o[:], ALU.mult, ALU.add).then_inc(S["oc"], 1)
                    W(dve, "oc", 1)
                    dve.tensor_tensor(osq[:], oc[:], oc[:], ALU.mult).then_inc(S["osq"], 1)
                    W(dve, "lnx", 1)
                    if not last:
                        shift(n + 1, W1)
                    W(dve, "vr", 1)
                    dve.scalar_tensor_tensor(oc[:], oc[:], lnx[:, 0:1], cs[:], ALU.mult, ALU.mult).then_inc(S["y"], 1)
                    W(dve, "y", 1)
                    dve.scalar_tensor_tensor(oc[:], oc[:], lnx[:, 1:2], bon[:], ALU.add, ALU.add).then_inc(S["y"], 1)
                    W(dve, "y", 2)
                    dve.tensor_tensor(self.mixT[:, bass.ds(p, 1), bass.ds(hf * H, H)], oc[:].unsqueeze(1), gs[:].unsqueeze(1),
                                      ALU.mult).then_inc(S["mx"], 1)

                loops(dve, body)

    def route_stage(self):
        nc = self.nc
        with ExitStack() as c:
            f = lambda n, shape, dt=F32: self.sb(c, "rt_" + n, [P] + shape, dt)
            wo = f("w_out", [KT, D])
            x2 = self.x2
            h2 = f("h2", [2, D])
            h2t = f("h2t", [2, KT, P])
            sq = f("sq", [D])
            gain = f("gain", [D])
            wr = f("w_router", [KT, 36])
            mb = f("bias", [36])
            ss, rs = f("ss", [NT]), f("rs", [NT])
            lg = f("logits", [NT, 36])
            S = {n: self.sem(c, "rt_" + n) for n in (
                "w", "x", "small", "prod", "x2", "ss", "ms", "rc", "rt", "h2", "turn", "turned", "log", "lg",
                "step", "ex", "cum", "oh", "slot", "gd", "vd")}
            ST = [self.sem(c, f"rt_stored{j}") for j in range(2)]
            sm = f("small", [24, NT])
            g4 = f("g4", [4, NT, 4])
            me = f("masked", [NT, 4, 8])
            el = f("el", [NT, 8])
            top = f("top", [NT, 8])
            topi = f("topi", [NT, 8], U32)
            eid = f("eid", [NT, 2])
            oh = f("onehot", [NT, 2, E])
            ohs = f("onehots", [NT, E])
            run = f("run", [NT + 1, E])
            rank = f("rank", [NT, E])
            tmp = sq[:, 4 * P:4 * P + NT * 2 * E].rearrange("p (i k e) -> p i k e", k=2, e=E)
            ov = f("ov", [8, E])
            cmp7 = f("cmp7", [E, 7])
            cmpb = f("cmpb", [NOV, E])
            dst = f("dst", [NT * 2])
            dsti = f("dsti", [NT * 2], U32)
            blki = f("blki", [NT * 2], U32)
            sloti = f("sloti", [NT * 2], U32)
            blkf, slotf, val = f("blkf", [NT * 2]), f("slotf", [NT * 2]), f("val", [NT * 2])
            rr = sq[:, 0:4 * P].rearrange("p (n s) -> p n s", n=4)
            bt = f("blk_onehot", [4, NBLK])
            vs = f("vs", [2, NBLK])
            bef = f("bef", [NOV + 1])
            block = c.enter_context(nc.Block())
            bank = self.bank
            xv = self.i["x"].rearrange("(i p) d -> p i d", p=P)

            @block.sync
            def _(sp):
                wv = self.i["w_out"].rearrange("(kt p) n -> p kt n", p=P)
                for q in range(4):
                    sp.dma_start(wo[:, 2 * q:2 * q + 2, :], wv[:, 2 * q:2 * q + 2, :]).then_inc(S["w"], 16)
                for q in range(2):
                    sp.dma_start(x2[:, 4 * q:4 * q + 4, :], xv[:, 4 * q:4 * q + 4, :]).then_inc(S["x"], 16)
                sp.dma_start(gain[:], self.i["norm_ffn_row"].partition_broadcast(P)).then_inc(S["small"], 16)
                sp.dma_start(mb[:], self.i["moe_b"].partition_broadcast(P)).then_inc(S["small"], 16)
                sp.dma_start(wr[:, :, 0:4], self.i["moe_w_group"].rearrange("(kt p) n -> p kt n", p=P)).then_inc(S["small"], 16)
                sp.dma_start(wr[:, :, 4:36], self.i["moe_w_expert"].rearrange("(kt p) n -> p kt n", p=P)).then_inc(S["small"], 16)
                for j in range(NEARLY):
                    self.load_expert(sp, j, (self.gu_early[:, j], self.dn_early[:, j]), self.w_landed[j])
                for i in range(NT):
                    sp.wait_ge(S["h2"], i + 1)
                    sp.dma_start(self.h2d[i * P:(i + 1) * P, :], h2[:, i % 2, :]).then_inc(ST[i % 2], 16)
                for j in range(2):
                    sp.wait_ge(ST[j], 16 * (NT // 2))

            @block.gpsimd
            def _(pool):
                pool.memset(self.xg_early[:], 0.0)

            @block.tensor
            def _(pe):
                pe.wait_ge(S["w"], 64)

                def turn(i):
                    pe.wait_ge(S["h2"], i + 1)
                    if i:
                        pe.wait_ge(S["turned"], 2 * i)
                    for kt in range(KT):
                        ins = pe.transpose(bank[4 + kt // 4][:, kt % 4 * P:(kt % 4 + 1) * P], h2[:, i % 2, kt * P:(kt + 1) * P],
                                           self.con("ident"))
                        if kt % 4 == 3:
                            ins.then_inc(S["turn"], 1)

                def logits(i):
                    pe.wait_ge(S["small"], 64)
                    pe.wait_ge(S["turned"], 2 * i + 2)
                    if i >= 2:
                        pe.wait_ge(S["lg"], i - 1)
                    for kt in range(KT):
                        ins = pe.matmul(bank[6 + i % 2][:, 0:36], h2t[:, i % 2, kt, :], wr[:, kt, :], start=kt == 0, stop=kt == KT - 1)
                    ins.then_inc(S["log"], 1)

                for i in range(NT + 3):
                    if i < NT:
                        for kt in range(KT):
                            for half in range(2):
                                if kt == 0 and i >= 2:
                                    pe.wait_ge(S["x2"], 2 * (i - 2) + half + 1)
                                ins = pe.matmul(bank[2 * (i % 2) + half][:], self.mixT[:, kt, i * P:(i + 1) * P],
                                                wo[:, kt, half * HALF:(half + 1) * HALF], start=kt == 0, stop=kt == KT - 1)
                        ins.then_inc(S["prod"], 1)
                    if 2 <= i < NT + 2:
                        turn(i - 2)
                    if i >= 3:
                        logits(i - 3)
                pe.wait_ge(S["oh"], 1)
                o = ohs[:].rearrange("p i e -> p (i e)")
                pe.matmul(bank[0][:, 0:NT * E], self.con("below"), o, start=True, stop=True)
                pe.matmul(bank[1][:, 0:NT * E], self.con("ones"), o, start=True, stop=True).then_inc(S["cum"], 1)
                for n in range(2 * NT):
                    pe.wait_ge(S["slot"], 2 * n + 2)
                    pe.matmul(bank[2][:, 0:NBLK], rr[:, n % 4, :], bt[:, n % 4, :], start=n == 0, stop=n == 2 * NT - 1).then_inc(S["cum"], 1)

            @block.scalar
            def _(act):
                for i in range(NT + 1):
                    if i < NT:
                        act.wait_ge(S["x2"], 2 * i + 2)
                        if i:
                            act.wait_ge(S["ss"], i)
                        act.activation(sq[:], x2[:, i, :], ACT.Square, accum_out=ss[:, i:i + 1]).then_inc(S["ss"], 1)
                        act.wait_ge(S["rc"], i + 1)
                        act.activation(rs[:, i:i + 1], rs[:, i:i + 1], ACT.Sqrt).then_inc(S["rt"], 1)
                    if i >= 1:
                        for b in range(2):
                            act.wait_ge(S["turn"], 2 * (i - 1) + b + 1)
                            if i >= 3:
                                act.wait_ge(S["log"], i - 2)
                            act.activation(h2t[:, (i - 1) % 2, 4 * b:4 * b + 4, :].rearrange("p a b -> p (a b)"), bank[4 + b][:],
                                           ACT.Copy).then_inc(S["turned"], 1)
                act.wait_ge(S["gd"], 1)
                act.activation(g4[:, 3, :, :], g4[:, 3, :, :], ACT.Exp).then_inc(S["ex"], 1)
                act.wait_ge(S["vd"], 1)
                act.activation(sm[:, 6, :], sm[:, 5, :], ACT.Exp).then_inc(S["ex"], 1)

            @block.vector
            def _(dve):
                dve.wait_ge(S["x"], 32)
                dve.wait_ge(S["small"], 64)

                def logits_out(i):
                    dve.wait_ge(S["log"], i + 1)
                    dve.tensor_tensor(lg[:, i, :], bank[6 + i % 2][:, 0:36], mb[:], ALU.add).then_inc(S["lg"], 1)

                for i in range(NT):
                    dve.wait_ge(S["prod"], i + 1)
                    for half in range(2):
                        xs = x2[:, i, half * HALF:(half + 1) * HALF]
                        dve.tensor_tensor(xs, bank[2 * (i % 2) + half][:], xs, ALU.add).then_inc(S["x2"], 1)
                    dve.wait_ge(S["ss"], i + 1)
                    dve.tensor_scalar(rs[:, i:i + 1], ss[:, i:i + 1], 1.0 / D, EPS, ALU.mult, ALU.add).then_inc(S["ms"], 1)
                    dve.wait_ge(S["ms"], i + 1)
                    dve.reciprocal(rs[:, i:i + 1], rs[:, i:i + 1]).then_inc(S["rc"], 1)
                    dve.wait_ge(S["rt"], i + 1)
                    if i >= 2:
                        dve.wait_ge(S["turn"], 2 * (i - 2) + 2)
                        dve.wait_ge(ST[i % 2], 16 * (i // 2))
                    dve.scalar_tensor_tensor(h2[:, i % 2, :], x2[:, i, :], rs[:, i:i + 1], gain[:], ALU.mult, ALU.mult).then_inc(S["h2"], 1)
                    if i >= 3:
                        logits_out(i - 3)
                for i in range(NT - 3, NT):
                    logits_out(i)
                dve.wait_ge(S["lg"], NT)
                step = Step(dve, S["step"])
                b4 = lambda a: a.unsqueeze(2).to_broadcast([P, NT, 4])
                grp = lg[:, :, 0:4]
                step(dve.tensor_reduce(sm[:, 0, :], grp, AX, ALU.max))
                dve.tensor_tensor(g4[:, 3, :, :], grp, b4(sm[:, 0, :]), ALU.subtract).then_inc(S["gd"], 1)
                step(dve.tensor_tensor(g4[:, 0, :, :], grp, b4(sm[:, 0, :]), ALU.is_equal))
                step(dve.tensor_tensor(g4[:, 1, :, :], g4[:, 0, :, :], self.con("idx4").unsqueeze(1).to_broadcast([P, NT, 4]), ALU.mult))
                step(dve.tensor_reduce(sm[:, 1, :], g4[:, 1, :, :], AX, ALU.max))
                step(dve.tensor_tensor(g4[:, 2, :, :], g4[:, 1, :, :], b4(sm[:, 1, :]), ALU.is_equal))
                step(dve.tensor_scalar(sm[:, 2, :], sm[:, 1, :], -8.0, 32.0, ALU.mult, ALU.add))
                step(dve.tensor_tensor(me[:], lg[:, :, 4:36].rearrange("p i (g e) -> p i g e", g=4),
                                       g4[:, 2, :, :].unsqueeze(3).to_broadcast([P, NT, 4, 8]), ALU.mult))
                step(dve.tensor_reduce(el[:], me[:].rearrange("p i g e -> p i e g"), AX, ALU.add))
                for i in range(NT):
                    step.inc(dve.max(top[:, i, :], el[:, i, :]))
                step.wait()
                dve.tensor_tensor(sm[:, 5, :], top[:, :, 1], top[:, :, 0], ALU.subtract).then_inc(S["vd"], 1)
                for i in range(NT):
                    step.inc(dve.max_index(topi[:, i, :], top[:, i, :], el[:, i, :]))
                step.wait()
                step(dve.tensor_copy(eid[:], topi[:, :, 0:2]))
                step(dve.tensor_tensor(eid[:], eid[:], sm[:, 2, :].unsqueeze(2).to_broadcast([P, NT, 2]), ALU.add))
                step(dve.tensor_tensor(oh[:].rearrange("p i k e -> p (i k) e"), self.con("iota_e").unsqueeze(1).to_broadcast([P, 2 * NT, E]),
                                       eid[:].rearrange("p i k -> p (i k)").unsqueeze(2).to_broadcast([P, 2 * NT, E]), ALU.is_equal))
                dve.tensor_tensor(ohs[:], oh[:, :, 0, :], oh[:, :, 1, :], ALU.add).then_inc(S["oh"], 1)
                dve.wait_ge(S["ex"], 2)
                step(dve.tensor_reduce(sm[:, 7, :], g4[:, 3, :, :], AX, ALU.add))
                step(dve.tensor_scalar(sm[:, 8, :], sm[:, 6, :], 1.0, None, ALU.add))
                step(dve.tensor_tensor(sm[:, 8, :], sm[:, 8, :], sm[:, 7, :], ALU.mult))
                step(dve.reciprocal(self.gates12[:, 0, :], sm[:, 8, :]))
                step(dve.tensor_tensor(self.gates12[:, 1, :], self.gates12[:, 0, :], sm[:, 6, :], ALU.mult))
                dve.wait_ge(S["cum"], 1)
                step(dve.memset(run[:, 0, :], 0.0))
                for i in range(NT):
                    step(dve.tensor_tensor(run[:, i + 1, :], run[:, i, :], bank[1][:, i * E:(i + 1) * E], ALU.add))
                step(dve.tensor_tensor(rank[:], run[:, 0:NT, :], bank[0][:, 0:NT * E].rearrange("p (i e) -> p i e", e=E), ALU.add))
                cnt = run[:, NT, :]
                step(dve.tensor_tensor(cmp7[:], cnt.unsqueeze(2).to_broadcast([P, E, 7]), self.con("j128").unsqueeze(1).to_broadcast([P, E, 7]),
                                       ALU.is_gt))
                step(dve.tensor_reduce(ov[:, 0, :], cmp7[:], AX, ALU.add))
                step(dve.tensor_tensor_scan(ov[:, 1, :], self.con("ones")[:, 0:E], ov[:, 0, :], 0.0, ALU.mult, ALU.add))
                step(dve.tensor_tensor(ov[:, 2, :], ov[:, 1, :], ov[:, 0, :], ALU.subtract))
                step(dve.tensor_scalar(ov[:, 3, :], ov[:, 2, :], float(P), float(P * (E - 1)), ALU.mult, ALU.add))
                step(dve.tensor_tensor(ov[:, 3, :], ov[:, 3, :], self.con("iota_e128"), ALU.subtract))
                step(dve.tensor_scalar(tmp[:, :, 0, :], rank[:], float(P), None, ALU.is_ge))
                step(dve.tensor_tensor(tmp[:, :, 0, :], tmp[:, :, 0, :], ov[:, 3, :].unsqueeze(1).to_broadcast([P, NT, E]), ALU.mult))
                step(dve.tensor_tensor(rank[:], rank[:], tmp[:, :, 0, :], ALU.add))
                step(dve.tensor_tensor(rank[:], rank[:], self.con("iota_e128").unsqueeze(1).to_broadcast([P, NT, E]), ALU.add))
                step(dve.tensor_tensor(tmp[:], oh[:], rank[:].unsqueeze(2).to_broadcast([P, NT, 2, E]), ALU.mult))
                step(dve.tensor_reduce(dst[:], tmp[:].rearrange("p i k e -> p (i k) e"), AX, ALU.add))
                step(dve.tensor_copy(dsti[:], dst[:]))
                step(dve.tensor_scalar(blki[:], dsti[:], 7, None, ALU.logical_shift_right))
                step(dve.tensor_scalar(sloti[:], dsti[:], P - 1, None, ALU.bitwise_and))
                step(dve.tensor_copy(blkf[:], blki[:]))
                step(dve.tensor_copy(slotf[:], sloti[:]))
                for k in range(2):
                    step(dve.tensor_scalar(val[:].rearrange("p (i k) -> p i k", k=2)[:, :, k], self.con("iota_tok"), 2.0, 1.0 + k, ALU.mult, ALU.add))
                for n in range(2 * NT):
                    if n >= 4:
                        dve.wait_ge(S["cum"], n - 2)
                    dve.tensor_scalar(rr[:, n % 4, :], self.con("iota128"), slotf[:, n:n + 1], None, ALU.is_equal).then_inc(S["slot"], 1)
                    dve.tensor_scalar(bt[:, n % 4, :], self.con("iota_blk"), blkf[:, n:n + 1], val[:, n:n + 1], ALU.is_equal,
                                      ALU.mult).then_inc(S["slot"], 1)
                step(dve.tensor_tensor(cmpb[:], ov[:, 1, :].unsqueeze(1).to_broadcast([P, NOV, E]),
                                       self.con("iota_blk")[:, 0:NOV].unsqueeze(2).to_broadcast([P, NOV, E]), ALU.is_le))
                step(dve.tensor_reduce(bef[:, 0:NOV], cmpb[:], AX, ALU.add))
                step(dve.tensor_scalar(bef[:, 0:NOV], bef[:, 0:NOV], float(E - 1), None, ALU.min))
                step(dve.tensor_copy(bef[:, NOV:NOV + 1], ov[:, 1, E - 1:E]))
                step(dve.tensor_copy(self.extra[:], bef[:]))
                dve.wait_ge(S["cum"], 1 + 2 * NT)
                step(dve.tensor_scalar(vs[:, 0, :], bank[2][:, 0:NBLK], 0.0, 8192.0, ALU.is_equal, ALU.mult))
                step(dve.scalar_tensor_tensor(vs[:, 1, :], bank[2][:, 0:NBLK], -1.0, vs[:, 0, :], ALU.add, ALU.add))
                step(dve.tensor_copy(self.slot_to[:], vs[:, 1, :]))
                step(dve.tensor_scalar(self.slot_from[:], self.slot_to[:], 1, None, ALU.logical_shift_right))

    def load_expert(self, eng, e, w, sem):
        for name, dst in (("moe_w_gate", w[0][:, :, 0:DE]), ("moe_w_up", w[0][:, :, DE:2 * DE]), ("moe_w_down", w[1])):
            eng.dma_start(dst, self.i[name][bass.ds(e, 1), :, :].rearrange("o (kt p) n -> p (o kt) n", p=P)).then_inc(sem, 16)

    def expert_stage(self):
        nc = self.nc
        with ExitStack() as c:
            f = lambda n, shape, dt=F32: self.sb(c, "ex_" + n, [P] + shape, dt)
            gu_late = self.mixT[:].rearrange("p (j a) (b n) -> p j (a b) n", j=NR - NEARLY, n=2 * DE)
            dn_late = f("w_down", [NR - NEARLY, 2, D])
            W = [(self.gu_early[:, j], self.dn_early[:, j]) for j in range(NEARLY)]
            W += [(gu_late[:, j], dn_late[:, j]) for j in range(NR - NEARLY)]
            xg_late = f("x", [2, D])
            xg = [self.xg_early[:, j, :] for j in range(2)] + [xg_late[:, j, :] for j in range(2)]
            xt = f("xt", [2, KT, P])
            si, hid, ht, yo = f("silu", [DE]), f("hid", [DE]), f("hid_t", [2, P]), f("y", [2, D])
            ifrom, ito = f("from", [NR], U32), f("to", [2], U32)
            names = ("turn", "ta", "tv", "gu", "si", "hid", "ht", "htc", "dn", "ya", "yv", "ix", "init")
            S = {n: self.sem(c, "ex_" + n) for n in names}
            WL = self.w_landed
            GA = [self.sem(c, f"ex_gathered{j}") for j in range(NR)]
            SC = [self.sem(c, f"ex_scattered{j}") for j in range(2)]
            V = {n: self.sem(c, "ov_" + n) for n in names + ("w", "ga", "sc")}
            block = c.enter_context(nc.Block())
            bank = self.bank
            later = lambda e, n: not (isinstance(e, int) and e < n)
            exists = lambda e: not (isinstance(e, int) and e >= E)

            def gather(pool, b, sem):
                pool.indirect_dma_start(xg[b], None, self.h2d, bass.IndirectOffsetOnAxis(ap=ifrom[:, b:b + 1], axis=0),
                                        bounds_check=T - 1, oob_is_err=False).then_inc(sem, 16)

            def scatter(pool, b, sem):
                pool.indirect_dma_start(self.yd, bass.IndirectOffsetOnAxis(ap=ito[:, b:b + 1], axis=0), yo[:, b, :], None,
                                        bounds_check=2 * T - 1, oob_is_err=False).then_inc(sem, 16)

            def turns(eng, body):
                body(0)
                with eng.Fori(1, E // NR - 1) as it:
                    body(it)
                body(E // NR - 1)

            def further(eng, body):
                n = eng.value_load(self.extra[0:1, NOV:NOV + 1], min_val=0, max_val=NOV)
                with eng.If(n > 0):
                    with eng.Fori(0, NOV) as b:
                        body(b)

            @block.sync
            def _(sp):
                for j in range(NEARLY, NR):
                    self.load_expert(sp, j, W[j], WL[j])
                with sp.Fori(1, E // NR) as it:
                    for j in range(NR):
                        sp.wait_ge(S["dn"], (it - 1) * (2 * NR) + 2 * j + 2)
                        self.load_expert(sp, it * NR + j, W[j], WL[j])

                def body(b):
                    e = sp.value_load(self.extra[0:1, bass.ds(b, 1)], min_val=0, max_val=E - 1)
                    self.load_expert(sp, e, W[0], V["w"])
                    sp.wait_ge(V["dn"], b * 2 + 2)
                    self.pass_gate(sp)

                sp.wait_ge(S["dn"], 2 * E)
                further(sp, body)

            @block.gpsimd
            def _(pool):
                def fetch(e, j, n):
                    pool.tensor_copy(ifrom[:, j:j + 1], self.slot_from[:, bass.ds(e, 1)]).then_inc(S["ix"], 1)
                    pool.wait_ge(S["ix"], n)
                    self.pass_gate(pool)
                    gather(pool, j, GA[j])

                for j in range(NR):
                    if j == 2:
                        pool.memset(xg_late[:], 0.0).then_inc(S["init"], 1)
                        pool.wait_ge(S["init"], 1)
                    fetch(j, j, j + 1)

                def body(it):
                    last = isinstance(it, int) and it == E // NR - 1
                    for j in range(NR):
                        e, b = it * NR + j, j % 2
                        n = NR + 2 * e + 1
                        if last:
                            n = NR + 2 * NR * it + j
                        else:
                            pool.wait_ge(S["turn"], (e + 1) * 2)
                            pool.wait_ge(GA[j], 16 * (it + 1))
                            fetch(e + NR, j, n)
                        if later(e, 2):
                            pool.wait_ge(SC[b], 16 * (it * 2 + j // 2))
                            self.pass_gate(pool)
                        pool.tensor_copy(ito[:, b:b + 1], self.slot_to[:, bass.ds(e, 1)]).then_inc(S["ix"], 1)
                        pool.wait_ge(S["ix"], n + 1)
                        self.pass_gate(pool)
                        pool.wait_ge(S["ya"], e + 1)
                        pool.wait_ge(S["yv"], e + 1)
                        self.pass_gate(pool)
                        scatter(pool, b, SC[b])

                turns(pool, body)
                for b in range(2):
                    pool.wait_ge(SC[b], 16 * (E // 2))

                def over(b):
                    pool.tensor_copy(ifrom[:, 0:1], self.slot_from[:, bass.ds(b + E, 1)]).then_inc(V["ix"], 1)
                    pool.tensor_copy(ito[:, 0:1], self.slot_to[:, bass.ds(b + E, 1)]).then_inc(V["ix"], 1)
                    pool.wait_ge(V["ix"], 2 * b + 2)
                    self.pass_gate(pool)
                    gather(pool, 0, V["ga"])
                    pool.wait_ge(V["ya"], b + 1)
                    pool.wait_ge(V["yv"], b + 1)
                    self.pass_gate(pool)
                    scatter(pool, 0, V["sc"])
                    pool.wait_ge(V["sc"], 16 * b + 16)
                    pool.wait_ge(V["ga"], 16 * b + 16)
                    self.pass_gate(pool)

                pool.wait_ge(S["turn"], 2 * E)
                further(pool, over)

            def pe_turn(pe, b, sem):
                for kt in range(KT):
                    ins = pe.transpose(bank[4 + kt // 4][:, kt % 4 * P:(kt % 4 + 1) * P], xg[b][:, kt * P:(kt + 1) * P], self.con("ident"))
                    if kt % 4 == 3:
                        ins.then_inc(sem, 1)

            def pe_up(pe, b, w, gb, sem):
                for kt in range(KT):
                    ins = pe.matmul(bank[gb][:], xt[:, b, kt, :], W[w][0][:, kt, :], start=kt == 0, stop=kt == KT - 1)
                ins.then_inc(sem, 1)

            def pe_hid(pe, sem):
                for q in range(2):
                    ins = pe.transpose(bank[6][:, q * P:(q + 1) * P], hid[:, q * P:(q + 1) * P], self.con("ident"))
                ins.then_inc(sem, 1)

            def pe_down(pe, w, sem):
                for half in range(2):
                    for q in range(2):
                        ins = pe.matmul(bank[2 + half][:], ht[:, q, :], W[w][1][:, q, half * HALF:(half + 1) * HALF], start=q == 0, stop=q == 1)
                    ins.then_inc(sem, 1)

            @block.tensor
            def _(pe):
                pe.wait_ge(GA[0], 16)
                pe_turn(pe, 0, S["turn"])
                pe.wait_ge(WL[0], 48)
                pe.wait_ge(S["ta"], 1)
                pe.wait_ge(S["tv"], 1)
                pe_up(pe, 0, 0, 0, S["gu"])
                pe.wait_ge(GA[1], 16)
                pe_turn(pe, 1, S["turn"])

                def body(it):
                    for j in range(NR):
                        e = it * NR + j
                        if exists(e + 1):
                            pe.wait_ge(WL[(j + 1) % NR], 48 * (it + 1 + (j + 1) // NR))
                            pe.wait_ge(S["ta"], e + 2)
                            pe.wait_ge(S["tv"], e + 2)
                            pe_up(pe, (j + 1) % 2, (j + 1) % NR, (j + 1) % 2, S["gu"])
                        pe.wait_ge(S["hid"], e + 1)
                        pe_hid(pe, S["ht"])
                        if exists(e + 2):
                            pe.wait_ge(GA[(j + 2) % NR], 16 * (it + 1 + (j + 2) // NR))
                            pe_turn(pe, (j + 2) % NR, S["turn"])
                        pe.wait_ge(S["htc"], e + 1)
                        if later(e, 1):
                            pe.wait_ge(S["ya"], e)
                            pe.wait_ge(S["yv"], e)
                        pe_down(pe, j, S["dn"])

                turns(pe, body)
                pe.wait_ge(S["ya"], E)
                pe.wait_ge(S["yv"], E)

                def over(b):
                    pe.wait_ge(V["ga"], 16 * b + 16)
                    pe_turn(pe, 0, V["turn"])
                    pe.wait_ge(V["w"], 48 * b + 48)
                    pe.wait_ge(V["ta"], b + 1)
                    pe.wait_ge(V["tv"], b + 1)
                    pe_up(pe, 0, 0, 0, V["gu"])
                    pe.wait_ge(V["hid"], b + 1)
                    pe_hid(pe, V["ht"])
                    pe.wait_ge(V["htc"], b + 1)
                    pe_down(pe, 0, V["dn"])
                    pe.wait_ge(V["ya"], b + 1)
                    pe.wait_ge(V["yv"], b + 1)
                    self.pass_gate(pe)

                further(pe, over)

            def act_turned(act, b, q, n, SS):
                act.wait_ge(SS["turn"], n)
                act.activation(xt[:, b, 0:4, :].rearrange("p a b -> p (a b)"), bank[4][:], ACT.Copy).then_inc(SS["ta"], 1)

            @block.scalar
            def _(act):
                for e in range(2):
                    act_turned(act, e, 0, 2 * e + 1, S)

                def body(it):
                    for j in range(NR):
                        e = it * NR + j
                        act.wait_ge(S["gu"], e + 1)
                        act.activation(si[:], bank[j % 2][:, 0:DE], ACT.Silu).then_inc(S["si"], 1)
                        if exists(e + 2):
                            act_turned(act, j % 2, 0, 2 * e + 5, S)
                        act.wait_ge(S["dn"], 2 * e + 1)
                        if later(e, 2):
                            act.wait_ge(SC[j % 2], 16 * (it * 2 + j // 2))
                        act.activation(yo[:, j % 2, 0:HALF], bank[2][:], ACT.Copy).then_inc(S["ya"], 1)

                turns(act, body)

                def over(b):
                    act_turned(act, 0, 0, 2 * b + 1, V)
                    act.wait_ge(V["gu"], b + 1)
                    act.activation(si[:], bank[0][:, 0:DE], ACT.Silu).then_inc(V["si"], 1)
                    act.wait_ge(V["dn"], 2 * b + 1)
                    act.activation(yo[:, 0, 0:HALF], bank[2][:], ACT.Copy).then_inc(V["ya"], 1)

                act.wait_ge(SC[0], 16 * (E // 2))
                further(act, over)

            def dve_turned(dve, b, n, SS):
                dve.wait_ge(SS["turn"], n)
                dve.tensor_copy(xt[:, b, 4:8, :].rearrange("p a b -> p (a b)"), bank[5][:]).then_inc(SS["tv"], 1)

            def dve_hid(dve, gb, n, SS):
                dve.wait_ge(SS["si"], n)
                dve.tensor_tensor(hid[:], si[:], bank[gb][:, DE:2 * DE], ALU.mult).then_inc(SS["hid"], 1)

            @block.vector
            def _(dve):
                for e in range(2):
                    dve_turned(dve, e, 2 * e + 2, S)

                def body(it):
                    for j in range(NR):
                        e = it * NR + j
                        dve_hid(dve, j % 2, e + 1, S)
                        dve.wait_ge(S["ht"], e + 1)
                        dve.tensor_copy(ht[:].rearrange("p a b -> p (a b)"), bank[6][:, 0:2 * P]).then_inc(S["htc"], 1)
                        if exists(e + 2):
                            dve_turned(dve, j % 2, 2 * e + 6, S)
                        dve.wait_ge(S["dn"], 2 * e + 2)
                        if later(e, 2):
                            dve.wait_ge(SC[j % 2], 16 * (it * 2 + j // 2))
                        dve.tensor_copy(yo[:, j % 2, HALF:D], bank[3][:]).then_inc(S["yv"], 1)

                turns(dve, body)

                def over(b):
                    dve_turned(dve, 0, 2 * b + 2, V)
                    dve_hid(dve, 0, b + 1, V)
                    dve.wait_ge(V["ht"], b + 1)
                    dve.tensor_copy(ht[:].rearrange("p a b -> p (a b)"), bank[6][:, 0:2 * P]).then_inc(V["htc"], 1)
                    dve.wait_ge(V["dn"], 2 * b + 2)
                    dve.tensor_copy(yo[:, 0, HALF:D], bank[3][:]).then_inc(V["yv"], 1)

                dve.wait_ge(SC[0], 16 * (E // 2))
                further(dve, over)

    def final_stage(self):
        nc = self.nc
        with ExitStack() as c:
            y = self.sb(c, "fin_y", [P, NT, 2, D])
            gain = self.sb(c, "fin_gain", [P, D])
            sq = self.sb(c, "fin_sq", [P, D])
            ss = self.sb(c, "fin_ss", [P, NT])
            x2 = self.x2
            S = {n: self.sem(c, "fin_" + n) for n in ("g", "a", "b", "ss", "ms", "rc", "rt", "o", "out")}
            Y = [self.sem(c, f"fin_y{i}") for i in range(NT)]
            block = c.enter_context(nc.Block())
            yv = self.yd.rearrange("(i p k) d -> p i k d", p=P, k=2)

            @block.sync
            def _(sp):
                for i in range(NT):
                    sp.dma_start(y[:, i, :, :], yv[:, i, :, :]).then_inc(Y[i], 16)
                    if i == 0:
                        sp.dma_start(gain[:], self.i["norm_final"].partition_broadcast(P)).then_inc(S["g"], 16)
                for i in range(NT):
                    sp.wait_ge(S["o"], i + 1)
                    sp.dma_start(self.out[i * P:(i + 1) * P, :], x2[:, i, :]).then_inc(S["out"], 16)
                sp.wait_ge(S["out"], 16 * NT)

            @block.scalar
            def _(act):
                for i in range(NT):
                    act.wait_ge(S["b"], i + 1)
                    if i:
                        act.wait_ge(S["ss"], i)
                    act.activation(sq[:], x2[:, i, :], ACT.Square, accum_out=ss[:, i:i + 1]).then_inc(S["ss"], 1)
                    act.wait_ge(S["rc"], i + 1)
                    act.activation(ss[:, i:i + 1], ss[:, i:i + 1], ACT.Sqrt).then_inc(S["rt"], 1)

            @block.vector
            def _(dve):
                def first(i):
                    dve.wait_ge(Y[i], 16)
                    dve.scalar_tensor_tensor(x2[:, i, :], y[:, i, 0, :], self.gates12[:, 0, i:i + 1], x2[:, i, :], ALU.mult, ALU.add).then_inc(S["a"], 1)
                    dve.wait_ge(S["a"], i + 1)
                    dve.scalar_tensor_tensor(x2[:, i, :], y[:, i, 1, :], self.gates12[:, 1, i:i + 1], x2[:, i, :], ALU.mult, ALU.add).then_inc(S["b"], 1)

                first(0)
                dve.wait_ge(S["g"], 16)
                for i in range(NT):
                    dve.wait_ge(S["ss"], i + 1)
                    dve.tensor_scalar(ss[:, i:i + 1], ss[:, i:i + 1], 1.0 / D, EPS, ALU.mult, ALU.add).then_inc(S["ms"], 1)
                    dve.wait_ge(S["ms"], i + 1)
                    dve.reciprocal(ss[:, i:i + 1], ss[:, i:i + 1]).then_inc(S["rc"], 1)
                    if i + 1 < NT:
                        first(i + 1)
                    dve.wait_ge(S["rt"], i + 1)
                    dve.scalar_tensor_tensor(x2[:, i, :], x2[:, i, :], ss[:, i:i + 1], gain[:], ALU.mult, ALU.mult).then_inc(S["o"], 1)

    def build(self):
        nc = self.nc
        with self.ctx as c:
            self.bank = [c.enter_context(nc.psum_tensor(f"bank{n}", [P, HALF], F32)) for n in range(8)]
            self.gates = {e.engine: self.sem(c, f"gate_{n}") for n, e in (
                ("dve", nc.vector), ("sp", nc.sync), ("pe", nc.tensor), ("pool", nc.gpsimd))}
            self.cons = self.sb(c, "cons_sb", [P, NCON])
            self.par = self.sb(c, "par_cols", [P, P])
            self.hT = self.x2 = self.sb(c, "hT_or_x2", [P, KT, T])
            self.gates12 = self.sb(c, "gates12", [P, 2, NT])
            self.slot_from = self.sb(c, "slot_from", [P, NBLK], U32)
            self.slot_to = self.sb(c, "slot_to", [P, NBLK], U32)
            self.extra = self.sb(c, "extra_blocks", [P, NOV + 1], I32)
            self.h2d = nc.dram_tensor("h2_rows", (T, D), F32, kind="Internal").ap()
            self.yd = nc.dram_tensor("expert_rows", (2 * T, D), F32, kind="Internal").ap()
            flat = lambda t: t.rearrange("p a b -> p (a b)")
            self.mixT = self.sb(c, "mixT", [P, KT, T])
            self.run_stage(self.norm_stage)
            self.run_stage(self.lru_stage)
            self.run_stage(self.rwkv_stage)
            self.run_stage(self.gdn_stage)
            self.w_landed = [self.sem(c, f"ex_weights{j}_landed") for j in range(NR)]
            with ExitStack() as m:
                self.gu_early = self.sb(m, "w_gate_up_early", [P, NEARLY, KT, 2 * DE])
                self.dn_early = self.sb(m, "w_down_early", [P, NEARLY, 2, D])
                self.xg_early = self.sb(m, "x_early", [P, 2, D])
                self.run_stage(self.route_stage)
                self.run_stage(self.expert_stage)
            self.run_stage(self.final_stage)


def build_program(nc, ins, out):
    Build(nc, ins, out).build()


def layout(inputs):
    f = {k: np.ascontiguousarray(v) for k, v in inputs.items()}
    rows = lambda a: a.reshape(-1, P)
    per = [f[n][0].reshape(2, P) for n in ("rwkv_w0", "rwkv_a0", "rwkv_k_k", "rwkv_k_a", "rwkv_r_k", "rwkv_lnx_w", "rwkv_lnx_b")]
    mu = f["rwkv_mu"][0].reshape(7, P)
    rwkv = np.stack([mu[0:2], mu[2:4], mu[4:6]] + per, 1).reshape(20, P)
    conv = f["gdn_conv_w"][0].reshape(4, 3, GH, P).transpose(2, 1, 0, 3).reshape(48, P)
    lru = f["lru_conv_w"][0].reshape(4, 2, P).transpose(1, 0, 2).reshape(8, P)
    par = np.concatenate([rows(f["norm_mix"]), rows(f["norm_ffn"]), mu[6:7], rwkv, conv, lru,
                          rows(f["lru_conv_b"]), rows(f["lru_b_a"]), rows(f["lru_b_x"]), rows(f["lru_lambda"]),
                          rows(f["gdn_norm_w"])], 0)
    return {
        "x": f["x"][0], "par_rows": np.ascontiguousarray(par), "cons": constants(),
        "w_in": f["w_in"][0], "w_out": f["w_out"][0],
        "rwkv_w2": f["rwkv_w2"][0], "rwkv_a2": f["rwkv_a2"][0], "rwkv_g2": f["rwkv_g2"][0],
        "gdn_ab": np.ascontiguousarray(np.concatenate([f["gdn_a_log"], f["gdn_dt_bias"]], 1)),
        "lru_w_a": f["lru_w_a"][0], "lru_w_x": f["lru_w_x"][0],
        "norm_ffn_row": f["norm_ffn"], "norm_final": f["norm_final"][None, :],
        "moe_b": np.ascontiguousarray(np.concatenate([f["moe_b_group"], f["moe_b_expert"]], 1)),
        "moe_w_group": f["moe_w_group"][0], "moe_w_expert": f["moe_w_expert"][0],
        "moe_w_gate": f["moe_w_gate"][0], "moe_w_up": f["moe_w_up"][0], "moe_w_down": f["moe_w_down"][0],
    }


def kernel(**inputs):
    from concourse import bacc, mybir as _mybir
    from concourse.bass_utils import run_bass_kernel_spmd as run

    arrays = layout(inputs)
    nc = bacc.Bacc("TRN2", target_bir_lowering=False, num_devices=1)
    ins = {k: nc.dram_tensor(k, a.shape, _mybir.dt.from_np(a.dtype), kind="ExternalInput").ap() for k, a in arrays.items()}
    out = nc.dram_tensor("out", (T, D), F32, kind="ExternalOutput").ap()
    build_program(nc, ins, out)
    r = run(nc, [arrays], core_ids=[0])
    return r.results[0]["out"].reshape(1, T, D)
```

```python
from contextlib import ExitStack

import numpy as np

import concourse.bass as bass
from concourse import mybir

F32 = mybir.dt.float32
I32 = mybir.dt.int32
U32 = mybir.dt.uint32
ALU = mybir.AluOpType
ACT = mybir.ActivationFunctionType
AX = mybir.AxisListType.X

P = 128
T = 1024
D = 1024
NT = T // P
KT = D // P
HALF = 512
EPS = 1e-6

DA, DB, DC = D // 4, D // 2, D // 4
A_COLS = 3 * DA + 32 + 32 + 64
B_COLS = 4 * DB + 8
COL_B = A_COLS
COL_BETA = COL_B + 4 * DB
COL_C = A_COLS + B_COLS
GN_EPS = 64e-5
EM05 = float(np.exp(-0.5))

GH = 4
NG = T // P
CR = 64
NCR = T // CR

E = 32
DE = D // 4
NOV = 15
NBLK = E + NOV
NR = 4
NEARLY = 2

PAR = {}
_n = 0
for _name, _rows in (("norm_mix", 8), ("norm_ffn", 8), ("mu_lo", 1), ("rwkv", 20), ("gdn_conv", 48),
                     ("lru_conv", 8), ("lru_conv_b", 2), ("lru_b_a", 2), ("lru_b_x", 2),
                     ("lru_lambda", 2), ("gdn_norm", 1)):
    PAR[_name] = _n
    _n += _rows
NPAR = _n

CON = {}
_n = 0
for _name, _cols in (("ident", P), ("ones", P), ("ones64", P), ("upper", P), ("below", P), ("low", P),
                     ("low_strict", P), ("up64_strict", P), ("up64", P), ("lev_low", 7 * P),
                     ("lev_up", 6 * P), ("iota128", P), ("iota_blk", NBLK), ("iota_tok", NT),
                     ("iota_e", E), ("iota_e128", E), ("half", 2), ("j128", 7), ("iota_p", 1), ("idx4", 4),
                     ("keep", 2), ("nhalf", 2)):
    CON[_name] = (_n, _cols)
    _n += _cols
NCON = _n


def constants():
    c = np.zeros((P, NCON), np.float32)
    i, j = np.arange(P)[:, None], np.arange(P)[None, :]

    def put(name, value):
        a, n = CON[name]
        c[:, a:a + n] = value

    put("ident", i == j)
    put("ones", 1)
    put("ones64", i // 64 == j // 64)
    put("upper", i <= j)
    put("below", i < j)
    put("low", i >= j)
    put("low_strict", i > j)
    put("up64_strict", (i < j) & (i // 64 == j // 64))
    put("up64", (i <= j) & (i // 64 == j // 64))
    lev = [(i // (2 * s) == j // (2 * s)) & (i % (2 * s) >= s) & (j % (2 * s) < s) for s in (1, 2, 4, 8, 16, 32, 64)]
    put("lev_low", np.concatenate(lev, 1))
    put("lev_up", np.concatenate([m.T for m in lev[:6]], 1))
    put("iota128", j)
    put("iota_blk", np.arange(NBLK)[None, :])
    put("iota_tok", i + P * np.arange(NT)[None, :])
    put("iota_e", np.arange(E)[None, :])
    put("iota_e128", P * np.arange(E)[None, :])
    put("half", i // 64 == np.arange(2)[None, :])
    put("j128", P * np.arange(1, 8)[None, :])
    put("iota_p", i)
    put("idx4", 4 - np.arange(4)[None, :])
    put("keep", np.arange(2)[None, :])
    put("nhalf", -1.0 * (i // 64 == np.arange(2)[None, :]))
    return c


LRU_AT = KT * 2 * DC
RWKV_ARENA = (3 + 7 + 4 + 4) * HALF + (5 + 3 + 4) * (HALF // CR) * P
assert RWKV_ARENA >= LRU_AT + 14 * T + 2 * (3 + T)


class Step:

    def __init__(self, eng, sem, base=0):
        self.eng, self.sem, self.base, self.n = eng, sem, base, 0

    def inc(self, ins):
        ins.then_inc(self.sem, 1)
        self.n += 1

    def wait(self):
        self.eng.wait_ge(self.sem, self.base + self.n)

    def __call__(self, ins):
        self.inc(ins)
        self.wait()


class Build:
    def __init__(self, nc, ins, out):
        self.nc, self.i, self.out = nc, ins, out
        self.ctx = ExitStack()

    def sb(self, ctx, name, shape, dt=F32):
        return ctx.enter_context(self.nc.sbuf_tensor(name, shape, dt))

    def sem(self, ctx, name):
        return self.nc.alloc_semaphore(name)

    def run_stage(self, stage):
        before = self.nc.snapshot_sems()
        stage()
        self.nc.clear_and_free_semaphores(self.nc.allocated_since(before))
        self.nc.all_engine_barrier()

    def con(self, name):
        a, n = CON[name]
        return self.cons[:, a:a + n]

    def parc(self, name, k=0, n=1):
        return self.par[:, PAR[name] + k:PAR[name] + k + n]

    def pass_gate(self, eng):
        eng.sem_inc(self.gates[eng.engine], 1)

    def norm_stage(self):
        nc = self.nc
        with ExitStack() as c:
            x = self.sb(c, "x_in", [P, NT, D])
            sq = self.sb(c, "x_sq", [P, D])
            prow = self.sb(c, "par_rows_sb", [P, P])
            ss = self.sb(c, "x_ss", [P, NT])
            rs = self.sb(c, "x_rs", [P, NT])
            s_par, s_con, s_ss, s_v, s_rs, s_xn, s_tr, s_par_t, s_par_ok = (
                self.sem(c, n) for n in ("par_landed", "cons_landed", "x_squared", "norm_dve", "norm_root", "x_scaled", "x_turned", "par_turned", "par_ready"))
            s_x = [self.sem(c, f"x{i}_landed") for i in range(NT)]
            s_ev = [self.sem(c, "turned_out_dve"), self.sem(c, "turned_out_act")]
            block = c.enter_context(nc.Block())
            xv = self.i["x"].rearrange("(i p) d -> p i d", p=P)

            @block.sync
            def _(sp):
                for i in range(NT):
                    sp.dma_start(x[:, i, :], xv[:, i, :]).then_inc(s_x[i], 16)
                    if i == 3:
                        sp.dma_start(prow[0:NPAR, :], self.i["par_rows"]).then_inc(s_par, 16)
                        sp.dma_start(self.cons[:], self.i["cons"]).then_inc(s_con, 16)
                for kt in range(KT):
                    sp.dma_start(self.w_lru[:, kt, :], self.i["w_in"][kt * P:(kt + 1) * P, COL_C:COL_C + 2 * DC]).then_inc(self.w_lru_landed, 16)

            @block.scalar
            def _(act):
                for half in range(2):
                    for i in range(4 * half, 4 * half + 4):
                        act.wait_ge(s_x[i], 16)
                        if i:
                            act.wait_ge(s_ss, i)
                        act.activation(sq[:], x[:, i, :], ACT.Square, accum_out=ss[:, i:i + 1]).then_inc(s_ss, 1)
                    act.wait_ge(s_v, 2 * half + 2)
                    cols = slice(4 * half, 4 * half + 4)
                    act.activation(rs[:, cols], rs[:, cols], ACT.Sqrt).then_inc(s_rs, 1)
                act.wait_ge(s_par_ok, 1)
                for t in range(1, 2 * KT, 2):
                    self.norm_out(act, t, s_tr, s_ev)

            @block.vector
            def _(dve):
                for half in range(2):
                    cols = slice(4 * half, 4 * half + 4)
                    dve.wait_ge(s_ss, 4 * half + 4)
                    dve.tensor_scalar(rs[:, cols], ss[:, cols], 1.0 / D, EPS, ALU.mult, ALU.add).then_inc(s_v, 1)
                    dve.wait_ge(s_v, 2 * half + 1)
                    dve.reciprocal(rs[:, cols], rs[:, cols]).then_inc(s_v, 1)
                    dve.wait_ge(s_rs, half + 1)
                    for i in range(4 * half, 4 * half + 4):
                        dve.tensor_scalar(x[:, i, :], x[:, i, :], rs[:, i:i + 1], None, ALU.mult).then_inc(s_xn, 1)
                    if half == 0:
                        dve.wait_ge(s_par_t, 1)
                        dve.tensor_copy(self.par[:, 0:NPAR], self.bank[7][:, 0:NPAR]).then_inc(s_par_ok, 1)
                dve.wait_ge(s_par_ok, 1)
                for t in range(0, 2 * KT, 2):
                    self.norm_out(dve, t, s_tr, s_ev)

            @block.tensor
            def _(pe):
                pe.wait_ge(s_par, 16)
                pe.wait_ge(s_con, 16)
                pe.transpose(self.bank[7][:, 0:NPAR], prow[0:NPAR, :], self.con("ident")[0:NPAR, 0:NPAR]).then_inc(s_par_t, 1)
                for t in range(2 * KT):
                    half, kt = t // KT, t % KT
                    pe.wait_ge(s_xn, 4 * half + 4)
                    if t >= 6:
                        pe.wait_ge(s_ev[t % 2], (t - 6) // 2 + 1)
                    for q in range(4):
                        ins = pe.transpose(self.bank[t % 6][:, q * P:(q + 1) * P],
                                           x[:, 4 * half + q, kt * P:(kt + 1) * P], self.con("ident"))
                    ins.then_inc(s_tr, 1)

    def norm_out(self, eng, t, s_tr, s_ev):
        half, kt = t // KT, t % KT
        eng.wait_ge(s_tr, t + 1)
        dst = self.hT[:, kt, half * HALF:(half + 1) * HALF]
        gain = self.parc("norm_mix", kt)
        if t % 2 == 0:
            eng.tensor_scalar(dst, self.bank[t % 6][:], gain, None, ALU.mult).then_inc(s_ev[0], 1)
        else:
            eng.activation(dst, self.bank[t % 6][:], ACT.Copy, scale=gain).then_inc(s_ev[1], 1)

    def lru_parts(self, c):
        w = self.w_lru
        wg = self.sb(c, "lru_gate_w", [P, 2, 2, P])
        two = lambda k: self.arena[:, LRU_AT + 2 * T * k:LRU_AT + 2 * T * (k + 1)].rearrange("p (j t) -> p j t", j=2)
        xb, gg, r, ig, a, th, lt = (two(k) for k in range(7))
        raw = self.arena[:, LRU_AT + 14 * T:LRU_AT + 14 * T + 2 * (3 + T)].rearrange("p (j t) -> p j t", j=2)
        v = self.sb(c, "lru_small", [P, 12, 2])
        S = {n: self.sem(c, "lru_" + n) for n in (
            "wz", "wg", "proj", "raw", "gelu", "conv", "gates", "sig", "spe", "spd", "act", "step", "init", "out")}

        def on_sync(sp):
            sp.wait_ge(S["wz"], 1)
            for g, name in enumerate(("lru_w_a", "lru_w_x")):
                for b in range(4):
                    o = 64 * (b % 2)
                    sp.dma_start(wg[o:o + 64, g, b // 2, o:o + 64], self.i[name][b]).then_inc(S["wg"], 16)

        def on_pool(pool):
            pool.memset(wg[:], 0.0).then_inc(S["wz"], 1)
            pool.memset(raw[:, :, 0:3], 0.0).then_inc(S["init"], 1)

        def on_pe(pe):
            pe.wait_ge(self.w_lru_landed, 16 * KT)
            for m in range(4):
                for kt in range(KT):
                    for half in range(2):
                        ins = pe.matmul(self.bank[2 * m + half][:], w[:, kt, m * P:(m + 1) * P],
                                        self.hT[:, kt, half * HALF:(half + 1) * HALF], start=kt == 0, stop=kt == KT - 1)
                ins.then_inc(S["proj"], 1)
            pe.wait_ge(S["wg"], 16 * 8)
            pe.wait_ge(S["raw"], 4)
            pe.wait_ge(S["conv"], 8)
            for g in range(2):
                if g:
                    pe.wait_ge(S["gelu"], 4)
                for j in range(2):
                    for half in range(2):
                        pe.matmul(self.bank[4 * g + 2 * j + half][:], wg[:, g, j, :],
                                  xb[:, j, half * HALF:(half + 1) * HALF], start=True, stop=True).then_inc(S["gates"], 1)

        def on_act(act):
            act.wait_ge(S["spd"], 2)
            act.activation(v[:, 2, :], v[:, 1, :], ACT.Exp, scale=-1.0).then_inc(S["spe"], 1)
            act.wait_ge(S["spd"], 3)
            act.activation(v[:, 4, :], v[:, 3, :], ACT.Ln).then_inc(S["spe"], 1)
            for m in range(2):
                act.wait_ge(S["proj"], m + 1)
                for half in range(2):
                    act.activation(raw[:, m, 3 + half * HALF:3 + (half + 1) * HALF], self.bank[2 * m + half][:],
                                   ACT.Copy).then_inc(S["raw"], 1)
            for m in range(2):
                act.wait_ge(S["proj"], m + 3)
                for half in range(2):
                    act.activation(gg[:, m, half * HALF:(half + 1) * HALF], self.bank[4 + 2 * m + half][:],
                                   ACT.Gelu_apprx_tanh).then_inc(S["gelu"], 1)
            for g, dst, bias in ((0, r, "lru_b_a"), (1, ig, "lru_b_x")):
                for j in range(2):
                    for half in range(2):
                        act.wait_ge(S["gates"], 4 * g + 2 * j + half + 1)
                        act.activation(dst[:, j, half * HALF:(half + 1) * HALF], self.bank[4 * g + 2 * j + half][:],
                                       ACT.Sigmoid, bias=self.parc(bias, j)).then_inc(S["sig"], 1)
            act.wait_ge(S["spd"], 13)
            act.wait_ge(S["sig"], 8)
            for j in range(2):
                act.activation(a[:, j, :], r[:, j, :], ACT.Exp, scale=v[:, 11, j:j + 1]).then_inc(S["act"], 1)
                act.activation(th[:, j, :], r[:, j, :], ACT.Tanh, scale=v[:, 11, j:j + 1]).then_inc(S["act"], 1)
            act.wait_ge(S["act"], 4)
            act.activation(lt, th, ACT.Ln, scale=-1.0, bias=1.0).then_inc(S["act"], 1)
            act.activation(r, th, ACT.Sqrt, scale=-2.0).then_inc(S["act"], 1)
            act.wait_ge(S["act"], 6)
            act.activation(lt, lt, ACT.Exp, scale=-0.5).then_inc(S["act"], 1)

        def on_dve(dve):
            step = Step(dve, S["step"])
            lam = self.parc("lru_lambda", 0, 2)
            dve.tensor_scalar(v[:, 0, :], lam, -1.0, None, ALU.mult).then_inc(S["spd"], 1)
            dve.wait_ge(S["spd"], 1)
            dve.tensor_tensor(v[:, 1, :], v[:, 0, :], lam, ALU.max).then_inc(S["spd"], 1)
            dve.wait_ge(S["spe"], 1)
            dve.tensor_scalar(v[:, 3, :], v[:, 2, :], 1.0, None, ALU.add).then_inc(S["spd"], 1)
            dve.wait_ge(S["spe"], 2)
            sp = Step(dve, S["spd"])
            sp.n = 3
            sp.wait()
            sp(dve.tensor_scalar(v[:, 5, :], v[:, 3, :], -1.0, None, ALU.add))
            sp(dve.tensor_scalar(v[:, 6, :], v[:, 5, :], 1e-30, None, ALU.max))
            sp(dve.reciprocal(v[:, 7, :], v[:, 6, :]))
            sp(dve.tensor_tensor(v[:, 8, :], v[:, 4, :], v[:, 2, :], ALU.mult))
            sp(dve.tensor_tensor(v[:, 8, :], v[:, 8, :], v[:, 7, :], ALU.mult))
            sp(dve.tensor_scalar(v[:, 9, :], v[:, 5, :], 0.0, None, ALU.is_equal))
            sp(dve.tensor_tensor(v[:, 9, :], v[:, 9, :], v[:, 2, :], ALU.mult))
            sp(dve.tensor_tensor(v[:, 8, :], v[:, 8, :], v[:, 9, :], ALU.add))
            sp(dve.tensor_scalar(v[:, 10, :], v[:, 0, :], 0.0, None, ALU.max))
            dve.tensor_tensor(v[:, 10, :], v[:, 10, :], v[:, 8, :], ALU.add).then_inc(S["step"], 1)
            step.n = 1
            step.wait()
            sp.inc(dve.tensor_scalar(v[:, 11, :], v[:, 10, :], -8.0, None, ALU.mult))
            dve.wait_ge(S["raw"], 4)
            dve.wait_ge(S["init"], 1)
            for j in range(2):
                taps = [self.parc("lru_conv", 4 * j + t) for t in range(4)]
                dve.tensor_scalar(xb[:, j, :], raw[:, j, 3:3 + T], taps[3], self.parc("lru_conv_b", j),
                                  ALU.mult, ALU.add).then_inc(S["conv"], 1)
                for t in (2, 1, 0):
                    dve.wait_ge(S["conv"], 4 * j + 3 - t)
                    dve.scalar_tensor_tensor(xb[:, j, :], raw[:, j, t:t + T], taps[t], xb[:, j, :],
                                             ALU.mult, ALU.add).then_inc(S["conv"], 1)
            dve.wait_ge(S["sig"], 8)
            dve.wait_ge(S["conv"], 8)
            step(dve.tensor_tensor(xb, xb, ig, ALU.mult))
            dve.wait_ge(S["act"], 7)
            step(dve.tensor_tensor(lt, lt, r, ALU.mult))
            step(dve.memset(lt[:, :, 0:1], 1.0))
            step(dve.tensor_tensor(xb, xb, lt, ALU.mult))
            for j in range(2):
                step.inc(dve.tensor_tensor_scan(th[:, j, :], a[:, j, :], xb[:, j, :], 0.0, ALU.mult, ALU.add))
            step.wait()
            dve.wait_ge(S["gelu"], 4)
            dve.tensor_tensor(self.mixT[:, 6:8, :], th, gg, ALU.mult).then_inc(S["out"], 1)

        self.lru_sig, self.lru_out = S["sig"], S["out"]
        return on_sync, on_pool, on_pe, on_act, on_dve

    def invert_pe(self, pe, W, S, lhs, upd, tur, ye, levels, final_turn, between=None):
        for lv in range(levels + (1 if final_turn else 0)):
            if between:
                between(lv)
            for g in range(2):
                W(pe, "i_upd", 2 * lv + g + 1)
                for q in range(4):
                    ins = pe.transpose(self.bank[g][:, q * P:(q + 1) * P], upd[:, 4 * g + q, :], self.con("ident"))
                ins.then_inc(S["i_turn"], 1)
            if lv == levels:
                break
            for g in range(2):
                W(pe, "i_tur", 2 * lv + g + 1)
                for q in range(4):
                    ins = pe.matmul(self.bank[2 + g][:, q * P:(q + 1) * P], lhs[:, 4 * g + q, :], tur[:, 4 * g + q, :],
                                    start=True, stop=True)
                ins.then_inc(S["i_y"], 1)
            for g in range(2):
                W(pe, "i_ye", 2 * lv + g + 1)
                for q in range(4):
                    ins = pe.matmul(self.bank[4 + g][:, q * P:(q + 1) * P], ye[:, 4 * g + q, :], upd[:, 4 * g + q, :],
                                    start=True, stop=True)
                ins.then_inc(S["i_w"], 1)

    def invert_act(self, act, W, S, tur, ye, levels, final_turn, between=None):
        flat = lambda t, g: t[:, 4 * g:4 * g + 4, :].rearrange("p a b -> p (a b)")
        for lv in range(levels + (1 if final_turn else 0)):
            if between:
                between(lv)
            for g in range(2):
                W(act, "i_turn", 2 * lv + g + 1)
                act.activation(flat(tur, g), self.bank[g][:], ACT.Copy).then_inc(S["i_tur"], 1)
            if lv == levels:
                break
            for g in range(2):
                W(act, "i_y", 2 * lv + g + 1)
                act.activation(flat(ye, g), self.bank[2 + g][:], ACT.Copy).then_inc(S["i_ye"], 1)

    def invert_dve(self, dve, W, S, upd, masks, levels, between=None):
        for lv in range(levels):
            m = self.cons[:, CON[masks][0] + (lv + 1) * P:CON[masks][0] + (lv + 2) * P].bitcast(U32)
            for g in range(2):
                W(dve, "i_w", 2 * lv + g + 1)
                self.pass_gate(dve)
                dve.copy_predicated(upd[:, 4 * g:4 * g + 4, :], m.unsqueeze(1).to_broadcast([P, 4, P]),
                                    self.bank[4 + g][:].rearrange("p (a b) -> p a b", a=4)).then_inc(S["i_upd"], 1)
            if between:
                between(lv)

    def gdn_stage(self):
        nc = self.nc
        K = dict(w0=16, w1=16, w2=16, proj=3, raw=6, sil=3, sq=2, ss=4, ln=4, rs=2, qn=2, gcr=2, gr=8, ge=2, gm=4, trv=2, trk=2,
                 kv=6, kk=2, qk=2, nn=8, am=2, at=2, ate=2, i_init=1, i_turn=14, i_tur=14, i_y=12, i_ye=12, i_w=12,
                 i_upd=14, u=2, ue=2, wt=2, wte=2, ws=8, vn=8, sk=8, st=9, qs=2, av=2, t1=2, o=2, osq=3, ol=2, og=2,
                 ot=2, mx=2, hs=2, taps=1, conv=12)
        with ExitStack() as c:
            zw = self.sb(c, "gdn_work", [P, 18624])
            raw = self.sb(c, "gdn_raw", [P, 3, 3 + T])
            wqkv = self.sb(c, "gdn_w", [P, 3, KT, P])
            cvv = self.sb(c, "gdn_v", [P, T])
            zs = self.sb(c, "gdn_z", [P, GH, NG, P])
            scal = self.sb(c, "gdn_scal", [P, GH, 8, NG])
            hs = self.sb(c, "gdn_head_scal", [P, 8, NG])
            taps = self.sb(c, "gdn_taps", [P, 12])
            wb = self.sb(c, "gdn_w_beta", [P, KT, 8])
            ab = self.sb(c, "gdn_ab_sb", [P, 8])
            ba = self.sb(c, "gdn_ba", [P, NT, 8])
            sm = self.sb(c, "gdn_small", [P, 6, GH, NG])
            ev = self.sb(c, "gdn_ea", [P, GH])
            ssum = self.sb(c, "gdn_ssum", [P, 3, NG])
            off = [0]

            def carve(n, shape=None):
                a = zw[:, off[0]:off[0] + n]
                off[0] += n
                return a

            v3 = lambda a, k: a.rearrange("p (a b) -> p a b", a=k)
            r1 = carve(3 * T)
            e, ei, es = (v3(r1[:, k * T:(k + 1) * T], NG) for k in range(3))
            osb, osq, og = e, ei, es
            r2 = carve(3 * T)
            cv = v3(r2, 3)
            nn, am, at = (v3(r2[:, k * T:(k + 1) * T], NG) for k in range(3))
            r3 = carve(2 * T)
            sq = v3(r3, 2)
            upd, tur = (v3(r3[:, k * T:(k + 1) * T], NG) for k in range(2))
            qn, kn = (v3(carve(T), NG) for _ in range(2))
            kd, kbg, vb = (v3(carve(T), NG) for _ in range(3))
            r6 = carve(T)
            glb = ye = v3(r6, NG)
            u, wt = v3(carve(T), NG), v3(carve(T), NG)
            vn = v3(carve(T), NG)
            st = v3(carve(9 * P), 9)
            wz = v3(zw[:, 0:KT * DB], KT)
            flat = lambda t, a, b: t[:, a:b, :].rearrange("p a b -> p (a b)")
            S = {n: self.sem(c, "gdn_" + n) for n in K}
            Z = {n: self.sem(c, "gdnz_" + n) for n in ("w", "z", "zs", "ba", "d", "a", "pe", "pad")}
            ZW = [self.sem(c, f"gdnz_w{kt}") for kt in range(KT)]
            block = c.enter_context(nc.Block())
            win = self.i["w_in"].rearrange("(kt p) c -> p kt c", p=P)

            def waits(h):
                return lambda eng, name, n: eng.wait_ge(S[name], h * K[name] + n)

            @block.sync
            def _(sp):
                sp.dma_start(wb[:], win[:, :, COL_BETA:COL_BETA + 8]).then_inc(Z["w"], 16)
                sp.dma_start(ab[:], self.i["gdn_ab"].partition_broadcast(P)).then_inc(Z["w"], 16)
                for kt in range(KT):
                    sp.dma_start(wz[:, kt, :], win[:, kt, COL_B + 3 * DB:COL_B + 4 * DB]).then_inc(ZW[kt], 16)
                for m in range(3):
                    sp.dma_start(wqkv[:, m, :, :], win[:, :, COL_B + m * DB:COL_B + m * DB + P]).then_inc(S[f"w{m}"], 16)
                with sp.Fori(1, GH) as h:
                    for m in range(3):
                        waits(h - 1)(sp, "proj", m + 1)
                        self.pass_gate(sp)
                        sp.dma_start(wqkv[:, m, :, :], win[:, :, bass.ds(h * P + (COL_B + m * DB), P)]).then_inc(S[f"w{m}"], 16)

            @block.gpsimd
            def _(pool):
                low = self.con("low").unsqueeze(1).to_broadcast([P, 4, P])
                lows = self.con("low_strict").unsqueeze(1).to_broadcast([P, 4, P])
                with pool.Fori(0, GH) as h:
                    W = waits(h)
                    for g in range(2):
                        W(pool, "ge", g + 1)
                        pool.tensor_tensor(es[:, 4 * g:4 * g + 4, :], e[:, 4 * g:4 * g + 4, :], lows, ALU.mult).then_inc(S["gm"], 1)
                        pool.tensor_tensor(ei[:, 4 * g:4 * g + 4, :], e[:, 4 * g:4 * g + 4, :], low, ALU.mult).then_inc(S["gm"], 1)

            @block.tensor
            def _(pe):
                for i in range(NT):
                    for kt in range(KT):
                        if i == 0:
                            pe.wait_ge(ZW[kt], 16)
                        ins = pe.matmul(self.bank[i % 7][:], self.hT[:, kt, i * P:(i + 1) * P], wz[:, kt, :],
                                        start=kt == 0, stop=kt == KT - 1)
                    ins.then_inc(Z["z"], 1)
                    if i == 0:
                        pe.wait_ge(Z["w"], 32)
                    for kt in range(KT):
                        ins = pe.matmul(self.bank[7][:, 8 * i:8 * i + 8], self.hT[:, kt, i * P:(i + 1) * P], wb[:, kt, :],
                                        start=kt == 0, stop=kt == KT - 1)
                    if i == 6:
                        pe.wait_ge(Z["zs"], 1)
                ins.then_inc(Z["ba"], 1)
                pe.wait_ge(Z["zs"], 8)
                for m, b0 in enumerate((4, 6)):
                    waits(0)(pe, f"w{m}", 16)
                    for n in range(2 * KT):
                        self.gdn_project(pe, S, wqkv, m, b0, n)
                    if m == 0:
                        pe.wait_ge(Z["d"], 8)
                        gl = scal[:, :, 7, :]
                        pe.matmul(self.bank[0][:, 0:32], self.con("upper"), gl, start=True, stop=True)
                        pe.matmul(self.bank[0][:, 32:64], self.con("ones"), gl, start=True, stop=True).then_inc(Z["pe"], 1)
                tiles = dict(raw=raw, sq=sq, qn=qn, kn=kn, cv=cv, glb=glb, am=am, nn=nn, upd=upd, tur=tur, ye=ye, vb=vb, cvv=cvv,
                             kd=kd, kbg=kbg, wt=wt, st=st, vn=vn, at=at, og=og, wqkv=wqkv)
                waits(0)(pe, "raw", 4)
                waits(0)(pe, "w2", 16)
                for n in range(KT):
                    self.gdn_project(pe, S, wqkv, 2, 6, n)
                self.heads(pe, lambda h, last: self.gdn_pe(pe, waits(h), waits(h + 1), last, S, tiles))

            @block.scalar
            def _(act):
                for i in range(NT):
                    act.wait_ge(Z["z"], i + 1)
                    act.activation(zs[:, :, i, :], self.bank[i % 7][:].rearrange("p (h v) -> p h v", h=GH), ACT.Silu).then_inc(Z["zs"], 1)
                act.wait_ge(Z["d"], 1)
                act.activation(scal[:, :, 4, :], ba[:, :, 0:4].rearrange("p i h -> p h i"), ACT.Sigmoid).then_inc(Z["a"], 1)
                act.wait_ge(Z["d"], 4)
                act.activation(sm[:, 2, :, :], sm[:, 1, :, :], ACT.Exp, scale=-1.0).then_inc(Z["a"], 1)
                act.activation(ev[:], ab[:, 0:4], ACT.Exp).then_inc(Z["a"], 1)
                act.wait_ge(Z["a"], 3)
                act.activation(sm[:, 3, :, :], sm[:, 2, :, :], ACT.Ln, bias=1.0).then_inc(Z["a"], 1)
                act.wait_ge(Z["d"], 11)
                act.activation(scal[:, :, 1, :], scal[:, :, 0, :], ACT.Exp).then_inc(Z["a"], 1)
                act.activation(scal[:, :, 6, :], sm[:, 4, :, :], ACT.Exp).then_inc(Z["a"], 1)
                act.activation(scal[:, :, 2, :], sm[:, 5, :, :], ACT.Exp).then_inc(Z["a"], 1)

                def raw_out(W, m):
                    W(act, "proj", m + 1)
                    for half in range(2):
                        act.activation(raw[:, m, 3 + half * HALF:3 + (half + 1) * HALF], self.bank[(4, 6, 6)[m] + half][:],
                                       ACT.Copy).then_inc(S["raw"], 1)

                def silu(W, m):
                    W(act, "conv", 4 * (m + 1))
                    dst = cv[:, m, :] if m < 2 else cvv[:]
                    act.activation(dst, dst, ACT.Silu).then_inc(S["sil"], 1)

                def body(h, last):
                    W, W1 = waits(h), waits(h + 1)
                    for m in range(2):
                        W(act, "sil", m + 1)
                        act.activation(sq[:, m, :], cv[:, m, :], ACT.Square).then_inc(S["sq"], 1)
                    for b in range(4):
                        W(act, "ss", b + 1)
                        act.activation(sq[:, b // 2, b % 2 * HALF:(b % 2 + 1) * HALF], self.bank[b][:], ACT.Ln, bias=EPS).then_inc(S["ln"], 1)
                    for m in range(2):
                        W(act, "ln", 2 * m + 2)
                        act.activation(sq[:, m, :], sq[:, m, :], ACT.Exp, scale=-0.5).then_inc(S["rs"], 1)
                    for g in range(2):
                        W(act, "gr", 4 * g + 4)
                        act.activation(flat(e, 4 * g, 4 * g + 4), flat(e, 4 * g, 4 * g + 4), ACT.Exp, scale=-1.0).then_inc(S["ge"], 1)
                    raw_out(W, 2)

                    def between(lv):
                        if lv == 3:
                            for g in range(2):
                                W(act, "at", g + 1)
                                act.activation(flat(at, 4 * g, 4 * g + 4), self.bank[6 + g][:], ACT.Copy).then_inc(S["ate"], 1)
                        if lv == 5:
                            silu(W, 2)

                    self.invert_act(act, W, S, tur, ye, 6, True, between)
                    for g in range(2):
                        W(act, "u", g + 1)
                        act.activation(flat(u, 4 * g, 4 * g + 4), self.bank[2 + g][:], ACT.Copy).then_inc(S["ue"], 1)
                    if not last:
                        raw_out(W1, 0)
                    W(act, "osq", 3)
                    act.activation(ssum[:, 1, :], ssum[:, 1, :], ACT.Ln).then_inc(S["ol"], 1)
                    W(act, "ol", 1)
                    act.activation(ssum[:, 2, :], ssum[:, 1, :], ACT.Exp, scale=-0.5).then_inc(S["ol"], 1)
                    if not last:
                        raw_out(W1, 1)
                        silu(W1, 0)
                    for g in range(2):
                        W(act, "ot", g + 1)
                        act.activation(self.mixT[:, bass.ds(h + 2, 1), g * HALF:(g + 1) * HALF],
                                       self.bank[g][:].unsqueeze(1), ACT.Copy, scale=self.parc("gdn_norm")).then_inc(S["mx"], 1)
                    if not last:
                        silu(W1, 1)

                for m in range(2):
                    raw_out(waits(0), m)
                for m in range(2):
                    silu(waits(0), m)
                self.heads(act, body)

            @block.vector
            def _(dve):
                zd = Step(dve, Z["d"])
                dve.wait_ge(Z["ba"], 1)
                zd(dve.tensor_copy(ba[:].rearrange("p i h -> p (i h)"), self.bank[7][:, 0:64]))
                dt = ab[:, 4:8].unsqueeze(2).to_broadcast([P, GH, NG])
                zd(dve.tensor_tensor(sm[:, 0, :, :], ba[:, :, 4:8].rearrange("p i h -> p h i"), dt, ALU.add))
                zd(dve.tensor_scalar(sm[:, 1, :, :], sm[:, 0, :, :], -1.0, None, ALU.mult))
                zd(dve.tensor_tensor(sm[:, 1, :, :], sm[:, 0, :, :], sm[:, 1, :, :], ALU.max))
                dve.wait_ge(Z["a"], 4)
                zd(dve.tensor_scalar(sm[:, 0, :, :], sm[:, 0, :, :], 0.0, None, ALU.max))
                zd(dve.tensor_tensor(sm[:, 0, :, :], sm[:, 0, :, :], sm[:, 3, :, :], ALU.add))
                zd(dve.tensor_tensor(sm[:, 0, :, :], sm[:, 0, :, :], ev[:].unsqueeze(2).to_broadcast([P, GH, NG]), ALU.mult))
                zd(dve.tensor_scalar(scal[:, :, 7, :], sm[:, 0, :, :], -1.0, None, ALU.mult))
                dve.wait_ge(Z["pe"], 1)
                v4 = lambda a: a.rearrange("p (h i) -> p h i", h=GH)
                zd(dve.tensor_copy(scal[:, :, 0, :], v4(self.bank[0][:, 0:32])))
                zd(dve.tensor_copy(sm[:, 4, :, :], v4(self.bank[0][:, 32:64])))
                zd(dve.tensor_tensor(sm[:, 5, :, :], sm[:, 4, :, :], scal[:, :, 0, :], ALU.subtract))
                dve.wait_ge(Z["a"], 7)
                zd(dve.tensor_tensor(scal[:, :, 3, :], scal[:, :, 4, :], scal[:, :, 1, :], ALU.mult))
                zd(dve.tensor_scalar(scal[:, :, 5, :], scal[:, :, 4, :], -1.0, None, ALU.mult))
                zd(dve.memset(st[:, 0, :], 0.0))
                dve.memset(raw[:, :, 0:3], 0.0).then_inc(Z["pad"], 1)
                dve.wait_ge(Z["pad"], 1)
                tiles = dict(raw=raw, sq=sq, qn=qn, kn=kn, cv=cv, glb=glb, am=am, nn=nn, upd=upd, vb=vb, cvv=cvv, kd=kd, kbg=kbg,
                             wt=wt, st=st, vn=vn, u=u, e=e, ei=ei, es=es, osb=osb, osq=osq, og=og, zs=zs, scal=scal, hs=hs,
                             taps=taps, ssum=ssum)
                self.gdn_taps(dve, 0, waits(0), S, tiles)
                for m in range(2):
                    self.gdn_conv(dve, waits(0), S, tiles, m)
                self.heads(dve, lambda h, last: self.gdn_dve(dve, h, waits(h), waits(h + 1), last, S, tiles))

    def heads(self, eng, body):
        with eng.Fori(0, GH - 1) as h:
            body(h, False)
        body(GH - 1, True)

    def gdn_project(self, pe, S, wqkv, m, b0, n):
        kt, half = n // 2, n % 2
        ins = pe.matmul(self.bank[b0 + half][:], wqkv[:, m, kt, :], self.hT[:, kt, half * HALF:(half + 1) * HALF],
                        start=kt == 0, stop=kt == KT - 1)
        if n == 2 * KT - 1:
            ins.then_inc(S["proj"], 1)

    def gdn_taps(self, dve, h, W, S, t):
        dve.tensor_copy(t["taps"][:], self.par[:, bass.ds(h * 12 + PAR["gdn_conv"], 12)]).then_inc(S["taps"], 1)
        W(dve, "taps", 1)

    def gdn_conv(self, dve, W, S, t, m, steps=range(4)):
        dst, raw = (t["cv"][:, m, :] if m < 2 else t["cvv"][:, :]), t["raw"]
        for k in steps:
            tap = t["taps"][:, 4 * m + 3 - k:4 * m + 4 - k]
            if k == 0:
                W(dve, "raw", 2 * m + 2)
                ins = dve.tensor_scalar(dst, raw[:, m, 3:3 + T], tap, None, ALU.mult)
            else:
                W(dve, "conv", 4 * m + k)
                ins = dve.scalar_tensor_tensor(dst, raw[:, m, 3 - k:3 - k + T], tap, dst, ALU.mult, ALU.add)
            ins.then_inc(S["conv"], 1)

    def gdn_pe(self, pe, W, W1, last, S, t):
        bank = self.bank
        ident = self.con("ident")
        col = lambda q: slice(q * P, (q + 1) * P)
        W(pe, "raw", 4)
        W(pe, "hs", 2)
        for g in range(2):
            for q in range(4):
                ins = pe.matmul(bank[4 + g][:, col(q)], t["glb"][:, 4 * g + q, :], self.con("upper"), start=True, stop=True)
            ins.then_inc(S["gcr"], 1)
        for b in range(4):
            W(pe, "sq", b // 2 + 1)
            pe.matmul(bank[b][:], self.con("ones"), t["sq"][:, b // 2, b % 2 * HALF:(b % 2 + 1) * HALF],
                      start=True, stop=True).then_inc(S["ss"], 1)
        for n in range(KT, 2 * KT):
            self.gdn_project(pe, S, t["wqkv"], 2, 6, n)
        W(pe, "qn", 2)
        for g in range(2):
            for q in range(4):
                k = t["kn"][:, 4 * g + q, :]
                ins = pe.matmul(bank[2 + g][:, col(q)], k, k, start=True, stop=True)
            ins.then_inc(S["kk"], 1)
        def between(lv):
            if lv == 1:
                W(pe, "raw", 6)
                for g in range(2):
                    for q in range(4):
                        ins = pe.transpose(bank[6 + g][:, col(q)], t["kn"][:, 4 * g + q, :], ident)
                    ins.then_inc(S["trk"], 1)
            if lv == 2:
                for g in range(2):
                    W(pe, "kv", 2 * g + 2)
                    for q in range(4):
                        ins = pe.matmul(bank[6 + g][:, col(q)], t["qn"][:, 4 * g + q, :], t["kn"][:, 4 * g + q, :], start=True, stop=True)
                    ins.then_inc(S["qk"], 1)
            if lv == 3:
                W(pe, "am", 2)
                for g in range(2):
                    for q in range(4):
                        ins = pe.transpose(bank[6 + g][:, col(q)], t["am"][:, 4 * g + q, :], ident)
                    ins.then_inc(S["at"], 1)
            if lv == 6:
                W(pe, "ate", 2)
                W(pe, "sil", 3)
                for g in range(2):
                    for q in range(4):
                        ins = pe.transpose(bank[6 + g][:, col(q)], t["cvv"][:, (4 * g + q) * P:(4 * g + q + 1) * P], ident)
                    ins.then_inc(S["trv"], 1)

        W(pe, "gr", 8)
        self.invert_pe(pe, W, S, t["nn"], t["upd"], t["tur"], t["ye"], 6, True, between)
        for g in range(2):
            W(pe, "i_tur", 12 + g + 1)
            for q in range(4):
                ins = pe.matmul(bank[4 + g][:, col(q)], t["kbg"][:, 4 * g + q, :], t["tur"][:, 4 * g + q, :], start=True, stop=True)
            ins.then_inc(S["wt"], 1)
        W(pe, "kv", 6)
        for g in range(2):
            for q in range(4):
                ins = pe.matmul(bank[2 + g][:, col(q)], t["tur"][:, 4 * g + q, :], t["vb"][:, 4 * g + q, :], start=True, stop=True)
            ins.then_inc(S["u"], 1)
        W(pe, "ate", 2)
        W(pe, "wte", 2)
        if not last:
            W1(pe, "w0", 16)
        for i in range(NG):
            W(pe, "st", i + 1)
            pe.matmul(bank[6][:, 0:P], t["wt"][:, i, :], t["st"][:, i, :], start=True, stop=True).then_inc(S["ws"], 1)
            if not last:
                self.gdn_project(pe, S, t["wqkv"], 0, 4, 2 * i)
            W(pe, "vn", i + 1)
            pe.matmul(bank[7][:, 0:P], t["kd"][:, i, :], t["vn"][:, i, :], start=True, stop=True).then_inc(S["sk"], 1)
            if not last:
                self.gdn_project(pe, S, t["wqkv"], 0, 4, 2 * i + 1)
        for g in range(2):
            for q in range(4):
                ins = pe.matmul(bank[g][:, col(q)], t["qn"][:, 4 * g + q, :], t["st"][:, 4 * g + q, :], start=True, stop=True)
            ins.then_inc(S["qs"], 1)
            for q in range(4):
                ins = pe.matmul(bank[2 + g][:, col(q)], t["at"][:, 4 * g + q, :], t["vn"][:, 4 * g + q, :], start=True, stop=True)
            ins.then_inc(S["av"], 1)
        if not last:
            W(pe, "st", 9)
            W1(pe, "w1", 16)
            for n in range(2 * KT):
                self.gdn_project(pe, S, t["wqkv"], 1, 6, n)
        W(pe, "og", 2)
        for g in range(2):
            for q in range(4):
                ins = pe.transpose(bank[g][:, col(q)], t["og"][:, 4 * g + q, :], ident)
            ins.then_inc(S["ot"], 1)
        if not last:
            W1(pe, "raw", 4)
            W1(pe, "w2", 16)
            for n in range(KT):
                self.gdn_project(pe, S, t["wqkv"], 2, 6, n)
        W(pe, "mx", 2)

    def gdn_dve(self, dve, h, W, W1, last, S, t):
        bank = self.bank
        four = lambda b: bank[b][:].rearrange("p (a b) -> p a b", a=4)
        grp = lambda a, g: a[:, 4 * g:4 * g + 4, :]
        hs, cv, raw = t["hs"], t["cv"], t["raw"]
        wide = lambda kind, g: hs[:, kind, 4 * g:4 * g + 4].unsqueeze(2).to_broadcast([P, 4, P])
        dve.tensor_copy(hs[:].rearrange("p a b -> p (a b)"), t["scal"][:, bass.ds(h, 1), :, :].rearrange("p o a b -> p (o a b)")).then_inc(S["hs"], 1)
        W(dve, "hs", 1)
        dve.tensor_copy(t["glb"], hs[:, 7, :].unsqueeze(2).to_broadcast([P, NG, P])).then_inc(S["hs"], 1)
        for i in range(NG):
            W(dve, "gcr", i // 4 + 1)
            dve.tensor_scalar(t["e"][:, i, :], bank[4 + i // 4][:, i % 4 * P:(i % 4 + 1) * P], hs[:, 0, i:i + 1], 0.0,
                              ALU.subtract, ALU.max).then_inc(S["gr"], 1)
        flat8 = lambda a: a.rearrange("p a b -> p (a b)")
        for m, dst, scale in ((0, t["qn"], float(P) ** -0.5), (1, t["kn"], 1.0)):
            W(dve, "rs", m + 1)
            dve.scalar_tensor_tensor(flat8(dst), cv[:, m, :], scale, t["sq"][:, m, :], ALU.mult, ALU.mult).then_inc(S["qn"], 1)
        W(dve, "qn", 2)
        dve.tensor_copy(t["upd"], self.con("ident").unsqueeze(1).to_broadcast([P, NG, P])).then_inc(S["i_init"], 1)
        for i in range(NG):
            W(dve, "kk", i // 4 + 1)
            W(dve, "gm", 2 * (i // 4) + 1)
            dve.scalar_tensor_tensor(t["nn"][:, i, :], bank[2 + i // 4][:, i % 4 * P:(i % 4 + 1) * P], hs[:, 5, i:i + 1],
                                     t["es"][:, i, :], ALU.mult, ALU.mult).then_inc(S["nn"], 1)
        W(dve, "i_init", 1)
        m0 = self.con("lev_low")[:, 0:P].bitcast(U32).unsqueeze(1).to_broadcast([P, 4, P])
        for g in range(2):
            W(dve, "nn", 4 * g + 4)
            self.pass_gate(dve)
            dve.copy_predicated(grp(t["upd"], g), m0, grp(t["nn"], g)).then_inc(S["i_upd"], 1)
        W(dve, "i_upd", 2)

        def between(lv):
            if lv == 0:
                for g in range(2):
                    W(dve, "trk", g + 1)
                    dve.tensor_tensor(grp(t["kd"], g), four(6 + g), wide(2, g), ALU.mult).then_inc(S["kv"], 1)
                    dve.tensor_tensor(grp(t["kbg"], g), four(6 + g), wide(3, g), ALU.mult).then_inc(S["kv"], 1)
            if 1 <= lv <= 4:
                self.gdn_conv(dve, W, S, t, 2, [lv - 1])
            if lv == 1:
                for g in range(2):
                    W(dve, "qk", g + 1)
                    W(dve, "gm", 2 * g + 2)
                    dve.tensor_tensor(grp(t["am"], g), four(6 + g), grp(t["ei"], g), ALU.mult).then_inc(S["am"], 1)

        self.invert_dve(dve, W, S, t["upd"], "lev_low", 6, between)
        for g in range(2):
            W(dve, "trv", g + 1)
            dve.tensor_tensor(grp(t["vb"], g), four(6 + g), wide(4, g), ALU.mult).then_inc(S["kv"], 1)
        for g in range(2):
            W(dve, "wt", g + 1)
            dve.tensor_copy(t["wt"][:, 4 * g:4 * g + 4, :].rearrange("p a b -> p (a b)"), bank[4 + g][:]).then_inc(S["wte"], 1)
        dve.memset(t["st"][:, 0, :], 0.0).then_inc(S["st"], 1)
        W(dve, "ue", 2)
        for i in range(NG):
            W(dve, "ws", i + 1)
            dve.tensor_tensor(t["vn"][:, i, :], t["u"][:, i, :], bank[6][:, 0:P], ALU.subtract).then_inc(S["vn"], 1)
            W(dve, "st", i + 1)
            W(dve, "sk", i + 1)
            dve.scalar_tensor_tensor(t["st"][:, i + 1, :], t["st"][:, i, :], hs[:, 6, i:i + 1], bank[7][:, 0:P],
                                     ALU.mult, ALU.add).then_inc(S["st"], 1)
        for g in range(2):
            W(dve, "qs", g + 1)
            dve.tensor_tensor(grp(t["osb"], g), four(g), wide(1, g), ALU.mult).then_inc(S["t1"], 1)
            W(dve, "t1", g + 1)
            W(dve, "av", g + 1)
            dve.tensor_tensor(grp(t["osb"], g), grp(t["osb"], g), four(2 + g), ALU.add).then_inc(S["o"], 1)
        W(dve, "o", 2)
        dve.tensor_tensor(t["osq"], t["osb"], t["osb"], ALU.mult).then_inc(S["osq"], 1)
        W(dve, "osq", 1)
        dve.tensor_reduce(t["ssum"][:, 0, :], t["osq"], AX, ALU.add).then_inc(S["osq"], 1)
        W(dve, "osq", 2)
        dve.tensor_scalar(t["ssum"][:, 1, :], t["ssum"][:, 0, :], 1.0 / P, EPS, ALU.mult, ALU.add).then_inc(S["osq"], 1)
        if not last:
            self.gdn_taps(dve, h + 1, W1, S, t)
            self.gdn_conv(dve, W1, S, t, 0)
        W(dve, "ol", 2)
        dve.tensor_tensor(t["og"], t["osb"], t["ssum"][:, 2, :].unsqueeze(2).to_broadcast([P, NG, P]), ALU.mult).then_inc(S["og"], 1)
        W(dve, "og", 1)
        zh = t["zs"][:, bass.ds(h, 1), :, :].rearrange("p o i v -> p (o i) v")
        dve.tensor_tensor(t["og"], t["og"], zh, ALU.mult).then_inc(S["og"], 1)
        if not last:
            self.gdn_conv(dve, W1, S, t, 1)
        W(dve, "mx", 2)

    def rwkv_stage(self):
        nc = self.nc
        K = dict(lnx=1, proj=3, raw=3, lo=3, sg=3, pp=1, car=2, xs=5, sq=1, ss=1, ln=1, rs=1, cs=1, ex=2, px=4, kp=5, rk=1, bs=1,
                 bon=1, bd=14, tr=6, tok=4, tokv=2, sc=8, am=8, i_init=1, i_turn=10, i_tur=10, i_y=10, i_ye=10, i_w=10, i_upd=12,
                 m0=1, c1=8, rh=8, c2=8, u=8, c3=8, st=8, ot=2, o=2, m1=1, oc=1, osq=1, m2=1, vl=1, vr=1, y=2, mx=1)
        with ExitStack() as c:
            f = lambda n, shape: self.sb(c, "rwkv_" + n, [P] + shape)
            used = [0]

            def g(*shape):
                n = int(np.prod(shape))
                a = self.arena[:, used[0]:used[0] + n]
                used[0] += n
                if len(shape) == 1:
                    return a
                names = "abc"[:len(shape)]
                return a.rearrange("p (%s) -> p %s" % (" ".join(names), " ".join(names)), **dict(zip(names, shape)))

            H = HALF
            NCH = H // CR
            w, lw, lot = f("w", [3, KT, P]), f("lora_w", [3, P]), f("lo", [T])
            raw, xs, pp, car = f("raw", [3, 1 + H]), g(3, H), f("par", [10]), f("carry", [3])
            sg, a, gs, rs, cs, ex, te = (g(H) for _ in range(7))
            pt, pin, pm, pe_ = (g(H) for _ in range(4))
            kk, k2, b, bon = (g(H) for _ in range(4))
            rm = f("reset", [H])
            kr = f("kap_r", [NCH, 2, P])
            ki, ni, vb, kh, nh = (g(NCH, P) for _ in range(5))
            vt, kht, nht = (g(NCH, P) for _ in range(3))
            ak, an = g(NCH, 2, P), g(NCH, 2, P)
            upd, tur, ye, us = f("upd", [NCH, P]), kh, nh, vb
            wlo = upd
            lraw = kr[:].rearrange("p a b c -> p (a b c)")[:, 0:1 + T]
            rhs = f("rhs", [2, P])
            lnx = f("lnx", [2])
            st = f("state", [NCH + 1, P])
            o, oc, osq = sg, ex, te
            S = {n: self.sem(c, "rwkv_" + n) for n in K}
            Z = {n: self.sem(c, "rwkvz_" + n) for n in ("w", "wl", "lz", "init", "lp", "lr", "ld", "lt")}
            block = c.enter_context(nc.Block())
            win = self.i["w_in"].rearrange("(kt p) c -> p kt c", p=P)
            bank = self.bank
            col = lambda q: slice(q * P, (q + 1) * P)

            def waits(n):
                return lambda e, name, k: e.wait_ge(S[name], n * K[name] + k)

            def loops(eng, body):
                with eng.Fori(0, 3) as n:
                    body(n, n >> 1, n & 1, waits(n), waits(n + 1), False)
                body(3, 1, 1, waits(3), waits(4), True)

            lru_sync, lru_pool, lru_pe, lru_act, lru_dve = self.lru_parts(c)

            @block.sync
            def _(sp):
                lru_sync(sp)
                sp.dma_start(wlo[:], win[:, :, 3 * DA:3 * DA + P]).then_inc(Z["wl"], 16)
                sp.wait_ge(Z["lz"], 1)
                with sp.Fori(0, 2) as p:
                    for m in range(3):
                        sp.dma_start(w[:, m, :, :], win[:, :, bass.ds(p * P + m * DA, P)]).then_inc(Z["w"], 16)
                    for m, (name, r0, r1) in enumerate((("rwkv_w2", 0, 32), ("rwkv_a2", 32, 64), ("rwkv_g2", 64, 128))):
                        sp.dma_start(lw[r0:r1, m, :], self.i[name][:, bass.ds(p * P, P)]).then_inc(Z["w"], 16)
                    sp.wait_ge(S["proj"], p * 6 + 6)
                    self.pass_gate(sp)

            @block.gpsimd
            def _(pool):
                lru_pool(pool)
                pool.memset(lw[:], 0.0).then_inc(Z["lz"], 1)
                pool.memset(lraw[:, 0:1], 0.0).then_inc(Z["init"], 1)
                pool.memset(rm[:], 1.0).then_inc(Z["init"], 1)
                pool.wait_ge(Z["init"], 2)
                pool.memset(rm[:].rearrange("p (c t) -> p c t", t=CR)[:, :, 0:1], 0.0).then_inc(Z["init"], 1)
                pool.memset(car[:], 0.0).then_inc(Z["init"], 1)
                pool.memset(st[:, NCH, :], 0.0).then_inc(Z["init"], 1)

            @block.tensor
            def _(pe):
                lru_pe(pe)
                pe.wait_ge(self.lru_sig, 8)
                pe.wait_ge(Z["wl"], 16)
                for kt in range(KT):
                    for half in range(2):
                        ins = pe.matmul(bank[6 + half][:], wlo[:, kt, :], self.hT[:, kt, half * H:(half + 1) * H],
                                        start=kt == 0, stop=kt == KT - 1)
                ins.then_inc(Z["lp"], 1)

                def project(n, k):
                    m, kt = k // KT, k % KT
                    ins = pe.matmul(bank[3 + m][:], w[:, m, kt, :], self.hT[:, kt, bass.ds((n & 1) * H, H)], start=kt == 0, stop=kt == KT - 1)
                    if kt == KT - 1:
                        ins.then_inc(S["proj"], 1)

                def turn(k, src, W):
                    W(pe, "bd", 2 * k + 2)
                    for g in range(2):
                        for q in range(4):
                            ins = pe.transpose(bank[2 * k + g][:, col(q)], src[:, 4 * g + q, :], self.con("ident"))
                        ins.then_inc(S["tr"], 1)

                def low_rank(n):
                    for m in range(3):
                        pe.matmul(bank[m][:], lw[:, m, :], lot[:, bass.ds((n & 1) * H, H)], start=True, stop=True).then_inc(S["lo"], 1)

                pe.wait_ge(Z["w"], 96)
                for k in range(3 * KT):
                    project(0, k)
                pe.wait_ge(Z["lt"], 2)
                low_rank(0)

                def body(n, p, hf, W, W1, last):
                    W(pe, "sq", 1)
                    pe.matmul(bank[6][:], self.con("ones64"), rs, start=True, stop=True).then_inc(S["ss"], 1)
                    W(pe, "sg", 3)
                    turn(0, vb, W)
                    W(pe, "rk", 1)
                    pe.matmul(bank[7][:], self.con("ones64"), b, start=True, stop=True).then_inc(S["bs"], 1)
                    W(pe, "raw", 3)
                    turn(1, kh, W)
                    turn(2, nh, W)
                    W(pe, "bon", 1)
                    W(pe, "ln", 1)
                    for s, src in enumerate((ki, ni)):
                        W(pe, "bd", 2 * s + 12)
                        for g in range(4):
                            bk = (6, 7, 0, 1, 2, 3, 4, 5)[4 * s + g]
                            if bk < 6:
                                W(pe, "tokv", bk + 1) if bk < 2 else W(pe, "tok", bk - 1)
                            for q in range(2):
                                i = 2 * g + q
                                ins = pe.matmul(bank[bk][:, q * 256:(q + 1) * 256], src[:, i, :],
                                                kr[:, i, :, :].rearrange("p a b -> p (a b)"), start=True, stop=True)
                            ins.then_inc(S["sc"], 1)
                    W(pe, "am", 8)
                    self.invert_pe(pe, W, S, an[:, :, 0, :], upd, tur, ye, 5, False)
                    W(pe, "i_upd", 12)
                    W(pe, "m0", 1)
                    if not last:
                        pe.wait_ge(Z["w"], ((n + 1) >> 1) * 96 + 96)
                    for i in range(NCH):
                        if i:
                            W(pe, "st", i)
                        pe.matmul(bank[6][:, 0:P], ak[:, i, 0, :], vt[:, i, :], start=True, stop=False)
                        pe.matmul(bank[6][:, 0:P], kr[:, i, 0, :], st[:, i, :], start=False, stop=True).then_inc(S["c1"], 1)
                        if not last:
                            project(n + 1, 2 * i)
                        W(pe, "rh", i + 1)
                        pe.matmul(bank[7][:, 0:P], upd[:, i, :], rhs[:, i % 2, :], start=True, stop=True).then_inc(S["c2"], 1)
                        pe.matmul(bank[0][:, 0:P], kht[:, i, :], vt[:, i, :], start=True, stop=False)
                        W(pe, "u", i + 1)
                        pe.matmul(bank[0][:, 0:P], nht[:, i, :], us[:, i, :], start=False, stop=True).then_inc(S["c3"], 1)
                        if not last:
                            project(n + 1, 2 * i + 1)
                    for g in range(2):
                        for q in range(4):
                            i = 4 * g + q
                            pe.matmul(bank[1 + g][:, col(q)], st[:, i, :], kr[:, i, 1, :], start=True, stop=False)
                            pe.matmul(bank[1 + g][:, col(q)], vt[:, i, :], ak[:, i, 1, :], start=False, stop=False)
                            ins = pe.matmul(bank[1 + g][:, col(q)], us[:, i, :], an[:, i, 1, :], start=False, stop=True)
                        ins.then_inc(S["ot"], 1)
                    W(pe, "o", 2)
                    pe.matmul(bank[6][:], self.con("ones64"), o, start=True, stop=True).then_inc(S["m1"], 1)
                    if not last:
                        W(pe, "st", 8)
                        low_rank(n + 1)
                    W(pe, "osq", 1)
                    pe.matmul(bank[7][:], self.con("ones64"), osq, start=True, stop=True).then_inc(S["m2"], 1)
                    if not last:
                        for k in range(2 * KT, 3 * KT):
                            project(n + 1, k)
                    W(pe, "mx", 1)

                loops(pe, body)

            @block.scalar
            def _(act):
                lru_act(act)
                act.wait_ge(self.lru_out, 1)
                act.wait_ge(Z["lp"], 1)
                for half in range(2):
                    act.activation(lraw[:, 1 + half * H:1 + (half + 1) * H], bank[6 + half][:], ACT.Copy).then_inc(Z["lr"], 1)
                act.wait_ge(Z["ld"], 2)
                act.activation(lot[0:32, :], lot[0:32, :], ACT.Tanh).then_inc(Z["lt"], 1)
                act.activation(lot[64:128, :], lot[64:128, :], ACT.Sigmoid).then_inc(Z["lt"], 1)

                def raw_out(W, m):
                    W(act, "proj", m + 1)
                    act.activation(raw[:, m, 1:1 + H], bank[3 + m][:], ACT.Copy).then_inc(S["raw"], 1)

                def key_squares(W):
                    W(act, "xs", 3)
                    act.activation(rs, xs[:, 1, :], ACT.Square, scale=pp[:, 5:6]).then_inc(S["sq"], 1)

                for m in range(3):
                    raw_out(waits(0), m)
                key_squares(waits(0))

                def body(n, p, hf, W, W1, last):
                    W(act, "pp", 1)
                    for m, dst in enumerate((sg, a)):
                        W(act, "lo", m + 1)
                        act.activation(dst[:], bank[m][:], ACT.Sigmoid, bias=pp[:, 3 + m:4 + m]).then_inc(S["sg"], 1)
                    W(act, "lo", 3)
                    act.activation(gs, bank[2][:], ACT.Copy).then_inc(S["sg"], 1)
                    W(act, "ss", 1)
                    act.activation(rs, bank[6][:], ACT.Ln, bias=EPS).then_inc(S["ln"], 1)
                    W(act, "ln", 1)
                    act.activation(rs, rs, ACT.Exp, scale=-0.5).then_inc(S["rs"], 1)
                    W(act, "ex", 2)
                    act.activation(pt, cs, ACT.Exp, scale=-EM05).then_inc(S["px"], 1)
                    act.activation(pin, cs, ACT.Exp, scale=EM05).then_inc(S["px"], 1)
                    act.activation(pm, ex, ACT.Exp, scale=-EM05).then_inc(S["px"], 1)
                    act.activation(pe_, te, ACT.Exp, scale=-EM05).then_inc(S["px"], 1)
                    for s, dst in ((1, kht), (2, nht)):
                        for g in range(2):
                            W(act, "tr", 2 * s + g + 1)
                            act.activation(dst[:, 4 * g:4 * g + 4, :].rearrange("p a b -> p (a b)"), bank[2 * s + g][:],
                                           ACT.Copy).then_inc(S["tok"], 1)
                    self.invert_act(act, W, S, tur, ye, 5, False)
                    for i in range(NCH):
                        W(act, "c1", i + 1)
                        act.activation(rhs[:, i % 2, :], bank[6][:, 0:P], ACT.Copy).then_inc(S["rh"], 1)
                        W(act, "c2", i + 1)
                        act.activation(us[:, i, :], bank[7][:, 0:P], ACT.Copy).then_inc(S["u"], 1)
                    if not last:
                        for m in range(2):
                            raw_out(W1, m)
                    W(act, "m2", 1)
                    act.activation(cs, bank[7][:], ACT.Ln, scale=1.0 / CR, bias=GN_EPS).then_inc(S["vl"], 1)
                    W(act, "vl", 1)
                    act.activation(cs, cs, ACT.Exp, scale=-0.5).then_inc(S["vr"], 1)
                    if not last:
                        key_squares(W1)
                        raw_out(W1, 2)
                    W(act, "mx", 1)

                loops(act, body)

            @block.vector
            def _(dve):
                lru_dve(dve)
                dve.wait_ge(Z["init"], 5)
                dve.wait_ge(Z["lr"], 2)
                dve.tensor_tensor(lot[:], lraw[:, 0:T], lraw[:, 1:1 + T], ALU.subtract).then_inc(Z["ld"], 1)
                dve.wait_ge(Z["ld"], 1)
                dve.scalar_tensor_tensor(lot[:], lot[:], self.parc("mu_lo"), lraw[:, 1:1 + T], ALU.mult, ALU.add).then_inc(Z["ld"], 1)
                dve.wait_ge(Z["lt"], 2)

                ch = lambda x: x.rearrange("p (c t) -> p c t", t=CR)

                def shift(n, W):
                    dve.tensor_copy(pp[:], self.par[:, bass.ds((n >> 1) * 10 + PAR["rwkv"], 10)]).then_inc(S["pp"], 1)
                    dve.tensor_tensor(raw[:, :, 0], car[:], keep(n).to_broadcast([P, 3]), ALU.mult).then_inc(S["car"], 1)
                    W(dve, "raw", 2)
                    W(dve, "car", 1)
                    W(dve, "pp", 1)
                    dve.tensor_tensor(xs[:, 0:2, :], raw[:, 0:2, 0:H], raw[:, 0:2, 1:1 + H], ALU.subtract).then_inc(S["xs"], 1)
                    W(dve, "xs", 1)
                    for m in range(2):
                        mix(m)

                def shift_v(W):
                    W(dve, "raw", 3)
                    dve.tensor_tensor(xs[:, 2, :], raw[:, 2, 0:H], raw[:, 2, 1:1 + H], ALU.subtract).then_inc(S["xs"], 1)
                    dve.tensor_copy(car[:], raw[:, :, H]).then_inc(S["car"], 1)
                    W(dve, "xs", 4)
                    mix(2)

                def mix(m):
                    dve.scalar_tensor_tensor(xs[:, m, :], xs[:, m, :], pp[:, m:m + 1], raw[:, m, 1:1 + H],
                                             ALU.mult, ALU.add).then_inc(S["xs"], 1)

                def keep(n):
                    return self.cons[:, bass.ds((n & 1) + CON["keep"][0], 1)]

                shift(0, waits(0))

                def body(n, p, hf, W, W1, last):
                    dve.tensor_copy(lnx[:], pp[:, 8:10]).then_inc(S["lnx"], 1)
                    dve.tensor_tensor(st[:, 0, :], st[:, NCH, :], keep(n).to_broadcast([P, P]), ALU.mult).then_inc(S["m0"], 1)
                    shift_v(W)
                    W(dve, "xs", 5)
                    for g in range(2):
                        dve.tensor_scalar(vb[:, :, g * CR:(g + 1) * CR], ch(xs[:, 2, :]), self.con("half")[:, g:g + 1], None,
                                          ALU.mult).then_inc(S["bd"], 1)
                    W(dve, "sg", 2)
                    dve.tensor_tensor_scan(cs, rm[:], sg, 0.0, ALU.mult, ALU.add).then_inc(S["cs"], 1)
                    dve.tensor_scalar(k2, a, -1.0, pp[:, 6:7], ALU.add, ALU.mult).then_inc(S["kp"], 1)
                    dve.tensor_scalar(kk, xs[:, 1, :], pp[:, 5:6], None, ALU.mult).then_inc(S["kp"], 1)
                    W(dve, "cs", 1)
                    dve.tensor_tensor(ex, cs, sg, ALU.subtract).then_inc(S["ex"], 1)
                    c3 = cs.rearrange("p (c t) -> p c t", t=CR)
                    dve.tensor_tensor(te.rearrange("p (c t) -> p c t", t=CR), c3[:, :, CR - 1:CR].to_broadcast([P, NCH, CR]),
                                      c3, ALU.subtract).then_inc(S["ex"], 1)
                    W(dve, "kp", 2)
                    dve.scalar_tensor_tensor(k2, k2, 1.0, xs[:, 1, :], ALU.add, ALU.mult).then_inc(S["kp"], 1)
                    W(dve, "kp", 3)
                    dve.scalar_tensor_tensor(b, xs[:, 0, :], pp[:, 7:8], k2, ALU.mult, ALU.mult).then_inc(S["rk"], 1)
                    W(dve, "rs", 1)
                    dve.tensor_tensor(kk, kk, rs, ALU.mult).then_inc(S["kp"], 1)
                    W(dve, "bs", 1)
                    dve.tensor_tensor(bon, bank[7][:], xs[:, 2, :], ALU.mult).then_inc(S["bon"], 1)
                    W(dve, "kp", 4)
                    dve.tensor_tensor(b, kk, a, ALU.mult).then_inc(S["kp"], 1)
                    W(dve, "kp", 5)
                    W(dve, "px", 4)
                    plus, minus = self.con("half"), self.con("nhalf")
                    for dst, src, sign, dec in ((kh, k2, plus, pe_), (nh, b, minus, pe_), (kr[:, :, 0, :], kk, plus, pm),
                                                (kr[:, :, 1, :], xs[:, 0, :], plus, pt), (ki, k2, plus, pin), (ni, b, minus, pin)):
                        for g in range(2):
                            dve.scalar_tensor_tensor(dst[:, :, g * CR:(g + 1) * CR], ch(src), sign[:, g:g + 1], ch(dec[:]),
                                                     ALU.mult, ALU.mult).then_inc(S["bd"], 1)
                    dve.tensor_copy(upd[:], self.con("ident").unsqueeze(1).to_broadcast([P, NCH, P])).then_inc(S["i_init"], 1)
                    for g in range(2):
                        W(dve, "tr", g + 1)
                        dve.tensor_copy(vt[:, 4 * g:4 * g + 4, :].rearrange("p a b -> p (a b)"), bank[g][:]).then_inc(S["tokv"], 1)
                    a0 = CON["up64_strict"][0]
                    mask = self.cons[:, a0:a0 + 2 * P].unsqueeze(1).to_broadcast([P, 2, 2 * P])
                    for s, dst in enumerate((ak, an)):
                        for g in range(4):
                            bk = (6, 7, 0, 1, 2, 3, 4, 5)[4 * s + g]
                            W(dve, "sc", 4 * s + g + 1)
                            dve.tensor_tensor(dst[:, 2 * g:2 * g + 2, :, :].rearrange("p a b c -> p a (b c)"),
                                              bank[bk][:].rearrange("p (a b) -> p a b", a=2), mask, ALU.mult).then_inc(S["am"], 1)
                    W(dve, "am", 8)
                    W(dve, "i_init", 1)
                    m0 = self.con("lev_up")[:, 0:P].bitcast(U32).unsqueeze(1).to_broadcast([P, 4, P])
                    for g in range(2):
                        self.pass_gate(dve)
                        dve.copy_predicated(upd[:, 4 * g:4 * g + 4, :], m0, an[:, 4 * g:4 * g + 4, 0, :]).then_inc(S["i_upd"], 1)
                    W(dve, "i_upd", 2)
                    self.invert_dve(dve, W, S, upd, "lev_up", 5)
                    for i in range(NCH):
                        W(dve, "c3", i + 1)
                        W(dve, "st", i) if i else W(dve, "m0", 1)
                        dve.scalar_tensor_tensor(st[:, i + 1, :], st[:, i, :], pt[:, i * CR + CR - 1:i * CR + CR], bank[0][:, 0:P],
                                                 ALU.mult, ALU.add).then_inc(S["st"], 1)
                    for g in range(2):
                        W(dve, "ot", g + 1)
                        dve.tensor_reduce(o[:, g * 256:(g + 1) * 256].rearrange("p (c t) -> p c t", t=CR),
                                          bank[1 + g][:].rearrange("p (c g t) -> p c t g", g=2, t=CR), AX, ALU.add).then_inc(S["o"], 1)
                    W(dve, "m1", 1)
                    dve.scalar_tensor_tensor(oc, bank[6][:], -1.0 / CR, o, ALU.mult, ALU.add).then_inc(S["oc"], 1)
                    W(dve, "oc", 1)
                    dve.tensor_tensor(osq, oc, oc, ALU.mult).then_inc(S["osq"], 1)
                    W(dve, "lnx", 1)
                    if not last:
                        shift(n + 1, W1)
                    W(dve, "vr", 1)
                    dve.scalar_tensor_tensor(oc, oc, lnx[:, 0:1], cs, ALU.mult, ALU.mult).then_inc(S["y"], 1)
                    W(dve, "y", 1)
                    dve.scalar_tensor_tensor(oc, oc, lnx[:, 1:2], bon, ALU.add, ALU.add).then_inc(S["y"], 1)
                    W(dve, "y", 2)
                    dve.tensor_tensor(self.mixT[:, bass.ds(p, 1), bass.ds(hf * H, H)], oc.unsqueeze(1), gs.unsqueeze(1),
                                      ALU.mult).then_inc(S["mx"], 1)

                loops(dve, body)

    def route_stage(self):
        nc = self.nc
        with ExitStack() as c:
            f = lambda n, shape, dt=F32: self.sb(c, "rt_" + n, [P] + shape, dt)
            wo = f("w_out", [KT, D])
            x2 = self.x2
            h2 = f("h2", [2, D])
            h2t = f("h2t", [2, KT, P])
            sq = f("sq", [D])
            gain = f("gain", [D])
            wr = f("w_router", [KT, 36])
            mb = f("bias", [36])
            ss, rs = f("ss", [NT]), f("rs", [NT])
            lg = f("logits", [NT, 36])
            S = {n: self.sem(c, "rt_" + n) for n in (
                "x", "small", "prod", "x2", "ss", "ms", "rc", "rt", "h2", "turn", "turned", "log", "lg",
                "step", "ex", "cum", "oh", "slot", "gd", "vd")}
            ST = [self.sem(c, f"rt_stored{j}") for j in range(2)]
            sm = f("small", [24, NT])
            g4 = f("g4", [4, NT, 4])
            me = f("masked", [NT, 4, 8])
            el = f("el", [NT, 8])
            top = f("top", [NT, 8])
            topi = f("topi", [NT, 8], U32)
            eid = f("eid", [NT, 2])
            oh = f("onehot", [NT, 2, E])
            ohs = f("onehots", [NT, E])
            run = f("run", [NT + 1, E])
            rank = f("rank", [NT, E])
            tmp = sq[:, 4 * P:4 * P + NT * 2 * E].rearrange("p (i k e) -> p i k e", k=2, e=E)
            ov = f("ov", [8, E])
            cmp7 = f("cmp7", [E, 7])
            cmpb = f("cmpb", [NOV, E])
            dst = f("dst", [NT * 2])
            dsti = f("dsti", [NT * 2], U32)
            blki = f("blki", [NT * 2], U32)
            sloti = f("sloti", [NT * 2], U32)
            blkf, slotf, val = f("blkf", [NT * 2]), f("slotf", [NT * 2]), f("val", [NT * 2])
            rr = sq[:, 0:4 * P].rearrange("p (n s) -> p n s", n=4)
            bt = f("blk_onehot", [4, NBLK])
            vs = f("vs", [2, NBLK])
            bef = f("bef", [NOV + 1])
            WO = [self.sem(c, f"rt_w{kt}") for kt in range(KT)]
            block = c.enter_context(nc.Block())
            bank = self.bank
            xv = self.i["x"].rearrange("(i p) d -> p i d", p=P)

            @block.sync
            def _(sp):
                wv = self.i["w_out"].rearrange("(kt p) n -> p kt n", p=P)
                for kt in range(KT):
                    sp.dma_start(wo[:, kt, :], wv[:, kt, :]).then_inc(WO[kt], 16)
                for q in range(2):
                    sp.dma_start(x2[:, 4 * q:4 * q + 4, :], xv[:, 4 * q:4 * q + 4, :]).then_inc(S["x"], 16)
                sp.dma_start(gain[:], self.i["norm_ffn_row"].partition_broadcast(P)).then_inc(S["small"], 16)
                sp.dma_start(mb[:], self.i["moe_b"].partition_broadcast(P)).then_inc(S["small"], 16)
                sp.dma_start(wr[:, :, 0:4], self.i["moe_w_group"].rearrange("(kt p) n -> p kt n", p=P)).then_inc(S["small"], 16)
                sp.dma_start(wr[:, :, 4:36], self.i["moe_w_expert"].rearrange("(kt p) n -> p kt n", p=P)).then_inc(S["small"], 16)
                for j in range(NEARLY):
                    self.load_expert(sp, j, (self.gu_early[:, j], self.dn_early[:, j]), self.w_landed[j])
                for i in range(NT):
                    sp.wait_ge(S["h2"], i + 1)
                    sp.dma_start(self.h2d[i * P:(i + 1) * P, :], h2[:, i % 2, :]).then_inc(ST[i % 2], 16)
                for j in range(2):
                    sp.wait_ge(ST[j], 16 * (NT // 2))

            @block.gpsimd
            def _(pool):
                pool.memset(self.xg_early[:], 0.0)

            @block.tensor
            def _(pe):
                def turn(i):
                    pe.wait_ge(S["h2"], i + 1)
                    if i:
                        pe.wait_ge(S["turned"], 2 * i)
                    for kt in range(KT):
                        ins = pe.transpose(bank[4 + kt // 4][:, kt % 4 * P:(kt % 4 + 1) * P], h2[:, i % 2, kt * P:(kt + 1) * P],
                                           self.con("ident"))
                        if kt % 4 == 3:
                            ins.then_inc(S["turn"], 1)

                def logits(i):
                    pe.wait_ge(S["small"], 64)
                    pe.wait_ge(S["turned"], 2 * i + 2)
                    if i >= 2:
                        pe.wait_ge(S["lg"], i - 1)
                    for kt in range(KT):
                        ins = pe.matmul(bank[6 + i % 2][:, 0:36], h2t[:, i % 2, kt, :], wr[:, kt, :], start=kt == 0, stop=kt == KT - 1)
                    ins.then_inc(S["log"], 1)

                for i in range(NT + 3):
                    if i < NT:
                        for kt in range(KT):
                            if i == 0:
                                pe.wait_ge(WO[kt], 16)
                            for half in range(2):
                                if kt == 0 and i >= 2:
                                    pe.wait_ge(S["x2"], 2 * (i - 2) + half + 1)
                                ins = pe.matmul(bank[2 * (i % 2) + half][:], self.mixT[:, kt, i * P:(i + 1) * P],
                                                wo[:, kt, half * HALF:(half + 1) * HALF], start=kt == 0, stop=kt == KT - 1)
                        ins.then_inc(S["prod"], 1)
                    if 2 <= i < NT + 2:
                        turn(i - 2)
                    if i >= 3:
                        logits(i - 3)
                pe.wait_ge(S["oh"], 1)
                o = ohs[:].rearrange("p i e -> p (i e)")
                pe.matmul(bank[0][:, 0:NT * E], self.con("below"), o, start=True, stop=True)
                pe.matmul(bank[1][:, 0:NT * E], self.con("ones"), o, start=True, stop=True).then_inc(S["cum"], 1)
                for n in range(2 * NT):
                    pe.wait_ge(S["slot"], 2 * n + 2)
                    pe.matmul(bank[2][:, 0:NBLK], rr[:, n % 4, :], bt[:, n % 4, :], start=n == 0, stop=n == 2 * NT - 1).then_inc(S["cum"], 1)

            @block.scalar
            def _(act):
                for i in range(NT + 1):
                    if i < NT:
                        act.wait_ge(S["x2"], 2 * i + 2)
                        if i:
                            act.wait_ge(S["ss"], i)
                        act.activation(sq[:], x2[:, i, :], ACT.Square, accum_out=ss[:, i:i + 1]).then_inc(S["ss"], 1)
                        act.wait_ge(S["rc"], i + 1)
                        act.activation(rs[:, i:i + 1], rs[:, i:i + 1], ACT.Sqrt).then_inc(S["rt"], 1)
                    if i >= 1:
                        for b in range(2):
                            act.wait_ge(S["turn"], 2 * (i - 1) + b + 1)
                            if i >= 3:
                                act.wait_ge(S["log"], i - 2)
                            act.activation(h2t[:, (i - 1) % 2, 4 * b:4 * b + 4, :].rearrange("p a b -> p (a b)"), bank[4 + b][:],
                                           ACT.Copy).then_inc(S["turned"], 1)
                act.wait_ge(S["gd"], 1)
                act.activation(g4[:, 3, :, :], g4[:, 3, :, :], ACT.Exp).then_inc(S["ex"], 1)
                act.wait_ge(S["vd"], 1)
                act.activation(sm[:, 6, :], sm[:, 5, :], ACT.Exp).then_inc(S["ex"], 1)

            @block.vector
            def _(dve):
                dve.wait_ge(S["x"], 32)
                dve.wait_ge(S["small"], 64)

                def logits_out(i):
                    dve.wait_ge(S["log"], i + 1)
                    dve.tensor_tensor(lg[:, i, :], bank[6 + i % 2][:, 0:36], mb[:], ALU.add).then_inc(S["lg"], 1)

                for i in range(NT):
                    dve.wait_ge(S["prod"], i + 1)
                    for half in range(2):
                        xs = x2[:, i, half * HALF:(half + 1) * HALF]
                        dve.tensor_tensor(xs, bank[2 * (i % 2) + half][:], xs, ALU.add).then_inc(S["x2"], 1)
                    dve.wait_ge(S["ss"], i + 1)
                    dve.tensor_scalar(rs[:, i:i + 1], ss[:, i:i + 1], 1.0 / D, EPS, ALU.mult, ALU.add).then_inc(S["ms"], 1)
                    dve.wait_ge(S["ms"], i + 1)
                    dve.reciprocal(rs[:, i:i + 1], rs[:, i:i + 1]).then_inc(S["rc"], 1)
                    dve.wait_ge(S["rt"], i + 1)
                    if i >= 2:
                        dve.wait_ge(S["turn"], 2 * (i - 2) + 2)
                        dve.wait_ge(ST[i % 2], 16 * (i // 2))
                    dve.scalar_tensor_tensor(h2[:, i % 2, :], x2[:, i, :], rs[:, i:i + 1], gain[:], ALU.mult, ALU.mult).then_inc(S["h2"], 1)
                    if i >= 3:
                        logits_out(i - 3)
                for i in range(NT - 3, NT):
                    logits_out(i)
                dve.wait_ge(S["lg"], NT)
                step = Step(dve, S["step"])
                b4 = lambda a: a.unsqueeze(2).to_broadcast([P, NT, 4])
                grp = lg[:, :, 0:4]
                step(dve.tensor_reduce(sm[:, 0, :], grp, AX, ALU.max))
                dve.tensor_tensor(g4[:, 3, :, :], grp, b4(sm[:, 0, :]), ALU.subtract).then_inc(S["gd"], 1)
                step(dve.tensor_tensor(g4[:, 0, :, :], grp, b4(sm[:, 0, :]), ALU.is_equal))
                step(dve.tensor_tensor(g4[:, 1, :, :], g4[:, 0, :, :], self.con("idx4").unsqueeze(1).to_broadcast([P, NT, 4]), ALU.mult))
                step(dve.tensor_reduce(sm[:, 1, :], g4[:, 1, :, :], AX, ALU.max))
                step(dve.tensor_tensor(g4[:, 2, :, :], g4[:, 1, :, :], b4(sm[:, 1, :]), ALU.is_equal))
                step(dve.tensor_scalar(sm[:, 2, :], sm[:, 1, :], -8.0, 32.0, ALU.mult, ALU.add))
                step(dve.tensor_tensor(me[:], lg[:, :, 4:36].rearrange("p i (g e) -> p i g e", g=4),
                                       g4[:, 2, :, :].unsqueeze(3).to_broadcast([P, NT, 4, 8]), ALU.mult))
                step(dve.tensor_reduce(el[:], me[:].rearrange("p i g e -> p i e g"), AX, ALU.add))
                for i in range(NT):
                    step.inc(dve.max(top[:, i, :], el[:, i, :]))
                step.wait()
                dve.tensor_tensor(sm[:, 5, :], top[:, :, 1], top[:, :, 0], ALU.subtract).then_inc(S["vd"], 1)
                for i in range(NT):
                    step.inc(dve.max_index(topi[:, i, :], top[:, i, :], el[:, i, :]))
                step.wait()
                step(dve.tensor_copy(eid[:], topi[:, :, 0:2]))
                step(dve.tensor_tensor(eid[:], eid[:], sm[:, 2, :].unsqueeze(2).to_broadcast([P, NT, 2]), ALU.add))
                step(dve.tensor_tensor(oh[:].rearrange("p i k e -> p (i k) e"), self.con("iota_e").unsqueeze(1).to_broadcast([P, 2 * NT, E]),
                                       eid[:].rearrange("p i k -> p (i k)").unsqueeze(2).to_broadcast([P, 2 * NT, E]), ALU.is_equal))
                dve.tensor_tensor(ohs[:], oh[:, :, 0, :], oh[:, :, 1, :], ALU.add).then_inc(S["oh"], 1)
                dve.wait_ge(S["ex"], 2)
                step(dve.tensor_reduce(sm[:, 7, :], g4[:, 3, :, :], AX, ALU.add))
                step(dve.tensor_scalar(sm[:, 8, :], sm[:, 6, :], 1.0, None, ALU.add))
                step(dve.tensor_tensor(sm[:, 8, :], sm[:, 8, :], sm[:, 7, :], ALU.mult))
                step(dve.reciprocal(self.gates12[:, 0, :], sm[:, 8, :]))
                step(dve.tensor_tensor(self.gates12[:, 1, :], self.gates12[:, 0, :], sm[:, 6, :], ALU.mult))
                dve.wait_ge(S["cum"], 1)
                step(dve.memset(run[:, 0, :], 0.0))
                for i in range(NT):
                    step(dve.tensor_tensor(run[:, i + 1, :], run[:, i, :], bank[1][:, i * E:(i + 1) * E], ALU.add))
                step(dve.tensor_tensor(rank[:], run[:, 0:NT, :], bank[0][:, 0:NT * E].rearrange("p (i e) -> p i e", e=E), ALU.add))
                cnt = run[:, NT, :]
                step(dve.tensor_tensor(cmp7[:], cnt.unsqueeze(2).to_broadcast([P, E, 7]), self.con("j128").unsqueeze(1).to_broadcast([P, E, 7]),
                                       ALU.is_gt))
                step(dve.tensor_reduce(ov[:, 0, :], cmp7[:], AX, ALU.add))
                step(dve.tensor_tensor_scan(ov[:, 1, :], self.con("ones")[:, 0:E], ov[:, 0, :], 0.0, ALU.mult, ALU.add))
                step(dve.tensor_tensor(ov[:, 2, :], ov[:, 1, :], ov[:, 0, :], ALU.subtract))
                step(dve.tensor_scalar(ov[:, 3, :], ov[:, 2, :], float(P), float(P * (E - 1)), ALU.mult, ALU.add))
                step(dve.tensor_tensor(ov[:, 3, :], ov[:, 3, :], self.con("iota_e128"), ALU.subtract))
                step(dve.tensor_scalar(tmp[:, :, 0, :], rank[:], float(P), None, ALU.is_ge))
                step(dve.tensor_tensor(tmp[:, :, 0, :], tmp[:, :, 0, :], ov[:, 3, :].unsqueeze(1).to_broadcast([P, NT, E]), ALU.mult))
                step(dve.tensor_tensor(rank[:], rank[:], tmp[:, :, 0, :], ALU.add))
                step(dve.tensor_tensor(rank[:], rank[:], self.con("iota_e128").unsqueeze(1).to_broadcast([P, NT, E]), ALU.add))
                step(dve.tensor_tensor(tmp[:], oh[:], rank[:].unsqueeze(2).to_broadcast([P, NT, 2, E]), ALU.mult))
                step(dve.tensor_reduce(dst[:], tmp[:].rearrange("p i k e -> p (i k) e"), AX, ALU.add))
                step(dve.tensor_copy(dsti[:], dst[:]))
                step(dve.tensor_scalar(blki[:], dsti[:], 7, None, ALU.logical_shift_right))
                step(dve.tensor_scalar(sloti[:], dsti[:], P - 1, None, ALU.bitwise_and))
                step(dve.tensor_copy(blkf[:], blki[:]))
                step(dve.tensor_copy(slotf[:], sloti[:]))
                for k in range(2):
                    step(dve.tensor_scalar(val[:].rearrange("p (i k) -> p i k", k=2)[:, :, k], self.con("iota_tok"), 2.0, 1.0 + k, ALU.mult, ALU.add))
                for n in range(2 * NT):
                    if n >= 4:
                        dve.wait_ge(S["cum"], n - 2)
                    dve.tensor_scalar(rr[:, n % 4, :], self.con("iota128"), slotf[:, n:n + 1], None, ALU.is_equal).then_inc(S["slot"], 1)
                    dve.tensor_scalar(bt[:, n % 4, :], self.con("iota_blk"), blkf[:, n:n + 1], val[:, n:n + 1], ALU.is_equal,
                                      ALU.mult).then_inc(S["slot"], 1)
                step(dve.tensor_tensor(cmpb[:], ov[:, 1, :].unsqueeze(1).to_broadcast([P, NOV, E]),
                                       self.con("iota_blk")[:, 0:NOV].unsqueeze(2).to_broadcast([P, NOV, E]), ALU.is_le))
                step(dve.tensor_reduce(bef[:, 0:NOV], cmpb[:], AX, ALU.add))
                step(dve.tensor_scalar(bef[:, 0:NOV], bef[:, 0:NOV], float(E - 1), None, ALU.min))
                step(dve.tensor_copy(bef[:, NOV:NOV + 1], ov[:, 1, E - 1:E]))
                step(dve.tensor_copy(self.extra[:], bef[:]))
                dve.wait_ge(S["cum"], 1 + 2 * NT)
                step(dve.tensor_scalar(vs[:, 0, :], bank[2][:, 0:NBLK], 0.0, 8192.0, ALU.is_equal, ALU.mult))
                step(dve.scalar_tensor_tensor(vs[:, 1, :], bank[2][:, 0:NBLK], -1.0, vs[:, 0, :], ALU.add, ALU.add))
                step(dve.tensor_copy(self.slot_to[:], vs[:, 1, :]))
                step(dve.tensor_scalar(self.slot_from[:], self.slot_to[:], 1, None, ALU.logical_shift_right))

    def load_expert(self, eng, e, w, sem):
        for name, dst in (("moe_w_gate", w[0][:, :, 0:DE]), ("moe_w_up", w[0][:, :, DE:2 * DE]), ("moe_w_down", w[1])):
            eng.dma_start(dst, self.i[name][bass.ds(e, 1), :, :].rearrange("o (p kt) n -> p (o kt) n", p=P)).then_inc(sem, 16)

    def expert_stage(self):
        nc = self.nc
        with ExitStack() as c:
            f = lambda n, shape, dt=F32: self.sb(c, "ex_" + n, [P] + shape, dt)
            gu_late = self.mixT[:].rearrange("p (j a) (b n) -> p j (a b) n", j=NR - NEARLY, n=2 * DE)
            dn_late = f("w_down", [NR - NEARLY, 2, D])
            W = [(self.gu_early[:, j], self.dn_early[:, j]) for j in range(NEARLY)]
            W += [(gu_late[:, j], dn_late[:, j]) for j in range(NR - NEARLY)]
            xg_late = f("x", [2, D])
            xg = [self.xg_early[:, j, :] for j in range(2)] + [xg_late[:, j, :] for j in range(2)]
            xt = f("xt", [2, KT, P])
            si, hid, ht, yo = f("silu", [DE]), f("hid", [DE]), f("hid_t", [2, P]), f("y", [2, D])
            ifrom, ito = f("from", [NR], U32), f("to", [2], U32)
            names = ("turn", "ta", "tv", "gu", "si", "hid", "ht", "htc", "dn", "ya", "yv", "ix", "init")
            S = {n: self.sem(c, "ex_" + n) for n in names}
            WL = self.w_landed
            GA = [self.sem(c, f"ex_gathered{j}") for j in range(NR)]
            SC = [self.sem(c, f"ex_scattered{j}") for j in range(2)]
            V = {n: self.sem(c, "ov_" + n) for n in names + ("w", "ga", "sc")}
            block = c.enter_context(nc.Block())
            bank = self.bank
            later = lambda e, n: not (isinstance(e, int) and e < n)
            exists = lambda e: not (isinstance(e, int) and e >= E)

            def gather(pool, b, sem):
                pool.indirect_dma_start(xg[b], None, self.h2d, bass.IndirectOffsetOnAxis(ap=ifrom[:, b:b + 1], axis=0),
                                        bounds_check=T - 1, oob_is_err=False).then_inc(sem, 16)

            def scatter(pool, b, sem):
                pool.indirect_dma_start(self.yd, bass.IndirectOffsetOnAxis(ap=ito[:, b:b + 1], axis=0), yo[:, b, :], None,
                                        bounds_check=2 * T - 1, oob_is_err=False).then_inc(sem, 16)

            def turns(eng, body):
                body(0)
                with eng.Fori(1, E // NR - 1) as it:
                    body(it)
                body(E // NR - 1)

            def further(eng, body):
                n = eng.value_load(self.extra[0:1, NOV:NOV + 1], min_val=0, max_val=NOV)
                with eng.If(n > 0):
                    with eng.Fori(0, NOV) as b:
                        body(b)

            @block.sync
            def _(sp):
                for j in range(2):
                    sp.wait_ge(GA[j], 16)
                for j in range(NEARLY, NR):
                    self.load_expert(sp, j, W[j], WL[j])
                with sp.Fori(1, E // NR) as it:
                    for j in range(NR):
                        sp.wait_ge(S["dn"], (it - 1) * (2 * NR) + 2 * j + 2)
                        self.load_expert(sp, it * NR + j, W[j], WL[j])

                def body(b):
                    e = sp.value_load(self.extra[0:1, bass.ds(b, 1)], min_val=0, max_val=E - 1)
                    self.load_expert(sp, e, W[0], V["w"])
                    sp.wait_ge(V["dn"], b * 2 + 2)
                    self.pass_gate(sp)

                sp.wait_ge(S["dn"], 2 * E)
                further(sp, body)

            @block.gpsimd
            def _(pool):
                def fetch(e, j, n):
                    pool.tensor_copy(ifrom[:, j:j + 1], self.slot_from[:, bass.ds(e, 1)]).then_inc(S["ix"], 1)
                    pool.wait_ge(S["ix"], n)
                    self.pass_gate(pool)
                    gather(pool, j, GA[j])

                for j in range(NR):
                    if j == 2:
                        pool.memset(xg_late[:], 0.0).then_inc(S["init"], 1)
                        pool.wait_ge(S["init"], 1)
                    fetch(j, j, j + 1)

                def body(it):
                    last = isinstance(it, int) and it == E // NR - 1
                    for j in range(NR):
                        e, b = it * NR + j, j % 2
                        n = NR + 2 * e + 1
                        if last:
                            n = NR + 2 * NR * it + j
                        else:
                            pool.wait_ge(S["turn"], (e + 1) * 2)
                            pool.wait_ge(GA[j], 16 * (it + 1))
                            fetch(e + NR, j, n)
                        if later(e, 2):
                            pool.wait_ge(SC[b], 16 * (it * 2 + j // 2))
                            self.pass_gate(pool)
                        pool.tensor_copy(ito[:, b:b + 1], self.slot_to[:, bass.ds(e, 1)]).then_inc(S["ix"], 1)
                        pool.wait_ge(S["ix"], n + 1)
                        self.pass_gate(pool)
                        pool.wait_ge(S["ya"], e + 1)
                        pool.wait_ge(S["yv"], e + 1)
                        self.pass_gate(pool)
                        scatter(pool, b, SC[b])

                turns(pool, body)
                for b in range(2):
                    pool.wait_ge(SC[b], 16 * (E // 2))

                def over(b):
                    pool.tensor_copy(ifrom[:, 0:1], self.slot_from[:, bass.ds(b + E, 1)]).then_inc(V["ix"], 1)
                    pool.tensor_copy(ito[:, 0:1], self.slot_to[:, bass.ds(b + E, 1)]).then_inc(V["ix"], 1)
                    pool.wait_ge(V["ix"], 2 * b + 2)
                    self.pass_gate(pool)
                    gather(pool, 0, V["ga"])
                    pool.wait_ge(V["ya"], b + 1)
                    pool.wait_ge(V["yv"], b + 1)
                    self.pass_gate(pool)
                    scatter(pool, 0, V["sc"])
                    pool.wait_ge(V["sc"], 16 * b + 16)
                    pool.wait_ge(V["ga"], 16 * b + 16)
                    self.pass_gate(pool)

                pool.wait_ge(S["turn"], 2 * E)
                further(pool, over)

            def pe_turn(pe, b, sem):
                for kt in range(KT):
                    ins = pe.transpose(bank[4 + kt // 4][:, kt % 4 * P:(kt % 4 + 1) * P], xg[b].rearrange("t (p kt) -> t kt p", kt=KT)[:, kt, :], self.con("ident"))
                    if kt % 4 == 3:
                        ins.then_inc(sem, 1)

            def pe_up(pe, b, w, gb, sem):
                for kt in range(KT):
                    ins = pe.matmul(bank[gb][:], xt[:, b, kt, :], W[w][0][:, kt, :], start=kt == 0, stop=kt == KT - 1)
                ins.then_inc(sem, 1)

            def pe_hid(pe, sem):
                for q in range(2):
                    ins = pe.transpose(bank[6][:, q * P:(q + 1) * P], hid[:].rearrange("t (p q) -> t q p", q=2)[:, q, :], self.con("ident"))
                ins.then_inc(sem, 1)

            def pe_down(pe, w, sem):
                for half in range(2):
                    for q in range(2):
                        ins = pe.matmul(bank[2 + half][:], ht[:, q, :], W[w][1][:, q, half * HALF:(half + 1) * HALF], start=q == 0, stop=q == 1)
                    ins.then_inc(sem, 1)

            @block.tensor
            def _(pe):
                pe.wait_ge(GA[0], 16)
                pe_turn(pe, 0, S["turn"])
                pe.wait_ge(WL[0], 48)
                pe.wait_ge(S["ta"], 1)
                pe.wait_ge(S["tv"], 1)
                pe_up(pe, 0, 0, 0, S["gu"])
                pe.wait_ge(GA[1], 16)
                pe_turn(pe, 1, S["turn"])

                def body(it):
                    for j in range(NR):
                        e = it * NR + j
                        if exists(e + 1):
                            pe.wait_ge(WL[(j + 1) % NR], 48 * (it + 1 + (j + 1) // NR))
                            pe.wait_ge(S["ta"], e + 2)
                            pe.wait_ge(S["tv"], e + 2)
                            pe_up(pe, (j + 1) % 2, (j + 1) % NR, (j + 1) % 2, S["gu"])
                        pe.wait_ge(S["hid"], e + 1)
                        pe_hid(pe, S["ht"])
                        if exists(e + 2):
                            pe.wait_ge(GA[(j + 2) % NR], 16 * (it + 1 + (j + 2) // NR))
                            pe_turn(pe, (j + 2) % NR, S["turn"])
                        pe.wait_ge(S["htc"], e + 1)
                        if later(e, 1):
                            pe.wait_ge(S["ya"], e)
                            pe.wait_ge(S["yv"], e)
                        pe_down(pe, j, S["dn"])

                turns(pe, body)
                pe.wait_ge(S["ya"], E)
                pe.wait_ge(S["yv"], E)

                def over(b):
                    pe.wait_ge(V["ga"], 16 * b + 16)
                    pe_turn(pe, 0, V["turn"])
                    pe.wait_ge(V["w"], 48 * b + 48)
                    pe.wait_ge(V["ta"], b + 1)
                    pe.wait_ge(V["tv"], b + 1)
                    pe_up(pe, 0, 0, 0, V["gu"])
                    pe.wait_ge(V["hid"], b + 1)
                    pe_hid(pe, V["ht"])
                    pe.wait_ge(V["htc"], b + 1)
                    pe_down(pe, 0, V["dn"])
                    pe.wait_ge(V["ya"], b + 1)
                    pe.wait_ge(V["yv"], b + 1)
                    self.pass_gate(pe)

                further(pe, over)

            def act_turned(act, b, q, n, SS):
                act.wait_ge(SS["turn"], n)
                act.activation(xt[:, b, 0:4, :].rearrange("p a b -> p (a b)"), bank[4][:], ACT.Copy).then_inc(SS["ta"], 1)

            @block.scalar
            def _(act):
                for e in range(2):
                    act_turned(act, e, 0, 2 * e + 1, S)

                def body(it):
                    for j in range(NR):
                        e = it * NR + j
                        act.wait_ge(S["gu"], e + 1)
                        act.activation(si[:], bank[j % 2][:, 0:DE], ACT.Silu).then_inc(S["si"], 1)
                        if exists(e + 2):
                            act_turned(act, j % 2, 0, 2 * e + 5, S)
                        act.wait_ge(S["dn"], 2 * e + 1)
                        if later(e, 2):
                            act.wait_ge(SC[j % 2], 16 * (it * 2 + j // 2))
                        act.activation(yo[:, j % 2, 0:HALF], bank[2][:], ACT.Copy).then_inc(S["ya"], 1)

                turns(act, body)

                def over(b):
                    act_turned(act, 0, 0, 2 * b + 1, V)
                    act.wait_ge(V["gu"], b + 1)
                    act.activation(si[:], bank[0][:, 0:DE], ACT.Silu).then_inc(V["si"], 1)
                    act.wait_ge(V["dn"], 2 * b + 1)
                    act.activation(yo[:, 0, 0:HALF], bank[2][:], ACT.Copy).then_inc(V["ya"], 1)

                act.wait_ge(SC[0], 16 * (E // 2))
                further(act, over)

            def dve_turned(dve, b, n, SS):
                dve.wait_ge(SS["turn"], n)
                dve.tensor_copy(xt[:, b, 4:8, :].rearrange("p a b -> p (a b)"), bank[5][:]).then_inc(SS["tv"], 1)

            def dve_hid(dve, gb, n, SS):
                dve.wait_ge(SS["si"], n)
                dve.tensor_tensor(hid[:], si[:], bank[gb][:, DE:2 * DE], ALU.mult).then_inc(SS["hid"], 1)

            @block.vector
            def _(dve):
                for e in range(2):
                    dve_turned(dve, e, 2 * e + 2, S)

                def body(it):
                    for j in range(NR):
                        e = it * NR + j
                        dve_hid(dve, j % 2, e + 1, S)
                        dve.wait_ge(S["ht"], e + 1)
                        dve.tensor_copy(ht[:].rearrange("p a b -> p (a b)"), bank[6][:, 0:2 * P]).then_inc(S["htc"], 1)
                        if exists(e + 2):
                            dve_turned(dve, j % 2, 2 * e + 6, S)
                        dve.wait_ge(S["dn"], 2 * e + 2)
                        if later(e, 2):
                            dve.wait_ge(SC[j % 2], 16 * (it * 2 + j // 2))
                        dve.tensor_copy(yo[:, j % 2, HALF:D], bank[3][:]).then_inc(S["yv"], 1)

                turns(dve, body)

                def over(b):
                    dve_turned(dve, 0, 2 * b + 2, V)
                    dve_hid(dve, 0, b + 1, V)
                    dve.wait_ge(V["ht"], b + 1)
                    dve.tensor_copy(ht[:].rearrange("p a b -> p (a b)"), bank[6][:, 0:2 * P]).then_inc(V["htc"], 1)
                    dve.wait_ge(V["dn"], 2 * b + 2)
                    dve.tensor_copy(yo[:, 0, HALF:D], bank[3][:]).then_inc(V["yv"], 1)

                dve.wait_ge(SC[0], 16 * (E // 2))
                further(dve, over)

    def final_stage(self):
        nc = self.nc
        with ExitStack() as c:
            y = self.sb(c, "fin_y", [P, NT, 2, D])
            gain = self.sb(c, "fin_gain", [P, D])
            sq = self.sb(c, "fin_sq", [P, D])
            ss = self.sb(c, "fin_ss", [P, NT])
            x2 = self.x2
            S = {n: self.sem(c, "fin_" + n) for n in ("g", "a", "b", "ss", "ms", "rc", "rt", "o", "out")}
            Y = [self.sem(c, f"fin_y{i}") for i in range(NT)]
            block = c.enter_context(nc.Block())
            yv = self.yd.rearrange("(i p k) d -> p i k d", p=P, k=2)

            @block.sync
            def _(sp):
                for i in range(NT):
                    sp.dma_start(y[:, i, :, :], yv[:, i, :, :]).then_inc(Y[i], 16)
                    if i == 0:
                        sp.dma_start(gain[:], self.i["norm_final"].partition_broadcast(P)).then_inc(S["g"], 16)
                for i in range(NT):
                    sp.wait_ge(S["o"], i + 1)
                    sp.dma_start(self.out[i * P:(i + 1) * P, :], x2[:, i, :]).then_inc(S["out"], 16)
                sp.wait_ge(S["out"], 16 * NT)

            @block.scalar
            def _(act):
                for i in range(NT):
                    act.wait_ge(S["b"], i + 1)
                    if i:
                        act.wait_ge(S["ss"], i)
                    act.activation(sq[:], x2[:, i, :], ACT.Square, accum_out=ss[:, i:i + 1]).then_inc(S["ss"], 1)
                    act.wait_ge(S["rc"], i + 1)
                    act.activation(ss[:, i:i + 1], ss[:, i:i + 1], ACT.Sqrt).then_inc(S["rt"], 1)

            @block.vector
            def _(dve):
                def first(i):
                    dve.wait_ge(Y[i], 16)
                    dve.scalar_tensor_tensor(x2[:, i, :], y[:, i, 0, :], self.gates12[:, 0, i:i + 1], x2[:, i, :], ALU.mult, ALU.add).then_inc(S["a"], 1)
                    dve.wait_ge(S["a"], i + 1)
                    dve.scalar_tensor_tensor(x2[:, i, :], y[:, i, 1, :], self.gates12[:, 1, i:i + 1], x2[:, i, :], ALU.mult, ALU.add).then_inc(S["b"], 1)

                first(0)
                dve.wait_ge(S["g"], 16)
                for i in range(NT):
                    dve.wait_ge(S["ss"], i + 1)
                    dve.tensor_scalar(ss[:, i:i + 1], ss[:, i:i + 1], 1.0 / D, EPS, ALU.mult, ALU.add).then_inc(S["ms"], 1)
                    dve.wait_ge(S["ms"], i + 1)
                    dve.reciprocal(ss[:, i:i + 1], ss[:, i:i + 1]).then_inc(S["rc"], 1)
                    if i + 1 < NT:
                        first(i + 1)
                    dve.wait_ge(S["rt"], i + 1)
                    dve.scalar_tensor_tensor(x2[:, i, :], x2[:, i, :], ss[:, i:i + 1], gain[:], ALU.mult, ALU.mult).then_inc(S["o"], 1)

    def build(self):
        nc = self.nc
        with self.ctx as c:
            self.bank = [c.enter_context(nc.psum_tensor(f"bank{n}", [P, HALF], F32)) for n in range(8)]
            self.gates = {e.engine: self.sem(c, f"gate_{n}") for n, e in (
                ("dve", nc.vector), ("sp", nc.sync), ("pe", nc.tensor), ("pool", nc.gpsimd))}
            self.cons = self.sb(c, "cons_sb", [P, NCON])
            self.par = self.sb(c, "par_cols", [P, P])
            self.hT = self.x2 = self.sb(c, "hT_or_x2", [P, KT, T])
            self.gates12 = self.sb(c, "gates12", [P, 2, NT])
            self.slot_from = self.sb(c, "slot_from", [P, NBLK], U32)
            self.slot_to = self.sb(c, "slot_to", [P, NBLK], U32)
            self.extra = self.sb(c, "extra_blocks", [P, NOV + 1], I32)
            self.h2d = nc.dram_tensor("h2_rows", (T, D), F32, kind="Internal").ap()
            self.yd = nc.dram_tensor("expert_rows", (2 * T, D), F32, kind="Internal").ap()
            flat = lambda t: t.rearrange("p a b -> p (a b)")
            self.mixT = self.sb(c, "mixT", [P, KT, T])
            self.w_lru_landed = self.sem(c, "lru_weights_landed")
            with ExitStack() as m:
                self.arena = self.sb(m, "arena", [P, RWKV_ARENA])
                self.w_lru = self.arena[:, 0:LRU_AT].rearrange("p (kt n) -> p kt n", kt=KT)
                self.run_stage(self.norm_stage)
                self.run_stage(self.rwkv_stage)
            self.run_stage(self.gdn_stage)
            self.w_landed = [self.sem(c, f"ex_weights{j}_landed") for j in range(NR)]
            with ExitStack() as m:
                self.gu_early = self.sb(m, "w_gate_up_early", [P, NEARLY, KT, 2 * DE])
                self.dn_early = self.sb(m, "w_down_early", [P, NEARLY, 2, D])
                self.xg_early = self.sb(m, "x_early", [P, 2, D])
                self.run_stage(self.route_stage)
                self.run_stage(self.expert_stage)
            self.run_stage(self.final_stage)


def build_program(nc, ins, out):
    Build(nc, ins, out).build()


def layout(inputs):
    f = {k: np.ascontiguousarray(v) for k, v in inputs.items()}
    rows = lambda a: a.reshape(-1, P)
    per = [f[n][0].reshape(2, P) for n in ("rwkv_w0", "rwkv_a0", "rwkv_k_k", "rwkv_k_a", "rwkv_r_k", "rwkv_lnx_w", "rwkv_lnx_b")]
    mu = f["rwkv_mu"][0].reshape(7, P)
    rwkv = np.stack([mu[0:2], mu[2:4], mu[4:6]] + per, 1).reshape(20, P)
    conv = f["gdn_conv_w"][0].reshape(4, 3, GH, P).transpose(2, 1, 0, 3).reshape(48, P)
    lru = f["lru_conv_w"][0].reshape(4, 2, P).transpose(1, 0, 2).reshape(8, P)
    par = np.concatenate([rows(f["norm_mix"]), rows(f["norm_ffn"]), mu[6:7], rwkv, conv, lru,
                          rows(f["lru_conv_b"]), rows(f["lru_b_a"]), rows(f["lru_b_x"]), rows(f["lru_lambda"]),
                          rows(f["gdn_norm_w"])], 0)
    return {
        "x": f["x"][0], "par_rows": np.ascontiguousarray(par), "cons": constants(),
        "w_in": f["w_in"][0], "w_out": f["w_out"][0],
        "rwkv_w2": f["rwkv_w2"][0], "rwkv_a2": f["rwkv_a2"][0], "rwkv_g2": f["rwkv_g2"][0],
        "gdn_ab": np.ascontiguousarray(np.concatenate([f["gdn_a_log"], f["gdn_dt_bias"]], 1)),
        "lru_w_a": f["lru_w_a"][0], "lru_w_x": f["lru_w_x"][0],
        "norm_ffn_row": f["norm_ffn"], "norm_final": f["norm_final"][None, :],
        "moe_b": np.ascontiguousarray(np.concatenate([f["moe_b_group"], f["moe_b_expert"]], 1)),
        "moe_w_group": f["moe_w_group"][0], "moe_w_expert": f["moe_w_expert"][0],
        "moe_w_gate": f["moe_w_gate"][0], "moe_w_up": f["moe_w_up"][0], "moe_w_down": f["moe_w_down"][0],
    }


def kernel(**inputs):
    from concourse import bacc, mybir as _mybir
    from concourse.bass_utils import run_bass_kernel_spmd as run

    arrays = layout(inputs)
    nc = bacc.Bacc("TRN2", target_bir_lowering=False, num_devices=1)
    ins = {k: nc.dram_tensor(k, a.shape, _mybir.dt.from_np(a.dtype), kind="ExternalInput").ap() for k, a in arrays.items()}
    out = nc.dram_tensor("out", (T, D), F32, kind="ExternalOutput").ap()
    build_program(nc, ins, out)
    r = run(nc, [arrays], core_ids=[0])
    return r.results[0]["out"].reshape(1, T, D)
```
